# Optimizing a Trainium2 kernel written in Bass

```python
import jax, jax.numpy as jnp
from jax import lax
import numpy as np

D_MODEL = 1024
BATCH = 1
SEQ = 128
DEPTH = 1
DEC_BATCH = 1
DEC_SEQ = 256
PAST_LEN = 128

GRID_W = 64
D_A = 1024
G_A = 8
CHUNK = 128
D_RNN = 1024
H_RNN = 8
BH_RNN = D_RNN // H_RNN
CONV_W = 4
RG_C = 8.0
N_EXPERTS = 16
EC_FACTOR = 2
D_FF = 2816
EPS = 1e-6
D_IN = 2 * D_A + 2 * D_RNN + 2 * D_MODEL

kernel_name = "hybrid_gmlp_rglru_ec_diffusion_step"

def rmsnorm(x, g):
    xf = x.astype(jnp.float32)
    xf = xf * lax.rsqrt(jnp.mean(xf * xf, axis=-1, keepdims=True) + EPS)
    return (xf * g.astype(jnp.float32)).astype(x.dtype)

def sincos_2d(n_tokens, dim, dtype):
    rows = n_tokens // GRID_W
    rr, cc = jnp.meshgrid(jnp.arange(rows, dtype=jnp.float32), jnp.arange(GRID_W, dtype=jnp.float32), indexing="ij")
    rr = rr.reshape(-1)[:, None]
    cc = cc.reshape(-1)[:, None]
    quarter = dim // 4
    omega = 1.0 / (10000.0 ** (jnp.arange(quarter, dtype=jnp.float32) / quarter))
    emb = jnp.concatenate([jnp.sin(rr * omega), jnp.cos(rr * omega), jnp.sin(cc * omega), jnp.cos(cc * omega)], axis=-1)
    return emb.astype(dtype)

def dwconv_centred(x, w, b):
    T = x.shape[1]
    xp = jnp.pad(x, ((0, 0), (2, 1), (0, 0)))
    out = b[None, None, :]
    for k in range(CONV_W):
        out = out + xp[:, k:k + T, :] * w[k][None, None, :]
    return out

def linear_scan(a, bterm, h0, reverse):
    if reverse:
        bterm = bterm.at[:, -1].add(a[:, -1] * h0)
    else:
        bterm = bterm.at[:, 0].add(a[:, 0] * h0)

    def combine(left, right):
        a_l, b_l = left
        a_r, b_r = right
        return a_l * a_r, a_r * b_l + b_r

    _, h = lax.associative_scan(combine, (a, bterm), axis=1, reverse=reverse)
    return h

def token_mix(h, h0_f, h0_b, p):
    B, T, _ = h.shape
    proj = h @ p["w_in"]
    u, v, xr, gr, gl = jnp.split(proj, [D_A, 2 * D_A, 2 * D_A + D_RNN, 2 * D_A + 2 * D_RNN], axis=-1)

    u = jax.nn.gelu(u)
    v = rmsnorm(jax.nn.gelu(v), p["v_norm_g"])
    n_chunks = T // CHUNK
    vc = v.reshape(B, n_chunks, CHUNK, G_A, D_A // G_A)
    s = jnp.einsum("gpq,bnqgc->bnpgc", p["w_spatial"], vc) + p["b_spatial"].T[None, None, :, :, None]
    y_a = u * s.reshape(B, T, D_A)

    xr = dwconv_centred(xr, p["conv_w"], p["conv_b"])
    xh = xr.reshape(B, T, H_RNN, BH_RNN)
    r = jax.nn.sigmoid((jnp.einsum("bthi,khij->kbthj", xh, p["rg_w_a"]).reshape(2, B, T, D_RNN)
                        + p["rg_b_a"][:, None, None, :]).astype(jnp.float32))
    gi = jax.nn.sigmoid((jnp.einsum("bthi,khij->kbthj", xh, p["rg_w_x"]).reshape(2, B, T, D_RNN)
                         + p["rg_b_x"][:, None, None, :]).astype(jnp.float32))
    log_a = -RG_C * jax.nn.softplus(-p["rg_lambda"].astype(jnp.float32))[:, None, None, :] * r
    a = jnp.exp(log_a)
    bterm = jnp.sqrt(jnp.maximum(1.0 - jnp.exp(2.0 * log_a), 0.0)) * gi * xr.astype(jnp.float32)[None]
    h_f = linear_scan(a[0], bterm[0], h0_f.astype(jnp.float32), False)
    h_b = linear_scan(a[1], bterm[1], h0_b.astype(jnp.float32), True)
    y_b = (h_f + h_b).astype(h.dtype) * jax.nn.gelu(gr)

    merged = (jax.nn.sigmoid(gl[..., :D_MODEL]) * (y_a @ p["w_br_a"])
              + jax.nn.sigmoid(gl[..., D_MODEL:]) * (y_b @ p["w_br_b"]))
    out = merged @ p["w_out"]
    return out, h_f[:, -1], h_b[:, 0]

def expert_choice_ffn(h, w_router, w_gate, w_up, w_down):
    B, T, D = h.shape
    cap = (EC_FACTOR * T) // N_EXPERTS
    logits = jnp.einsum("btd,de->bte", h, w_router).astype(jnp.float32)
    aff = jax.nn.softmax(logits, axis=-1)
    vals, idx = lax.top_k(jnp.swapaxes(aff, 1, 2), cap)
    xg = jax.vmap(lambda hb, ib: hb[ib])(h, idx)
    g = jnp.einsum("becd,edf->becf", xg, w_gate)
    up = jnp.einsum("becd,edf->becf", xg, w_up)
    o = jnp.einsum("becf,efd->becd", jax.nn.silu(g) * up, w_down) * vals[..., None].astype(h.dtype)
    y = jax.vmap(lambda ib, ob: jnp.zeros((T, D), ob.dtype).at[ib.reshape(-1)].add(ob.reshape(-1, D)))(idx, o)
    return y

def trunk_layer(x, mod, h0_f, h0_b, p):
    sh1, sc1, g1, sh2, sc2, g2 = [m[:, None, :] for m in jnp.split(mod, 6, axis=-1)]
    h = rmsnorm(x, p["norm1_g"]) * (1.0 + sc1) + sh1
    mix, hf, hb = token_mix(h, h0_f, h0_b, p)
    x = x + g1 * mix
    h = rmsnorm(x, p["norm2_g"]) * (1.0 + sc2) + sh2
    x = x + g2 * expert_choice_ffn(h, p["w_router"], p["w_gate_e"], p["w_up_e"], p["w_down_e"])
    return x, hf, hb

def setup_inputs(seed: int = 0) -> dict:
    key = jax.random.key(seed)
    ks = jax.random.split(key, 28)
    f32 = jnp.float32
    nrm = lambda k, shape, scale: jax.random.normal(k, shape, f32) * scale
    u_lam = jax.random.uniform(ks[20], (DEPTH, 2, D_RNN), f32, minval=0.9, maxval=0.999)
    s_lam = u_lam ** (1.0 / RG_C)
    return {
        "x_prompt": nrm(ks[0], (BATCH, SEQ, D_MODEL), 1.0),
        "x_sample": nrm(ks[1], (DEC_BATCH, DEC_SEQ, D_MODEL), 1.0),
        "state_rglru": nrm(ks[2], (DEC_BATCH, DEPTH, 2, D_RNN), 0.5),
        "c": nrm(ks[3], (DEC_BATCH, D_MODEL), 1.0),
        "c_ctx": nrm(ks[4], (D_MODEL,), 1.0),
        "w_ada": nrm(ks[5], (DEPTH, D_MODEL, 6 * D_MODEL), 0.5 * D_MODEL ** -0.5),
        "b_ada": nrm(ks[6], (DEPTH, 6 * D_MODEL), 0.02),
        "norm1_g": 1.0 + nrm(ks[7], (DEPTH, D_MODEL), 0.02),
        "norm2_g": 1.0 + nrm(ks[8], (DEPTH, D_MODEL), 0.02),
        "w_in": nrm(ks[9], (DEPTH, D_MODEL, D_IN), D_MODEL ** -0.5),
        "v_norm_g": 1.0 + nrm(ks[10], (DEPTH, D_A), 0.02),
        "w_spatial": nrm(ks[11], (DEPTH, G_A, CHUNK, CHUNK), CHUNK ** -0.5),
        "b_spatial": 1.0 + nrm(ks[12], (DEPTH, G_A, CHUNK), 0.02),
        "conv_w": nrm(ks[13], (DEPTH, CONV_W, D_RNN), CONV_W ** -0.5),
        "conv_b": nrm(ks[14], (DEPTH, D_RNN), 0.02),
        "rg_w_a": nrm(ks[15], (DEPTH, 2, H_RNN, BH_RNN, BH_RNN), BH_RNN ** -0.5),
        "rg_b_a": nrm(ks[16], (DEPTH, 2, D_RNN), 0.02),
        "rg_w_x": nrm(ks[17], (DEPTH, 2, H_RNN, BH_RNN, BH_RNN), BH_RNN ** -0.5),
        "rg_b_x": nrm(ks[18], (DEPTH, 2, D_RNN), 0.02),
        "rg_lambda": jnp.log(s_lam) - jnp.log1p(-s_lam),
        "w_br_a": nrm(ks[19], (DEPTH, D_A, D_MODEL), D_A ** -0.5),
        "w_br_b": nrm(ks[21], (DEPTH, D_RNN, D_MODEL), D_RNN ** -0.5),
        "w_out": nrm(ks[22], (DEPTH, D_MODEL, D_MODEL), D_MODEL ** -0.5),
        "w_router": nrm(ks[23], (DEPTH, D_MODEL, N_EXPERTS), D_MODEL ** -0.5),
        "w_gate_e": nrm(ks[24], (DEPTH, N_EXPERTS, D_MODEL, D_FF), D_MODEL ** -0.5),
        "w_up_e": nrm(ks[25], (DEPTH, N_EXPERTS, D_MODEL, D_FF), D_MODEL ** -0.5),
        "w_down_e": nrm(ks[26], (DEPTH, N_EXPERTS, D_FF, D_MODEL), D_FF ** -0.5),
        "final_norm_g": 1.0 + nrm(ks[27], (D_MODEL,), 0.02),
    }

def reference(x_prompt, x_sample, state_rglru, c, c_ctx, w_ada, b_ada, norm1_g, norm2_g, w_in, v_norm_g,
              w_spatial, b_spatial, conv_w, conv_b, rg_w_a, rg_b_a, rg_w_x, rg_b_x, rg_lambda,
              w_br_a, w_br_b, w_out, w_router, w_gate_e, w_up_e, w_down_e, final_norm_g):
    xp = x_prompt
    xs = x_sample + sincos_2d(x_sample.shape[1], D_MODEL, x_sample.dtype)[None]
    zero_state = jnp.zeros((x_prompt.shape[0], D_RNN), jnp.float32)
    new_states = []
    for l in range(DEPTH):
        p = {
            "norm1_g": norm1_g[l], "norm2_g": norm2_g[l], "w_in": w_in[l], "v_norm_g": v_norm_g[l],
            "w_spatial": w_spatial[l], "b_spatial": b_spatial[l], "conv_w": conv_w[l], "conv_b": conv_b[l],
            "rg_w_a": rg_w_a[l], "rg_b_a": rg_b_a[l], "rg_w_x": rg_w_x[l], "rg_b_x": rg_b_x[l],
            "rg_lambda": rg_lambda[l], "w_br_a": w_br_a[l], "w_br_b": w_br_b[l], "w_out": w_out[l],
            "w_router": w_router[l], "w_gate_e": w_gate_e[l], "w_up_e": w_up_e[l], "w_down_e": w_down_e[l],
        }
        mod_ctx = (jax.nn.silu(c_ctx)[None, :] @ w_ada[l] + b_ada[l][None, :])
        xp, hf, hb = trunk_layer(xp, mod_ctx, zero_state, zero_state, p)
        new_states.append(jnp.stack([hf, hb], axis=1).astype(x_prompt.dtype))
        mod_lat = jax.nn.silu(c) @ w_ada[l] + b_ada[l][None, :]
        xs, _, _ = trunk_layer(xs, mod_lat, state_rglru[:, l, 0], state_rglru[:, l, 1], p)
    y_prompt = rmsnorm(xp, final_norm_g)
    y_sample = rmsnorm(xs, final_norm_g)
    new_state_rglru = jnp.stack(new_states, axis=1)
    return (y_prompt, y_sample, new_state_rglru)


_drawn_inputs = setup_inputs


def setup_inputs(seed=0):
    import zlib

    import numpy as np

    out = dict(_drawn_inputs(seed))
    spreads = {}
    factors = {'norm1_g': 5.637,
     'norm2_g': 8.0,
     'v_norm_g': 8.0,
     'b_spatial': 8.0,
     'rg_b_a': 8.0,
     'rg_b_x': 7.317,
     'final_norm_g': 3.126}
    for name, (base, spread) in spreads.items():
        noise = np.random.default_rng([zlib.crc32(name.encode()), seed]).standard_normal(out[name].shape)
        drawn = base * np.exp(spread * noise) if base else spread * noise
        out[name] = __import__('jax').numpy.asarray(drawn.astype(out[name].dtype))
    for name, factor in factors.items():
        out[name] = (out[name] * factor).astype(out[name].dtype)
    return out
```

```python
from contextlib import ExitStack

import concourse.bass as bass
from concourse import mybir

D = 1024
P = 128
KT = D // P
TILES = 3
NCTX, NLAT = 128, 256
NTOK = NCTX + NLAT
GRID_W = 64
NE = 16
PAIRS = NE // 2
D_FF = 2816
UW = 512
FCH = [(f, min(UW, D_FF - f)) for f in range(0, D_FF, UW)]
NJ = len(FCH)
CAP_CTX, CAP_LAT = 2 * NCTX // NE, 2 * NLAT // NE
SL = 32
RG_C = 8.0
EPS = 1e-6
CONV_W = 4
SLOTS = 9
SLOT_F = KT * UW
PH_SLOT0, PH_SLOTS = 5, 4

COLS, _at = {}, 0
for _name, _n in (("c", 2 * KT), ("norm1_g", KT), ("norm2_g", KT), ("b_ada", 6 * KT), ("v_norm_g", KT),
                  ("conv_w", CONV_W * KT), ("conv_b", KT), ("rg_b_a", 2 * KT), ("rg_b_x", 2 * KT),
                  ("rg_lambda", 2 * KT), ("state", 2 * KT)):
    COLS[_name] = (_at, _n)
    _at += _n
NCOLS = _at

ADA_FIRST = [2, 3, 0, 1]
ADA_GATE1, ADA_SCALE2, ADA_SHIFT2, ADA_GATE2 = [4, 5], [8, 9], [6, 7], [10, 11]
ADA_ORDER = ADA_FIRST + ADA_GATE1 + ADA_SCALE2 + ADA_SHIFT2 + ADA_GATE2
def _units(kind, *us):
    return [(kind, u) for u in us]


PHASE_UNITS = (_units("ada", *ADA_FIRST) + _units("in", 4, 5, 6, 0, 7, 1, 2, 3, 8, 9) + _units("br_a", 0, 1)
               + _units("in", 10, 11) + _units("ada", *ADA_GATE1, *ADA_SCALE2) + _units("br_b", 0, 1)
               + _units("out", 0, 1) + _units("ada", *ADA_SHIFT2, *ADA_GATE2))
NPH = len(PHASE_UNITS)
UNIT_AT = {u: n for n, u in enumerate(PHASE_UNITS)}
ADA_AT = {u: n for n, u in enumerate(ADA_ORDER)}

WIDE_BANKS = 5
WIDE, _EVAC = {}, []


def _groups(name, n, engines):
    WIDE[name] = len(_EVAC)
    _EVAC.extend(engines[i % len(engines)] for i in range(n))


_groups("hT", KT, "va")
_groups("xr", KT, "a")
for _b in range(KT):
    _groups(f"gr{_b}", 1, "a")
    _groups(f"u{_b}", 1, "a")
    _groups(f"rg{_b}", 4, "a")
_groups("v", 2 * TILES, "a")
_groups("spatial", KT, "v")
_groups("glA", KT, "a")
_groups("br_a", KT, "v")
_groups("glB", KT, "a")
_groups("br_b", KT, "v")
_groups("out", 2 * TILES, "v")
_groups("h2T", KT, "va")


def emptied_by(engine, n):
    return sum(e == engine for e in _EVAC[:n])


PAIR_UNITS = []
for _p in range(2):
    for _j in range(NJ):
        PAIR_UNITS += [(_p, "gate", _j), (_p, "up", _j)]
        if _j >= 1:
            PAIR_UNITS.append((_p, "down", _j - 1))
    PAIR_UNITS.append((_p, "down", NJ - 1))
UPP = len(PAIR_UNITS)
assert UPP % SLOTS == 0
PAIR_AT = {u: n for n, u in enumerate(PAIR_UNITS)}
FREED = [PH_SLOT0 + n % PH_SLOTS for n in range(NPH - PH_SLOTS, NPH)]
SLOT_ORDER = [0, 3, 4, 1, 2, FREED[0], FREED[1], FREED[2], FREED[3]]
PH_LOADS = [sum(PH_SLOT0 + n % PH_SLOTS == s for n in range(NPH)) for s in range(SLOTS)]


def build(nc, x_prompt, x_sample, emb, cols, w_ada, b_ada, w_in, w_spatial_t, b_spatial, rg_w, w_br_a,
          w_br_b, w_out, w_router, w_gate, w_up, w_down, final_norm_g, y_prompt, y_sample, new_state):
    F32, I32 = mybir.dt.float32, mybir.dt.int32
    ALU, ACT, AX = mybir.AluOpType, mybir.ActivationFunctionType, mybir.AxisListType

    ctx = ExitStack()
    with ctx:
        def sb(name, shape, dt=F32):
            return ctx.enter_context(nc.sbuf_tensor(name, shape, dt))

        def sem(name):
            return ctx.enter_context(nc.semaphore(name))

        ring = sb("ring", [P, SLOTS * SLOT_F])
        x = sb("x", [P, TILES, D])
        xh = sb("xh", [P, TILES, D])
        work = sb("work", [P, 6656])
        col = sb("col", [P, NCOLS])
        ident = sb("ident", [P, P])
        c32 = sb("c32", [P, KT, 32])
        selb = sb("selb", [P, 2, P])
        selg = sb("selg", [P, P])
        two_ones = sb("two_ones", [1, 32])
        mod1 = sb("mod1", [P, 2, KT, 2])
        mod2 = sb("mod2", [P, 2, KT, 2])
        mod_raw = sb("mod_raw", [P, 4, 2])
        mod_sum = sb("mod_sum", [P, 4, 2])
        negsp = sb("negsp", [P, 2, KT])
        lam = sb("lam", [P, 4, 2 * KT])
        ss = sb("ss", [P, 4, 2 * TILES])
        rstd = sb("rstd", [P, 4, TILES])
        half = sb("half", [P, 1])
        tiny = sb("tiny", [P, 1])
        ns = sb("ns", [P, 2, KT])
        wr = sb("wr", [P, KT, NE])
        iota_i = sb("iota_i", [P, SL], I32)
        iota = sb("iota", [P, SL])
        posm = sb("posm", [P, TILES, NE + 1])
        aff = sb("aff", [P, TILES, NE])
        smax = sb("smax", [P, 3, TILES])

        def part(tensor, at, n):
            return tensor[:, at:at + n]

        def chan(at):
            return part(ring, at, KT * NTOK).rearrange("p (k t) -> p k t", k=KT)

        W1 = KT * NTOK
        hT, xr, glA, xc, uT, grT = (chan(n * W1) for n in range(6))
        glB = xc
        vtok = part(ring, 2 * W1, TILES * D).rearrange("p (t d) -> p t d", t=TILES)
        merged = glA
        embt = part(ring, 2 * W1, 2 * D).rearrange("p (t d) -> p t d", t=2)
        g1b = part(ring, SLOT_F, 2 * D).rearrange("p (m d) -> p m d", m=2)
        b_gate1 = ring[0:1, 4 * W1:4 * W1 + D]
        spare = 6 * W1
        tmpc = part(ring, spare, 2 * UW).rearrange("p (b n) -> p b n", b=2)
        junk_v = part(ring, spare + 2 * UW, 2 * UW)
        assert spare + 4 * UW == PH_SLOT0 * SLOT_F
        rgw = [part(ring, 2 * W1 + n * D, D) for n in range(3)] + [xh[:, 2, :]]
        wsp = part(xh[:, :, :].rearrange("p t d -> p (t d)"), 0, D).rearrange("p (g q) -> p g q", g=KT)
        bsp = part(xh[:, :, :].rearrange("p t d -> p (t d)"), D, D).rearrange("p (g q) -> p g q", g=KT)
        gfin = xh[:, 0, :]
        junk_f = xh[:, 1, :]

        def slot(s):
            return part(ring, s * SLOT_F, SLOT_F)

        def by_rows(s, width):
            return part(ring, s * SLOT_F, KT * width).rearrange("p (k n) -> p k n", k=KT)

        def by_ff(s, tiles):
            return part(ring, s * SLOT_F, tiles * D).rearrange("p (t n) -> p t n", t=tiles)

        HB = 2 * NTOK
        rbuf = [part(work, n * HB, HB).rearrange("p (d t) -> p d t", d=2) for n in range(2)]
        gibuf = [part(work, (2 + n) * HB, HB).rearrange("p (d t) -> p d t", d=2) for n in range(2)]
        qb, ab, om, hs = (part(work, (4 + n) * HB, HB).rearrange("p (d t) -> p d t", d=2) for n in range(4))
        junk_x = part(work, 4 * HB, D)
        def modp(q):
            early = q < len(ADA_ORDER) - 2
            return part(work, (4 * HB + D if early else 3 * UW) + (q % 2) * UW, UW)

        tmpo = part(work, 4 * HB, 2 * UW).rearrange("p (b n) -> p b n", b=2)
        g2s = part(work, 6144, UW)
        h2T = part(work, 0, KT * NTOK).rearrange("p (k t) -> p k t", k=KT)
        lgT = work[0:NE, 3072:3072 + NTOK]
        affT = work[0:NE, 3456:3456 + NTOK]
        posT = work[0:NE, 3840:3840 + NTOK]
        onesT = work[0:NE, 4224:4224 + NTOK]
        top8 = work[0:NE, 4608:4608 + 48].rearrange("p (r n) -> p r n", n=8)
        exl = part(work, 4672, TILES * NE).rearrange("p (t e) -> p t e", t=TILES)
        maskT = work[0:NE, 4736:4736 + NTOK]
        xg = part(work, 0, UW)
        xgT = [part(work, UW * (1 + n), UW).rearrange("p (k s) -> p k s", k=KT) for n in range(2)]
        sgact = [part(work, UW * (3 + n), UW) for n in range(2)]
        actT = [part(work, 2560 + 256 * n, 256).rearrange("p (f s) -> p f s", f=4) for n in range(2)]
        o_pair = part(work, 3072, D)
        GT = part(work, 4096, 2 * P).rearrange("p (b t) -> p b t", b=2)
        S = [part(work, 5120 + 96 * n, 96).rearrange("p (t s) -> p t s", t=TILES) for n in range(2)]
        G = part(work, 5312, 192).rearrange("p (b e s) -> p b e s", b=3, e=2)
        b_gate2 = work[0:1, 5632:5632 + D]
        ns_t = work[0:2 * KT, 5504:5504 + P]

        bank = [ctx.enter_context(nc.psum_tensor(f"bank{n}", [P, 512], F32)) for n in range(8)]

        rg_in, bg2_in = sem("rg_in"), sem("bg2_in")
        x_in, emb_in, col_in, wr_in = sem("x_in"), sem("emb_in"), sem("col_in"), sem("wr_in")
        sp_in, bg_in, gf_in = sem("sp_in"), sem("bg_in"), sem("gf_in")
        slot_in = [sem(f"slot_in{s}") for s in range(SLOTS)]
        consts = sem("consts")
        c32_ready = sem("c32_ready")
        link_v, link_p, link_a = sem("link_v"), sem("link_p"), sem("link_a")
        ms_ready, rstd_ready = sem("ms_ready"), sem("rstd_ready")
        xh_ready = sem("xh_ready")
        ada_mm, modp_ready, ada_out, mod_ready = sem("ada_mm"), sem("modp_ready"), sem("ada_out"), sem("mod_ready")
        wide_mm = sem("wide_mm")
        emptied = {"v": sem("emptied_v"), "a": sem("emptied_a")}
        lam_exp, lam_one, lam_ln, lam_ready = sem("lam_exp"), sem("lam_one"), sem("lam_ln"), sem("lam_ready")
        conv_done, tanh_done, om_ready, sqrt_done = sem("conv_done"), sem("tanh_done"), sem("om_ready"), sem("sqrt_done")
        gx_done, scan_done, yb_done = sem("gx_done"), sem("scan_done"), sem("yb_done")
        v_ready, ya_ready, merged_ready, x1_ready = sem("v_ready"), sem("ya_ready"), sem("merged_ready"), sem("x1_ready")
        ns_mm, ns_ready, out_done = sem("ns_mm"), sem("ns_ready"), sem("out_done")
        lg_mm, lg_ready, lg_tok, sub_ready, exp_ready = (sem(n) for n in ("lg_mm", "lg_ready", "lg_tok", "sub_ready", "exp_ready"))
        aff_ready, aff_mm, pos_ready, pos_mm = (sem(n) for n in ("aff_ready", "aff_mm", "pos_ready", "pos_mm"))
        s_ready, gather_mm, xg_ready, xgt_mm, xgt_ready = (sem(n) for n in ("s_ready", "gather_mm", "xg_ready", "xgt_mm", "xgt_ready"))
        xgt_scaled = sem("xgt_scaled")
        gu_mm, silu_done, act_done, actt_mm, actt_ready = (sem(n) for n in ("gu_mm", "silu_done", "act_done", "actt_mm", "actt_ready"))
        down_mm, o_ready, g_ready, gt_mm, gt_ready = (sem(n) for n in ("down_mm", "o_ready", "g_ready", "gt_mm", "gt_ready"))
        comb_mm, comb_added, y_ready = sem("comb_mm"), sem("comb_added"), sem("y_ready")

        def vcol(name, *shape):
            at, n = COLS[name]
            v = col[:, at:at + n]
            if len(shape) == 2:
                v = v.rearrange("p (a b) -> p a b", a=shape[0])
            return v

        cw, cb = vcol("conv_w", CONV_W, KT), vcol("conv_b")
        st0 = vcol("state", 2, KT)

        def phase_slot(n):
            return PH_SLOT0 + n % PH_SLOTS

        def expert_loads(i, u):
            s = SLOT_ORDER[u % SLOTS]
            return s, 16 * (PH_LOADS[s] + u // SLOTS + 1) + i * (16 * (UPP // SLOTS))

        def phase_used(n):
            kind, u = PHASE_UNITS[n]
            if kind == "ada":
                return ada_mm, ADA_AT[u] + 1
            if kind == "in" and u in (0, 1, 6, 7):
                return wide_mm, WIDE[f"{'gr' if u >= 6 else 'u'}{4 * (u % 2) + 3}"] + 1
            name = {4: "xr", 5: "xr", 2: "v", 3: "v", 8: "glA", 9: "glA", 10: "glB", 11: "glB"}[u] \
                if kind == "in" else kind
            return wide_mm, WIDE[name] + (TILES if name in ("v", "out") else KT // 2) * (u % 2 + 1)

        def pair_used(i, u):
            p, kind, j = PAIR_UNITS[u]
            return (down_mm, i * (2 * NJ) + (NJ * p + j + 3)) if kind == "down" else (gu_mm, i * (2 * NJ) + (NJ * p + j + 1))

        def outs_before(q):
            return sum(2 if u // 2 == 2 else 1 for u in ADA_ORDER[:q])

        def comb_bank(c):
            return bank[6 + c % 2]

        SETS = ((0, 0, NCTX), (1, NCTX, NTOK))

        block = ctx.enter_context(nc.Block())

        @block.sync
        def _(sp):
            sources = {
                "ada": w_ada, "in": w_in, "br_a": w_br_a, "br_b": w_br_b, "out": w_out}
            sp.dma_start(x[:, 0, :], x_prompt).then_inc(x_in, 16)
            sp.dma_start(x[:, 1:3, :], x_sample.rearrange("(t p) d -> p t d", p=P)).then_inc(x_in, 16)
            sp.dma_start(embt, emb.rearrange("(t p) d -> p t d", p=P)).then_inc(emb_in, 16)
            for n, (kind, u) in enumerate(PHASE_UNITS):
                if n >= PH_SLOTS:
                    sp.wait_ge(*phase_used(n - PH_SLOTS))
                s = phase_slot(n)
                src = sources[kind].rearrange("(k p) n -> p k n", p=P)[:, :, u * UW:(u + 1) * UW]
                sp.dma_start(by_rows(s, UW), src).then_inc(slot_in[s], 16)

            def load(i, u, e):
                _, kind, j = PAIR_UNITS[u]
                f, w = FCH[j]
                s, _ = expert_loads(i, u)
                if kind == "down":
                    dst = by_ff(s, w // P)
                    src = w_down[bass.ds(e, 1), f:f + w, :].rearrange("e (t p) n -> p (e t) n", p=P)
                else:
                    dst = by_rows(s, w)
                    src = (w_gate if kind == "gate" else w_up)[bass.ds(e, 1), :, f:f + w]
                    src = src.rearrange("e (k p) n -> p (e k) n", p=P)
                sp.dma_start(dst, src).then_inc(slot_in[s], 16)

            def used(kind, u):
                return phase_used(UNIT_AT[kind, u])

            dead = [
                used("in", 11),
                used("br_b", 1),
                (merged_ready, KT),
                (emptied["v"], emptied_by("v", WIDE["out"] + 2 * TILES)),
                used("out", 1),
            ] + [phase_used(n) for n in range(NPH - PH_SLOTS, NPH)]
            for n in range(SLOTS):
                sp.wait_ge(*dead[n])
                load(0, n, PAIR_UNITS[n][0])

            def ahead(i, u):
                sp.wait_ge(*pair_used(i, u - SLOTS))
                nxt, v = divmod(u, UPP)
                load(i, v, i * 2 + (2 * nxt + PAIR_UNITS[v][0]))

            with sp.Fori(0, PAIRS - 1) as i:
                for u in range(SLOTS, UPP + SLOTS):
                    ahead(i, u)
            for u in range(SLOTS, UPP):
                ahead(PAIRS - 1, u)

            for t in range(TILES):
                sp.wait_ge(y_ready, t + 1)
                dst = y_prompt if t == 0 else y_sample[(t - 1) * P:t * P, :]
                sp.dma_start(dst, x[:, t, :]).then_inc(out_done, 16)
            sp.wait_ge(out_done, 16 * (TILES + 1))

        @block.gpsimd
        def _(pool):
            count = [0]

            def link(ins):
                count[0] += 1
                ins.then_inc(link_p, 1)
                pool.wait_ge(link_p, count[0])

            link(pool.memset(c32[:, :, :], 0.0))
            pool.memset(half[:, :], -0.5)
            link(pool.memset(two_ones[:, :], 0.0))
            pool.memset(two_ones[:, 0:2], 1.0)
            pool.memset(posm[:, :, :], 0.0)
            pool.memset(selb[:, :, :], 0.0)
            link(pool.memset(ident[:, :], 0.0))
            for j in range(4):
                link(pool.affine_select(out=selb[:, :, :], in_=selb[:, :, :], compare_op=ALU.not_equal, fill=1.0,
                                        base=-32 * j, pattern=[[-1, 2], [0, P]], channel_multiplier=1))
            link(pool.affine_select(out=ident[:, :], in_=ident[:, :], compare_op=ALU.not_equal, fill=1.0,
                                    base=0, pattern=[[-1, P]], channel_multiplier=1))
            sg = selg[:, :].rearrange("p (h m s) -> p h m s", h=2, m=2)
            for m in range(2):
                sv = selb[:, 1 - m, 0:64].rearrange("p (h s) -> p h s", h=2)
                pool.tensor_copy(sg[:, :, m, :], sv)
            link(pool.iota(iota_i[:, :], pattern=[[1, SL]], base=1, channel_multiplier=0))
            pool.tensor_copy(iota[:, :], iota_i[:, :]).then_inc(consts, 1)

            def power(n):
                pool.wait_ge(ms_ready, n + 1)
                pool.tensor_tensor(rstd[:, n, :], ss[:, n, 0:TILES], half[:, 0:1].to_broadcast([P, TILES]),
                                   ALU.pow).then_inc(rstd_ready, 1)

            def gates_times_x(h):
                pool.wait_ge(emptied["a"], emptied_by("a", WIDE[f"rg{h}"] + 4))
                pool.wait_ge(conv_done, h + 1)
                g = gibuf[h % 2]
                pool.tensor_tensor(g, g, xc[:, h, :].unsqueeze(1).to_broadcast([P, 2, NTOK]),
                                   ALU.mult).then_inc(gx_done, 1)

            def states_times_gr(h):
                pool.wait_ge(scan_done, h + 1)
                pool.wait_ge(emptied["a"], emptied_by("a", WIDE[f"gr{h}"] + 1))
                link(pool.tensor_copy(ns[:, 0, h:h + 1], hs[:, 0, NCTX - 1:NCTX]))
                link(pool.tensor_copy(ns[:, 1, h:h + 1], hs[:, 1, 0:1]))
                link(pool.tensor_tensor(hs[:, 0, :], hs[:, 0, :], hs[:, 1, :], ALU.add))
                pool.tensor_tensor(grT[:, h, :], grT[:, h, :], hs[:, 0, :], ALU.mult).then_inc(yb_done, 1)

            power(0)
            for h in range(KT):
                gates_times_x(h)
                if h >= 1:
                    states_times_gr(h - 1)
            states_times_gr(KT - 1)
            for n in range(1, 4):
                power(n)

        @block.scalar
        def _(act):
            act.dma_start(col[:, :], cols).then_inc(col_in, 16)
            act.dma_start(wr[:, :, :], w_router.rearrange("p (k e) -> p k e", k=KT)).then_inc(wr_in, 16)
            act.wait_ge(col_in, 16)
            act.wait_ge(link_p, 1)
            act.activation(c32[:, :, 0:2], vcol("c", KT, 2), ACT.Silu).then_inc(c32_ready, 1)
            act.wait_ge(lam_one, 1)
            act.activation(lam[:, 1, :], lam[:, 0, :], ACT.Exp, scale=-1.0).then_inc(lam_exp, 1)
            act.wait_ge(lam_one, 2)
            act.activation(lam[:, 3, :], lam[:, 2, :], ACT.Ln).then_inc(lam_ln, 1)

            def take(n, out, src, func, **kw):
                act.wait_ge(wide_mm, n + 1)
                return act.activation(out, src, func, **kw).then_inc(emptied["a"], 1)

            def modulated(name, out, mod):
                for k in range(1, KT, 2):
                    n = WIDE[name] + k
                    act.wait_ge(wide_mm, n + 1)
                    for m, a, b in SETS:
                        ins = act.activation(out[:, k, a:b], bank[n % WIDE_BANKS][:, a:b], ACT.Identity,
                                             scale=mod[:, 0, k, m:m + 1], bias=mod[:, 1, k, m:m + 1])
                    ins.then_inc(emptied["a"], 1)

            act.wait_ge(mod_ready, 4)
            modulated("hT", hT, mod1)
            act.wait_ge(wide_mm, WIDE["hT"] + KT)
            act.dma_start(wsp, w_spatial_t.rearrange("q (g p) -> q g p", g=KT)).then_inc(sp_in, 16)
            act.dma_start(bsp, b_spatial.to_broadcast([P, D]).rearrange("q (g p) -> q g p", g=KT)).then_inc(sp_in, 16)
            for n in range(4):
                act.dma_start(rgw[n], rg_w[:, n * D:(n + 1) * D]).then_inc(rg_in, 16)
            for b in range(KT):
                n = WIDE["xr"] + b
                take(n, xr[:, b, :], bank[n % WIDE_BANKS][:, 0:NTOK], ACT.Copy)

            def root(h):
                act.wait_ge(om_ready, h + 1)
                act.activation(om, om, ACT.Sqrt, bias=tiny[:, 0:1]).then_inc(sqrt_done, 1)

            act.wait_ge(lam_ready, 1)
            for b in range(KT):
                n = WIDE[f"gr{b}"]
                take(n, grT[:, b, :], bank[n % WIDE_BANKS][:, 0:NTOK], ACT.Gelu_apprx_tanh)
                n = WIDE[f"u{b}"]
                take(n, uT[:, b, :], bank[n % WIDE_BANKS][:, 0:NTOK], ACT.Gelu_apprx_tanh)
                if b >= 2:
                    act.wait_ge(scan_done, b - 1)
                    act.wait_ge(gx_done, b - 1)
                n = WIDE[f"rg{b}"]
                for q in range(4):
                    d, buf, bias = q // 2, (rbuf, gibuf)[q % 2][b % 2], vcol(("rg_b_a", "rg_b_x")[q % 2], 2, KT)
                    take(n + q, buf[:, d, :], bank[(n + q) % WIDE_BANKS][:, 0:NTOK], ACT.Sigmoid,
                         bias=bias[:, d, b:b + 1])
                act.wait_ge(emptied["a"], emptied_by("a", n + 4))
                for d in range(2):
                    act.activation(rbuf[b % 2][:, d, :], rbuf[b % 2][:, d, :], ACT.Tanh,
                                   scale=negsp[:, d, b:b + 1]).then_inc(tanh_done, 1)
                if b >= 1:
                    root(b - 1)
            root(KT - 1)
            for g in range(2 * TILES):
                n, t, hf = WIDE["v"] + g, g % TILES, g // TILES
                take(n, vtok[:, t, hf * UW:(hf + 1) * UW], bank[n % WIDE_BANKS][:, :], ACT.Gelu_apprx_tanh)
            for b in range(KT):
                n = WIDE["glA"] + b
                take(n, glA[:, b, :], bank[n % WIDE_BANKS][:, 0:NTOK], ACT.Sigmoid)
            act.wait_ge(wide_mm, WIDE["br_a"] + KT)
            act.dma_start(b_gate1, b_ada[:, 2 * D:3 * D]).then_inc(bg_in, 16)
            act.wait_ge(gx_done, KT)
            for b in range(KT):
                n = WIDE["glB"] + b
                take(n, glB[:, b, :], bank[n % WIDE_BANKS][:, 0:NTOK], ACT.Sigmoid)
            act.wait_ge(yb_done, KT)
            act.dma_start(b_gate2, b_ada[:, 5 * D:6 * D]).then_inc(bg2_in, 16)
            act.wait_ge(mod_ready, outs_before(10))
            act.wait_ge(ns_ready, 1)
            act.dma_start(new_state, ns_t).then_inc(out_done, 16)
            modulated("h2T", h2T, mod2)
            act.wait_ge(sub_ready, 1)
            act.activation(exl, exl, ACT.Exp).then_inc(exp_ready, 1)

            with act.Fori(0, PAIRS) as i:
                for p in range(2):
                    for j, (_, w) in enumerate(FCH):
                        act.wait_ge(gu_mm, i * (2 * NJ) + (NJ * p + j + 1))
                        act.activation(sgact[j % 2][0:64, 0:w], bank[j % 2][0:64, 0:w],
                                       ACT.Silu).then_inc(silu_done, 1)
            act.wait_ge(gather_mm, NE + 1)
            act.dma_start(gfin, final_norm_g.to_broadcast([P, D])).then_inc(gf_in, 16)

        @block.vector
        def _(dve):
            count = [0]

            def link(ins):
                count[0] += 1
                ins.then_inc(link_v, 1)
                dve.wait_ge(link_v, count[0])

            dve.memset(tiny[:, :], 1e-30)
            dve.wait_ge(col_in, 16)
            L = vcol("rg_lambda")
            link(dve.tensor_scalar(lam[:, 1, :], L, -1.0, None, ALU.mult))
            dve.tensor_tensor(lam[:, 0, :], L, lam[:, 1, :], ALU.max).then_inc(lam_one, 1)
            dve.wait_ge(lam_exp, 1)
            dve.tensor_scalar(lam[:, 2, :], lam[:, 1, :], 1.0, None, ALU.add).then_inc(lam_one, 1)
            dve.wait_ge(lam_ln, 1)
            link(dve.tensor_scalar(lam[:, 2, :], lam[:, 2, :], -1.0, None, ALU.add))
            link(dve.tensor_scalar(lam[:, 0, :], lam[:, 2, :], 0.0, None, ALU.is_equal))
            dve.tensor_tensor(lam[:, 2, :], lam[:, 2, :], lam[:, 0, :], ALU.add)
            link(dve.tensor_tensor(lam[:, 3, :], lam[:, 3, :], lam[:, 0, :], ALU.add))
            link(dve.reciprocal(lam[:, 2, :], lam[:, 2, :]))
            link(dve.tensor_tensor(lam[:, 3, :], lam[:, 3, :], lam[:, 2, :], ALU.mult))
            link(dve.tensor_tensor(lam[:, 3, :], lam[:, 3, :], lam[:, 1, :], ALU.mult))
            link(dve.tensor_scalar(lam[:, 2, :], L, -1.0, 0.0, ALU.mult, ALU.max))
            link(dve.tensor_tensor(lam[:, 3, :], lam[:, 3, :], lam[:, 2, :], ALU.add))
            dve.tensor_scalar(negsp[:, :, :].rearrange("p d k -> p (d k)"), lam[:, 3, :], -RG_C / 2, None,
                              ALU.mult).then_inc(lam_ready, 1)

            dve.wait_ge(emb_in, 16)
            dve.wait_ge(x_in, 32)
            link(dve.tensor_tensor(x[:, 1:3, :], x[:, 1:3, :], embt, ALU.add))

            def mean_square(n, sums=1):
                if sums == 2:
                    link(dve.tensor_tensor(ss[:, n, 0:TILES], ss[:, n, 0:TILES], ss[:, n, TILES:2 * TILES], ALU.add))
                dve.tensor_scalar(ss[:, n, 0:TILES], ss[:, n, 0:TILES], 1.0 / D, EPS, ALU.mult,
                                  ALU.add).then_inc(ms_ready, 1)
                dve.wait_ge(rstd_ready, n + 1)

            def squares(n, t, src, junk):
                link(dve.tensor_tensor_reduce(out=junk, in0=src, in1=src, scale=1.0, scalar=0.0, op0=ALU.mult,
                                              op1=ALU.add, accum_out=ss[:, n, t:t + 1]))

            def normed(n, out, src, signal):
                for t in range(TILES):
                    dve.tensor_scalar(out[:, t, :], src[:, t, :], rstd[:, n, t:t + 1], None,
                                      ALU.mult).then_inc(signal, 1)

            for t in range(TILES):
                squares(0, t, x[:, t, :], junk_x)
            mean_square(0)
            normed(0, xh, x, xh_ready)

            def ada(u):
                ada_rows(u)
                ada_result(u)

            def ada_rows(u):
                q = ADA_AT[u]
                dve.wait_ge(ada_mm, q + 1)
                if q >= 2:
                    dve.wait_ge(ada_out, outs_before(q - 1))
                dve.tensor_copy(modp(q), bank[6 + q % 2][:, :]).then_inc(modp_ready, 1)

            def ada_result(u):
                q, kind, hf = ADA_AT[u], u // 2, u % 2
                base = outs_before(q)
                if kind in (2, 5):
                    for m in range(2 if kind == 2 else 1):
                        dve.wait_ge(ada_out, base + m + 1)
                        if kind == 2:
                            dve.tensor_copy(g1b[:, m, hf * UW:(hf + 1) * UW], bank[5][:, :]).then_inc(mod_ready, 1)
                        else:
                            rows = slice(64 * hf, 64 * hf + 64)
                            dve.tensor_copy(g2s[rows, :], bank[5][rows, :]).then_inc(mod_ready, 1)
                    return
                dve.wait_ge(ada_out, base + 1)
                ks = slice(4 * hf, 4 * hf + 4)
                rows = bank[5][:, :].rearrange("p (k j c) -> p k c j", k=4, j=4)[:, :, 0:2, :]
                got = mod_sum[:, :, :]
                link(dve.tensor_reduce(got, rows, AX.X, ALU.add))
                bias = vcol("b_ada", 6, KT)[:, kind, ks].unsqueeze(2).to_broadcast([P, 4, 2])
                mod, gain = (mod1, vcol("norm1_g")) if kind < 2 else (mod2, vcol("norm2_g"))
                if kind in (0, 3):
                    dve.tensor_tensor(mod[:, 1, ks, :], got, bias, ALU.add).then_inc(mod_ready, 1)
                else:
                    link(dve.tensor_tensor(mod_raw[:, :, :], got, bias, ALU.add))
                    dve.scalar_tensor_tensor(out=mod[:, 0, ks, :], in0=mod_raw[:, :, :], scalar=1.0,
                                             in1=gain[:, ks].unsqueeze(2).to_broadcast([P, 4, 2]), op0=ALU.add,
                                             op1=ALU.mult).then_inc(mod_ready, 1)

            def modulated(name, out, mod):
                for k in range(0, KT, 2):
                    n = WIDE[name] + k
                    dve.wait_ge(wide_mm, n + 1)
                    for m, a, b in SETS:
                        ins = dve.tensor_scalar(out[:, k, a:b], bank[n % WIDE_BANKS][:, a:b],
                                                mod[:, 0, k, m:m + 1], mod[:, 1, k, m:m + 1], ALU.mult, ALU.add)
                    ins.then_inc(emptied["v"], 1)

            for u in ADA_FIRST:
                ada(u)
            dve.wait_ge(mod_ready, 4)
            modulated("hT", hT, mod1)

            for h in range(KT):
                dve.wait_ge(emptied["a"], emptied_by("a", WIDE["xr"] + h + 1))
                link(dve.tensor_scalar(xc[:, h, :], xr[:, h, :], cw[:, 2, h:h + 1], cb[:, h:h + 1], ALU.mult, ALU.add))
                for k in (0, 1, 3):
                    s = k - 2
                    for _, a, b in SETS:
                        lo, hi = max(a, a - s), min(b, b - s)
                        ins = dve.scalar_tensor_tensor(out=xc[:, h, lo:hi], in0=xr[:, h, lo + s:hi + s],
                                                       scalar=cw[:, k, h:h + 1], in1=xc[:, h, lo:hi],
                                                       op0=ALU.mult, op1=ALU.add)
                        if k == 3 and a:
                            ins.then_inc(conv_done, 1)
                        elif a:
                            link(ins)

            def decay(h):
                t2 = rbuf[h % 2]
                dve.wait_ge(tanh_done, 2 * h + 2)
                link(dve.tensor_scalar(qb, t2, -1.0, 1.0, ALU.mult, ALU.add))
                link(dve.reciprocal(qb, qb))
                dve.tensor_scalar(ab, qb, 2.0, -1.0, ALU.mult, ALU.add)
                link(dve.scalar_tensor_tensor(out=om, in0=t2, scalar=-2.0, in1=qb, op0=ALU.mult, op1=ALU.mult))
                dve.scalar_tensor_tensor(out=om, in0=ab, scalar=1.0, in1=om, op0=ALU.add,
                                         op1=ALU.mult).then_inc(om_ready, 1)

            def scans(h):
                dve.wait_ge(sqrt_done, h + 1)
                dve.wait_ge(gx_done, h + 1)
                link(dve.tensor_tensor(om, om, gibuf[h % 2], ALU.mult))
                if h >= 1:
                    dve.wait_ge(yb_done, h)
                for m, a, b in SETS:
                    start = [0.0, 0.0] if m == 0 else [st0[:, d, h:h + 1] for d in range(2)]
                    dve.tensor_tensor_scan(hs[:, 0, a:b], ab[:, 0, a:b], om[:, 0, a:b], start[0], ALU.mult, ALU.add)
                    ins = dve.tensor_tensor_scan(hs[:, 1, a:b][:, ::-1], ab[:, 1, a:b][:, ::-1],
                                                 om[:, 1, a:b][:, ::-1], start[1], ALU.mult, ALU.add)
                ins.then_inc(scan_done, 1)

            for h in range(KT):
                if h >= 1:
                    scans(h - 1)
                decay(h)
            scans(KT - 1)

            dve.wait_ge(emptied["a"], emptied_by("a", WIDE["v"] + 2 * TILES))
            for t in range(TILES):
                squares(1, t, vtok[:, t, :], junk_v)
            mean_square(1)
            normed(1, vtok, vtok, v_ready)
            dve.wait_ge(sp_in, 32)

            def three(ap):
                return ap.rearrange("p (t q) -> p t q", t=TILES)

            for g in range(KT):
                n = WIDE["spatial"] + g
                tmp = tmpc[:, g % 2, 0:NTOK]
                dve.wait_ge(wide_mm, n + 1)
                dve.scalar_tensor_tensor(out=three(tmp), in0=three(bank[n % WIDE_BANKS][:, 0:NTOK]),
                                         scalar=vcol("v_norm_g")[:, g:g + 1],
                                         in1=bsp[:, g, :].unsqueeze(1).to_broadcast([P, TILES, P]),
                                         op0=ALU.mult, op1=ALU.add).then_inc(emptied["v"], 1)
                dve.wait_ge(emptied["v"], emptied_by("v", n + 1))
                dve.wait_ge(emptied["a"], emptied_by("a", WIDE[f"u{g}"] + 1))
                dve.tensor_tensor(uT[:, g, :], uT[:, g, :], tmp, ALU.mult).then_inc(ya_ready, 1)

            for b in range(KT):
                n = WIDE["br_a"] + b
                dve.wait_ge(wide_mm, n + 1)
                dve.wait_ge(emptied["a"], emptied_by("a", WIDE["glA"] + b + 1))
                dve.tensor_tensor(glA[:, b, :], glA[:, b, :], bank[n % WIDE_BANKS][:, 0:NTOK],
                                  ALU.mult).then_inc(emptied["v"], 1)
            for u in ADA_GATE1 + ADA_SCALE2:
                ada(u)
            for b in range(KT):
                n = WIDE["br_b"] + b
                tmp = tmpc[:, b % 2, 0:NTOK]
                dve.wait_ge(wide_mm, n + 1)
                dve.wait_ge(emptied["a"], emptied_by("a", WIDE["glB"] + b + 1))
                dve.tensor_tensor(tmp, glB[:, b, :], bank[n % WIDE_BANKS][:, 0:NTOK],
                                  ALU.mult).then_inc(emptied["v"], 1)
                dve.wait_ge(emptied["v"], emptied_by("v", n + 1))
                dve.tensor_tensor(merged[:, b, :], glA[:, b, :], tmp, ALU.add).then_inc(merged_ready, 1)

            for g in range(2 * TILES):
                n, t, hf = WIDE["out"] + g, g % TILES, g // TILES
                hs_ = slice(hf * UW, (hf + 1) * UW)
                dve.wait_ge(wide_mm, n + 1)
                dve.tensor_tensor(tmpo[:, g % 2, :], g1b[:, min(t, 1), hs_], bank[n % WIDE_BANKS][:, :],
                                  ALU.mult).then_inc(emptied["v"], 1)
                dve.wait_ge(emptied["v"], emptied_by("v", n + 1))
                dve.tensor_tensor(x[:, t, hs_], x[:, t, hs_], tmpo[:, g % 2, :], ALU.add).then_inc(x1_ready, 1)
            dve.wait_ge(x1_ready, 2 * TILES)
            for t in range(TILES):
                squares(2, t, x[:, t, :], junk_x)
            mean_square(2)
            normed(2, xh, x, xh_ready)
            dve.wait_ge(ns_mm, 1)
            dve.tensor_copy(ns_t, bank[5][0:2 * KT, 0:P]).then_inc(ns_ready, 1)
            for u in ADA_SHIFT2:
                ada(u)
            dve.wait_ge(mod_ready, outs_before(10))
            modulated("h2T", h2T, mod2)

            dve.wait_ge(lg_mm, 1)
            dve.tensor_copy(lgT, bank[0][0:NE, 0:NTOK]).then_inc(lg_ready, 1)
            dve.wait_ge(lg_tok, 1)
            lg = bank[1][:, 0:TILES * NE].rearrange("p (t e) -> p t e", t=TILES)
            link(dve.tensor_reduce(smax[:, 0, :], lg, AX.X, ALU.max))
            dve.tensor_tensor(exl, lg, smax[:, 0, :].unsqueeze(2).to_broadcast([P, TILES, NE]),
                              ALU.subtract).then_inc(sub_ready, 1)
            dve.wait_ge(exp_ready, 1)
            link(dve.tensor_reduce(smax[:, 1, :], exl, AX.X, ALU.add))
            link(dve.reciprocal(smax[:, 2, :], smax[:, 1, :]))
            dve.tensor_tensor(aff[:, :, :], exl, smax[:, 2, :].unsqueeze(2).to_broadcast([P, TILES, NE]),
                              ALU.mult).then_inc(aff_ready, 1)
            dve.memset(onesT, 1.0)
            dve.wait_ge(aff_mm, 1)
            link(dve.tensor_copy(affT, bank[2][0:NE, 0:NTOK]))
            r = 0
            for (_, a, b), cap in zip(SETS, (CAP_CTX, CAP_LAT)):
                for _ in range(cap // 8):
                    link(dve.max(top8[:, r, :], affT[:, a:b]))
                    link(dve.match_replace(out=affT[:, a:b], in_to_replace=top8[:, r, :], in_values=affT[:, a:b],
                                           imm_value=-1.0))
                    r += 1
            link(dve.tensor_scalar(maskT, affT, -1.0, None, ALU.is_equal))
            for _, a, b in SETS:
                last = dve.tensor_tensor_scan(posT[:, a:b], onesT[:, a:b], maskT[:, a:b], 0.0, ALU.mult, ALU.add)
            link(last)
            dve.tensor_tensor(posT, posT, maskT, ALU.mult).then_inc(pos_ready, 1)
            dve.wait_ge(pos_mm, 1)
            link(dve.tensor_copy(posm[:, :, 0:NE], bank[1][:, 0:TILES * NE].rearrange("p (t e) -> p t e", t=TILES)))

            def choose(e, par):
                dve.tensor_tensor(S[par], iota[:, :].unsqueeze(1).to_broadcast([P, TILES, SL]),
                                  posm[:, :, bass.ds(e, 1)].to_broadcast([P, TILES, SL]),
                                  ALU.is_equal).then_inc(s_ready, 1)

            def gathered():
                dve.tensor_copy(xg, bank[6][:, :]).then_inc(xg_ready, 1)

            def modulate(par, n):
                for m, rows in ((1, slice(0, SL)), (0, slice(SL, 2 * SL))):
                    got = bank[7][:, :].rearrange("p (b h s) -> p h b s", b=4, h=2)[:, :, :, rows]
                    out = xgT[par].rearrange("p (h b) s -> p h b s", h=2)[:, :, :, rows]
                    for hf in range(2):
                        ks = slice(4 * hf, 4 * hf + 4)
                        last = dve.tensor_tensor(out[:, hf], got[:, hf],
                                                 mod2[:, 0, ks, m:m + 1].to_broadcast([P, 4, SL]), ALU.mult)
                last.then_inc(xgt_scaled, 1)
                dve.wait_ge(xgt_scaled, n)
                for m, rows in ((1, slice(0, SL)), (0, slice(SL, 2 * SL))):
                    last = dve.tensor_tensor(xgT[par][:, :, rows], xgT[par][:, :, rows],
                                             mod2[:, 1, :, m:m + 1].to_broadcast([P, KT, SL]), ALU.add)
                last.then_inc(xgt_ready, 1)

            def add_combined(c, n):
                t, hf = c // 2, c % 2
                dve.wait_ge(comb_mm, n + 1)
                hs_ = slice(hf * UW, (hf + 1) * UW)
                dve.tensor_tensor(x[:, t, hs_], x[:, t, hs_], comb_bank(c)[:, :], ALU.add).then_inc(comb_added, 1)

            def copy_act_t(n, j):
                dve.wait_ge(actt_mm, n + 3)
                dve.wait_ge(down_mm, n + 1)
                tiles = FCH[j][1] // P
                got = bank[2 + j % 2][:, 0:P * tiles].rearrange("p (f h s) -> p f h s", f=tiles, h=2)
                dve.tensor_copy(actT[j % 2][:, 0:tiles, :], got[:, :, 1, :]).then_inc(actt_ready, 1)

            choose(0, 0)
            for u in ADA_GATE2:
                ada_rows(u)
            dve.wait_ge(gather_mm, 1)
            gathered()
            dve.wait_ge(xgt_mm, 1)
            modulate(0, 1)
            for u in ADA_GATE2:
                ada_result(u)
            dve.memset(o_pair, 0.0).then_inc(o_ready, 2)
            dve.memset(GT, 0.0).then_inc(gt_ready, 1)
            for n, (freed, uses) in enumerate(((act_done, 2), (actt_mm, 2), (actt_ready, 2), (down_mm, 2),
                                               (gt_mm, 1), (comb_added, 1))):
                dve.memset(lam[:, 0, n:n + 1], 0.0).then_inc(freed, uses)

            with dve.Fori(0, PAIRS) as i:
                for p in range(2):
                    e = i * 2 + p
                    for j, (_, w) in enumerate(FCH):
                        n = i * (2 * NJ) + (NJ * p + j)
                        if j >= 1:
                            copy_act_t(n - 1, j - 1)
                        dve.wait_ge(silu_done, n + 1)
                        dve.wait_ge(actt_mm, n + 1)
                        dve.tensor_tensor(sgact[j % 2][64:128, 0:w], sgact[j % 2][0:64, 0:w],
                                          bank[j % 2][64:128, 0:w], ALU.mult).then_inc(act_done, 1)
                        if j == 0:
                            dve.wait_ge(s_ready, e + 1)
                            dve.wait_ge(gt_mm, i + 1)
                            dve.tensor_tensor(G[:, 0:3:2, p, :], S[p][:, 1:3, :],
                                              aff[:, 1:3, bass.ds(e, 1)].to_broadcast([P, 2, SL]), ALU.mult)
                            dve.tensor_tensor(G[:, 1, p, :].unsqueeze(1), S[p][:, 0:1, :],
                                              aff[:, 0:1, bass.ds(e, 1)].to_broadcast([P, 1, SL]),
                                              ALU.mult).then_inc(g_ready, 1)
                            dve.wait_ge(gather_mm, e + 1)
                            choose(e + 1, 1 - p)
                        if j == 2:
                            dve.wait_ge(gather_mm, e + 2)
                            gathered()
                        if j == 3:
                            dve.wait_ge(xgt_mm, e + 2)
                            modulate(1 - p, e + 2)
                        if p == 0 and j >= 4:
                            for c in range(2 * (j - 4), 2 * (j - 4) + 2):
                                add_combined(c, i * 6 + c)
                        if p == 1 and j == 4:
                            dve.wait_ge(gt_mm, i + 2)
                            dve.tensor_copy(GT[:, 0, :], bank[6][:, 0:P])
                            dve.tensor_copy(GT[0:64, 1, :], bank[6][0:64, P:2 * P]).then_inc(gt_ready, 1)
                    if p == 0:
                        for c in (4, 5):
                            add_combined(c, i * 6 + c)
                    copy_act_t(i * (2 * NJ) + (NJ * p + NJ - 1), NJ - 1)
                    dve.wait_ge(down_mm, i * (2 * NJ) + (NJ * (p + 1) + 2))
                    for q, row in enumerate((32 * p, 64 + 32 * p, 32 * p, 64 + 32 * p)):
                        src, hf = slice(32 * q, 32 * q + 32), q // 2
                        last = dve.tensor_tensor(o_pair[row:row + 32, hf * UW:(hf + 1) * UW], bank[4 + p][src, :],
                                                 g2s[src, :], ALU.mult)
                    last.then_inc(o_ready, 1)

            for c in range(6):
                add_combined(c, PAIRS * 6 + c)
            dve.wait_ge(comb_added, (PAIRS + 1) * 6 + 1)
            dve.wait_ge(gf_in, 16)
            for t in range(TILES):
                squares(3, t, x[:, t, :], junk_f)
            mean_square(3)
            for t in range(TILES):
                dve.scalar_tensor_tensor(out=x[:, t, :], in0=x[:, t, :], scalar=rstd[:, 3, t:t + 1], in1=gfin,
                                         op0=ALU.mult, op1=ALU.mult).then_inc(y_ready, 1)

        @block.tensor
        def _(pe):
            def unit_in(kind, u):
                n = UNIT_AT[kind, u]
                s = phase_slot(n)
                pe.wait_ge(slot_in[s], 16 * (n // PH_SLOTS + 1))
                return s

            def wide(n):
                if n >= WIDE_BANKS:
                    e = _EVAC[n - WIDE_BANKS]
                    pe.wait_ge(emptied[e], emptied_by(e, n - WIDE_BANKS + 1))
                return bank[n % WIDE_BANKS]

            def all_emptied(n):
                for e in "va":
                    pe.wait_ge(emptied[e], emptied_by(e, n))

            def transposed(name):
                for k in range(KT):
                    to = wide(WIDE[name] + k)
                    for t in range(TILES):
                        ins = pe.transpose(to[:, t * P:(t + 1) * P], xh[:, t, k * P:(k + 1) * P], ident[:, :])
                    ins.then_inc(wide_mm, 1)

            def channel_major(kind, u, src, name):
                s = unit_in(kind, u)
                w = by_rows(s, UW)
                for b in range(4):
                    channel_block(w, b, src, WIDE[name] + 4 * (u % 2) + b)

            def channel_block(w, b, src, n):
                to = wide(n)
                for k in range(KT):
                    ins = pe.matmul(to[:, 0:NTOK], w[:, k, b * P:(b + 1) * P], src[:, k, :],
                                    start=(k == 0), stop=(k == KT - 1))
                ins.then_inc(wide_mm, 1)

            def token_major(kind, u, src, name):
                s = unit_in(kind, u)
                w = by_rows(s, UW)
                for t in range(TILES):
                    n = WIDE[name] + TILES * (u % 2) + t
                    to = wide(n)
                    for k in range(KT):
                        ins = pe.matmul(to[:, :], src[:, k, t * P:(t + 1) * P], w[:, k, :],
                                        start=(k == 0), stop=(k == KT - 1))
                    ins.then_inc(wide_mm, 1)

            def ada_rows(u):
                q, gate = ADA_AT[u], u // 2 in (2, 5)
                s = unit_in("ada", u)
                w = by_rows(s, UW)
                if q >= 2:
                    pe.wait_ge(modp_ready, q - 1)
                to = bank[6 + q % 2]
                for k in range(KT):
                    j = k % 4
                    ins = pe.matmul(to[32 * j:32 * j + 32, :], c32[:, k, :], w[:, k, :], start=(k < 4),
                                    stop=(k >= 4 and not (gate and j == 0)))
                if gate:
                    bias = (b_gate1 if u // 2 == 2 else b_gate2)[:, (u % 2) * UW:(u % 2 + 1) * UW]
                    ins = pe.matmul(to[0:32, :], two_ones[:, :], bias, start=False, stop=True)
                ins.then_inc(ada_mm, 1)

            def ada_sums(u):
                q, kind = ADA_AT[u], u // 2
                pe.wait_ge(modp_ready, q + 1)
                rows = modp(q)
                if kind in (2, 5):
                    for m in range(2 if kind == 2 else 1):
                        pe.wait_ge(mod_ready, outs_before(q) + m)
                        pe.matmul(bank[5][:, :], selb[:, m, :] if kind == 2 else selg[:, :], rows, start=True,
                                  stop=True).then_inc(ada_out, 1)
                    return
                pe.wait_ge(mod_ready, outs_before(q))
                for b in range(4):
                    ins = pe.transpose(bank[5][:, b * P:(b + 1) * P], rows[:, b * P:(b + 1) * P], ident[:, :])
                ins.then_inc(ada_out, 1)

            def ada(units):
                for a, b in zip(units, units[1:] + [None]):
                    if a == units[0]:
                        ada_rows(a)
                    if b is not None:
                        ada_rows(b)
                    ada_sums(a)

            pe.wait_ge(consts, 1)
            pe.wait_ge(c32_ready, 1)
            ada(ADA_FIRST)
            pe.wait_ge(xh_ready, TILES)
            transposed("hT")
            all_emptied(WIDE["hT"] + KT)
            channel_major("in", 4, hT, "xr")
            channel_major("in", 5, hT, "xr")
            pe.wait_ge(rg_in, 64)
            for b in range(KT):
                for name, u in (("gr", 6), ("u", 0)):
                    w = by_rows(unit_in("in", u + b // 4), UW)
                    channel_block(w, b % 4, hT, WIDE[f"{name}{b}"])
                pe.wait_ge(conv_done, b + 1)
                for q in range(4):
                    n = WIDE[f"rg{b}"] + q
                    to = wide(n)
                    at = rgw[2 * (q % 2) + q // 2]
                    pe.matmul(to[:, 0:NTOK], at[:, b * P:(b + 1) * P], xc[:, b, :], start=True,
                              stop=True).then_inc(wide_mm, 1)
            token_major("in", 2, hT, "v")
            token_major("in", 3, hT, "v")
            pe.wait_ge(v_ready, TILES)
            pe.wait_ge(sp_in, 32)
            for g in range(KT):
                n = WIDE["spatial"] + g
                to = wide(n)
                for t in range(TILES):
                    ins = pe.matmul(to[:, t * P:(t + 1) * P], vtok[:, t, g * P:(g + 1) * P], wsp[:, g, :],
                                    start=True, stop=True)
                ins.then_inc(wide_mm, 1)
            channel_major("in", 8, hT, "glA")
            channel_major("in", 9, hT, "glA")
            pe.wait_ge(ya_ready, KT)
            channel_major("br_a", 0, uT, "br_a")
            channel_major("br_a", 1, uT, "br_a")
            channel_major("in", 10, hT, "glB")
            channel_major("in", 11, hT, "glB")
            pe.wait_ge(bg_in, 16)
            ada(ADA_GATE1 + ADA_SCALE2)
            pe.wait_ge(yb_done, KT)
            channel_major("br_b", 0, grT, "br_b")
            channel_major("br_b", 1, grT, "br_b")
            pe.wait_ge(merged_ready, KT)
            token_major("out", 0, merged, "out")
            token_major("out", 1, merged, "out")
            pe.wait_ge(mod_ready, outs_before(8))
            pe.transpose(bank[5][0:2 * KT, 0:P], ns[:, :, :].rearrange("p d k -> p (d k)"), ident[:, :])\
                .then_inc(ns_mm, 1)
            pe.wait_ge(ns_ready, 1)
            ada(ADA_SHIFT2)
            pe.wait_ge(xh_ready, 2 * TILES)
            transposed("h2T")
            pe.wait_ge(wr_in, 16)
            all_emptied(WIDE["h2T"] + KT)
            for k in range(KT):
                ins = pe.matmul(bank[0][0:NE, 0:NTOK], wr[:, k, :], h2T[:, k, :], start=(k == 0), stop=(k == KT - 1))
            ins.then_inc(lg_mm, 1)
            pe.wait_ge(lg_ready, 1)
            for t in range(TILES):
                ins = pe.transpose(bank[1][:, t * NE:(t + 1) * NE], lgT[:, t * P:(t + 1) * P], ident[0:NE, 0:NE])
            ins.then_inc(lg_tok, 1)
            pe.wait_ge(aff_ready, 1)
            for t in range(TILES):
                ins = pe.transpose(bank[2][0:NE, t * P:(t + 1) * P], aff[:, t, :], ident[:, :])
            ins.then_inc(aff_mm, 1)
            pe.wait_ge(bg2_in, 16)
            for u in ADA_GATE2:
                ada_rows(u)
            pe.wait_ge(pos_ready, 1)
            for t in range(TILES):
                ins = pe.transpose(bank[1][:, t * NE:(t + 1) * NE], posT[:, t * P:(t + 1) * P], ident[0:NE, 0:NE])
            ins.then_inc(pos_mm, 1)

            def gather(par):
                for t in (1, 0, 2):
                    for hf in range(2):
                        at = 64 * hf + (SL if t == 0 else 0)
                        ins = pe.matmul(bank[6][at:at + SL, :], S[par][:, t, :], xh[:, t, hf * UW:(hf + 1) * UW],
                                        start=(t != 2), stop=(t != 1))
                ins.then_inc(gather_mm, 1)

            def gathered_t():
                for b in range(4):
                    ins = pe.transpose(bank[7][:, b * P:(b + 1) * P], xg[:, b * P:(b + 1) * P], ident[:, :])
                ins.then_inc(xgt_mm, 1)

            def combine(c):
                t, hf = c // 2, c % 2
                rows = slice(64, 128) if t == 0 else slice(0, 64)
                pe.matmul(comb_bank(c)[:, :], GT[rows, 1 if t == 2 else 0, :], o_pair[rows, hf * UW:(hf + 1) * UW],
                          start=True, stop=True).then_inc(comb_mm, 1)

            def gate_up(i, p, j):
                n = i * (2 * NJ) + (NJ * p + j)
                w = FCH[j][1]
                slots = []
                for kind in ("gate", "up"):
                    s, loads = expert_loads(i, PAIR_AT[p, kind, j])
                    pe.wait_ge(slot_in[s], loads)
                    slots.append(by_rows(s, w))
                if j == 0:
                    pe.wait_ge(xgt_ready, i * 2 + (p + 1))
                pe.wait_ge(act_done, n + 1)
                for k in range(KT):
                    for q in range(2):
                        ins = pe.matmul(bank[j % 2][64 * q:64 * q + 64, 0:w], xgT[p][:, k, :], slots[q][:, k, :],
                                        start=(k == 0), stop=(k == KT - 1))
                ins.then_inc(gu_mm, 1)

            def act_t(i, p, j):
                n = i * (2 * NJ) + (NJ * p + j)
                pe.wait_ge(act_done, n + 3)
                pe.wait_ge(actt_ready, n + 1)
                for f in range(FCH[j][1] // P):
                    ins = pe.transpose(bank[2 + j % 2][:, f * P:(f + 1) * P],
                                       sgact[j % 2][:, f * P:(f + 1) * P], ident[:, :])
                ins.then_inc(actt_mm, 1)

            def down(i, p, j):
                n = i * (2 * NJ) + (NJ * p + j)
                s, loads = expert_loads(i, PAIR_AT[p, "down", j])
                tiles = FCH[j][1] // P
                w = by_ff(s, tiles)
                pe.wait_ge(slot_in[s], loads)
                pe.wait_ge(actt_ready, n + 3)
                if j == 0:
                    pe.wait_ge(o_ready, i * 2 + (p + 1))
                for f in range(tiles):
                    for q in range(2):
                        ins = pe.matmul(bank[4 + p][64 * q:64 * q + 64, :], actT[j % 2][:, f, :],
                                        w[:, f, q * UW:(q + 1) * UW], start=(j == 0 and f == 0),
                                        stop=(j == NJ - 1 and f == tiles - 1))
                ins.then_inc(down_mm, 1)

            pe.wait_ge(s_ready, 1)
            pe.wait_ge(modp_ready, len(ADA_ORDER))
            gather(0)
            pe.wait_ge(xg_ready, 1)
            gathered_t()
            for u in ADA_GATE2:
                ada_sums(u)
            with pe.Fori(0, PAIRS) as i:
                for p in range(2):
                    e = i * 2 + p
                    for j in range(NJ):
                        gate_up(i, p, j)
                        if j >= 1:
                            act_t(i, p, j - 1)
                        if j == 1:
                            pe.wait_ge(s_ready, e + 2)
                            pe.wait_ge(xg_ready, e + 1)
                            pe.wait_ge(comb_added, i * 6 + (6 * p + 1))
                            pe.wait_ge(gt_ready, i + 1)
                            gather(1 - p)
                        if j == 2:
                            pe.wait_ge(xg_ready, e + 2)
                            pe.wait_ge(xgt_ready, e + 1)
                            gathered_t()
                        if p == 0 and j >= 3:
                            for c in range(2 * (j - 3), 2 * (j - 3) + 2):
                                if c == 0:
                                    pe.wait_ge(gt_ready, i + 1)
                                    pe.wait_ge(o_ready, e + 2)
                                    pe.wait_ge(xgt_ready, e + 2)
                                if c >= 2:
                                    pe.wait_ge(comb_added, i * 6 + c)
                                combine(c)
                        if p == 1 and j == 3:
                            pe.wait_ge(g_ready, i * 2 + 2)
                            pe.transpose(bank[6][:, 0:P], G[:, 0:2, :, :].rearrange("p b e s -> p (b e s)"), ident[:, :])
                            pe.transpose(bank[6][0:64, P:2 * P], G[:, 2, :, :].rearrange("p e s -> p (e s)"),
                                         ident[:, :]).then_inc(gt_mm, 1)
                        if j >= 1:
                            down(i, p, j - 1)
                    act_t(i, p, NJ - 1)
                    down(i, p, NJ - 1)
            pe.wait_ge(gt_ready, PAIRS + 1)
            pe.wait_ge(o_ready, NE + 2)
            pe.wait_ge(xgt_ready, NE + 1)
            for c in range(6):
                if c >= 2:
                    pe.wait_ge(comb_added, PAIRS * 6 + c)
                combine(c)


def position_table():
    import numpy as np

    rr, cc = np.meshgrid(np.arange(NLAT // GRID_W, dtype=np.float32), np.arange(GRID_W, dtype=np.float32), indexing="ij")
    quarter = D // 4
    omega = (1.0 / (10000.0 ** (np.arange(quarter, dtype=np.float32) / np.float32(quarter)))).astype(np.float32)
    r, c = rr.reshape(-1)[:, None] * omega, cc.reshape(-1)[:, None] * omega
    return np.ascontiguousarray(np.concatenate([np.sin(r), np.cos(r), np.sin(c), np.cos(c)], axis=-1), np.float32)


def kernel(x_prompt, x_sample, state_rglru, c, c_ctx, w_ada, b_ada, norm1_g, norm2_g, w_in, v_norm_g,
           w_spatial, b_spatial, conv_w, conv_b, rg_w_a, rg_b_a, rg_w_x, rg_b_x, rg_lambda,
           w_br_a, w_br_b, w_out, w_router, w_gate_e, w_up_e, w_down_e, final_norm_g):
    import concourse.bacc as bacc
    import numpy as np
    from concourse.bass_utils import run_bass_kernel_spmd

    def columns(a):
        return np.asarray(a).reshape(-1, P).T

    conditions = np.stack([np.asarray(c_ctx).reshape(KT, P), np.asarray(c).reshape(KT, P)], axis=1)
    cols = np.concatenate([columns(conditions)] + [columns(a) for a in (
        norm1_g, norm2_g, b_ada, v_norm_g, conv_w, conv_b, rg_b_a, rg_b_x, rg_lambda, state_rglru)], axis=1)
    arrays = {
        "x_prompt": np.asarray(x_prompt)[0], "x_sample": np.asarray(x_sample)[0], "emb": position_table(),
        "cols": cols, "w_ada": np.asarray(w_ada)[0], "b_ada": np.asarray(b_ada), "w_in": np.asarray(w_in)[0],
        "w_spatial_t": np.asarray(w_spatial)[0].transpose(2, 0, 1).reshape(P, D),
        "b_spatial": np.asarray(b_spatial).reshape(1, D),
        "rg_w": np.stack([np.asarray(rg_w_a)[0], np.asarray(rg_w_x)[0]]).transpose(3, 0, 1, 2, 4).reshape(P, -1),
        "w_br_a": np.asarray(w_br_a)[0], "w_br_b": np.asarray(w_br_b)[0], "w_out": np.asarray(w_out)[0],
        "w_router": np.asarray(w_router)[0].reshape(KT, P, NE).transpose(1, 0, 2).reshape(P, KT * NE),
        "w_gate": np.asarray(w_gate_e)[0], "w_up": np.asarray(w_up_e)[0], "w_down": np.asarray(w_down_e)[0],
        "final_norm_g": np.asarray(final_norm_g).reshape(1, D),
    }
    arrays = {k: np.ascontiguousarray(v) for k, v in arrays.items()}
    outs = {"y_prompt": (NCTX, D), "y_sample": (NLAT, D), "new_state": (2 * KT, P)}

    nc = bacc.Bacc("TRN2", target_bir_lowering=False, num_devices=1)
    args = {k: nc.dram_tensor(f"in_{k}", v.shape, mybir.dt.from_np(v.dtype), kind="ExternalInput").ap()
            for k, v in arrays.items()}
    args |= {k: nc.dram_tensor(f"out_{k}", shape, mybir.dt.float32, kind="ExternalOutput").ap()
             for k, shape in outs.items()}
    build(nc, **args)
    r = run_bass_kernel_spmd(nc, [{f"in_{k}": v for k, v in arrays.items()}], core_ids=[0]).results[0]
    return (r["out_y_prompt"].reshape(x_prompt.shape), r["out_y_sample"].reshape(x_sample.shape),
            r["out_new_state"].reshape(x_prompt.shape[0], 1, 2, D))
```

```python
from contextlib import ExitStack

import concourse.bass as bass
from concourse import mybir

D = 1024
P = 128
KT = D // P
TILES = 3
NCTX, NLAT = 128, 256
NTOK = NCTX + NLAT
GRID_W = 64
NE = 16
PAIRS = NE // 2
D_FF = 2816
UW = 512
FCH = [(f, min(UW, D_FF - f)) for f in range(0, D_FF, UW)]
NJ = len(FCH)
CAP_CTX, CAP_LAT = 2 * NCTX // NE, 2 * NLAT // NE
SL = 32
RG_C = 8.0
EPS = 1e-6
CONV_W = 4
SLOTS = 9
SLOT_F = KT * UW
PW = 256
PIECE_F = KT * PW
RAW, SPLIT = 4, 2

COLS, _at = {}, 0
for _name, _n in (("c", 2 * KT), ("norm1_g", KT), ("norm2_g", KT), ("b_ada", 6 * KT), ("v_norm_g", KT),
                  ("conv_w", CONV_W * KT), ("conv_b", KT), ("rg_b_a", 2 * KT), ("rg_b_x", 2 * KT),
                  ("rg_lambda", 2 * KT), ("state", 2 * KT)):
    COLS[_name] = (_at, _n)
    _at += _n
NCOLS = _at

ADA_FIRST = [2, 3, 0, 1]
ADA_GATE1, ADA_SCALE2, ADA_SHIFT2, ADA_GATE2 = [4, 5], [8, 9], [6, 7], [10, 11]
ADA_LATER = ADA_SCALE2 + ADA_SHIFT2 + ADA_GATE2 + ADA_GATE1
ADA_ORDER = ADA_FIRST + ADA_LATER
def _chan(kind, first, n=4):
    return [("chan", kind, first + g) for g in range(n)]


def _tok(kind, first):
    return [("tok", kind, first + hf, kh) for hf in range(2) for kh in range(2)]


def _ada(*us):
    return [("ada", u, h) for u in us for h in range(2)]


PIECES = _ada(*ADA_FIRST) + _chan("in", 8)
for _g in range(4):
    PIECES += _chan("in", 12 + _g, 1) + _chan("in", _g, 1)
PIECES += _tok("in", 2)
_later = iter(ADA_LATER)
for _kind, _first in (("in", 20), ("in", 16), ("br_a", 0), ("br_b", 0)):
    for _g in (0, 2):
        PIECES += _chan(_kind, _first + _g, 2) + _ada(next(_later))
PIECES += _tok("out", 0)
NPIECES = len(PIECES)
PIECE_AT = {q: n for n, q in enumerate(PIECES)}
SPLITS = [n for n, q in enumerate(PIECES) if q[0] != "ada"]
SPLIT_AT = {PIECES[n]: m for m, n in enumerate(SPLITS)}
ADA_AT = {u: n for n, u in enumerate(ADA_ORDER)}

WIDE_BANKS = 5
WIDE, _EVAC = {}, []


def _groups(name, n, engines):
    WIDE[name] = len(_EVAC)
    _EVAC.extend(engines[i % len(engines)] for i in range(n))


_groups("hT", KT, "va")
_groups("xr", KT, "a")
for _g in range(4):
    _groups(f"gr{_g}", 2, "a")
    _groups(f"u{_g}", 2, "a")
    _groups(f"rg{_g}", 8, "a")
_groups("v", 2 * TILES, "a")
_groups("glB", KT, "a")
_groups("spatial", KT, "v")
_groups("glA", KT, "a")
_groups("br_a", KT, "v")
_groups("br_b", KT, "v")
_groups("out", 2 * TILES, "v")
_groups("h2T", KT, "va")


def emptied_by(engine, n):
    return sum(e == engine for e in _EVAC[:n])


PAIR_UNITS = []
for _p in range(2):
    for _j in range(NJ):
        PAIR_UNITS += [(_p, "gate", _j), (_p, "up", _j)]
        if _j >= 1:
            PAIR_UNITS.append((_p, "down", _j - 1))
    PAIR_UNITS.append((_p, "down", NJ - 1))
UPP = len(PAIR_UNITS)
assert UPP % SLOTS == 0
PAIR_AT = {u: n for n, u in enumerate(PAIR_UNITS)}
SLOT_ORDER = [0, 1, 2, 6, 7, 8, 4, 5, 3]


def build(nc, x_prompt, x_sample, emb, cols, w_ada, b_ada, w_in, w_spatial_t, b_spatial, rg_w, w_br_a,
          w_br_b, w_out, w_router, w_gate, w_up, w_down, final_norm_g, y_prompt, y_sample, new_state):
    F32, F32R, I32 = mybir.dt.float32, mybir.dt.float32r, mybir.dt.int32
    ALU, ACT, AX = mybir.AluOpType, mybir.ActivationFunctionType, mybir.AxisListType

    ctx = ExitStack()
    with ctx:
        def sb(name, shape, dt=F32):
            return ctx.enter_context(nc.sbuf_tensor(name, shape, dt))

        def sem(name):
            return ctx.enter_context(nc.semaphore(name))

        ring_at = -(-nc.sbuf_base // 32) * 32
        W1 = KT * NTOK
        raw0 = 7 * W1
        split0 = raw0 + RAW * PIECE_F
        ring = sb("ring", [P, max(SLOTS * SLOT_F, split0 + SPLIT * 2 * PIECE_F)])
        x = sb("x", [P, TILES, D])
        xh = sb("xh", [P, TILES, D])
        work = sb("work", [P, 6656])
        col = sb("col", [P, NCOLS])
        ident = sb("ident", [P, P])
        c32 = sb("c32", [P, KT, 32])
        selb = sb("selb", [P, 2, P])
        selg = sb("selg", [P, P])
        two_ones = sb("two_ones", [1, 32])
        mod1 = sb("mod1", [P, 2, KT, 2])
        mod2 = sb("mod2", [P, 2, KT, 2])
        mod_raw = sb("mod_raw", [P, 4, 2])
        mod_sum = sb("mod_sum", [P, 4, 2])
        negsp = sb("negsp", [P, 2, KT])
        lam = sb("lam", [P, 4, 2 * KT])
        ss = sb("ss", [P, 4, 2 * TILES])
        rstd = sb("rstd", [P, 4, TILES])
        half = sb("half", [P, 1])
        tiny = sb("tiny", [P, 1])
        ns = sb("ns", [P, 2, KT])
        wr = sb("wr", [P, KT, 32])
        sel4 = sb("sel4", [P, NE])
        iota_i = sb("iota_i", [P, SL], I32)
        iota = sb("iota", [P, SL])
        posm = sb("posm", [P, TILES, NE + 1])
        aff = sb("aff", [P, TILES, NE])
        smax = sb("smax", [P, 3, TILES])

        def part(tensor, at, n):
            return tensor[:, at:at + n]

        def chan(at):
            return part(ring, at, KT * NTOK).rearrange("p (k t) -> p k t", k=KT)

        def rounded(name, at, n):
            return nc.alloc_sbuf_tensor_at(name, [P, n], F32R, offset=ring_at + 4 * at)

        area_r = {a: rounded(f"area_r{a}", a * W1, W1) for a in (0, 3, 4, 5, 6)}

        def chan_r(area):
            return area_r[area][:, :].rearrange("p (k t) -> p k t", k=KT)

        def f32(ap):
            return ap.bitcast(F32)

        hT = [chan_r(0), chan_r(4)]
        ybT = [chan_r(0), chan_r(3)]
        yaT, mT = ([chan_r(5), chan_r(6)] for _ in range(2))
        vtok = part(ring, W1, TILES * D).rearrange("p (t d) -> p t d", t=TILES)
        embt = part(ring, W1, 2 * D).rearrange("p (t d) -> p t d", t=2)
        glA = chan(W1)
        xc = glB = chan(2 * W1)
        grT = chan(3 * W1)
        g1b = part(ring, 4 * W1, 2 * D).rearrange("p (m d) -> p m d", m=2)
        b_gate1 = ring[0:1, 4 * W1 + 2 * D:4 * W1 + 3 * D]
        xr = hfull = chan(5 * W1)
        uT = chan(6 * W1)
        tmpc = xh[:, 2, :].rearrange("p (b n) -> p b n", b=2)
        rgw = [part(ring, W1 + n * D, D) for n in range(3)] + [xh[:, 2, :]]
        wsp = part(xh[:, :, :].rearrange("p t d -> p (t d)"), 0, D).rearrange("p (g q) -> p g q", g=KT)
        bsp = part(xh[:, :, :].rearrange("p t d -> p (t d)"), D, D).rearrange("p (g q) -> p g q", g=KT)
        gfin = xh[:, 0, :]
        junk_f = xh[:, 1, :]

        split_r = [[rounded(f"split{n}_{h}", split0 + (2 * n + h) * PIECE_F, PIECE_F) for h in range(2)]
                   for n in range(SPLIT)]

        def piece(tensor, at, q):
            width = UW if q[0] == "tok" else PW
            return part(tensor, at, PIECE_F).rearrange("p (k n) -> p k n", n=width)

        def raw_piece(n):
            return piece(ring, raw0 + n % RAW * PIECE_F, PIECES[n])

        def split_piece(m):
            return [piece(tensor, 0, PIECES[SPLITS[m]]) for tensor in split_r[m % SPLIT]]

        def by_rows(s, width):
            return part(ring, s * SLOT_F, KT * width).rearrange("p (k n) -> p k n", k=KT)

        def by_ff(s, tiles):
            return part(ring, s * SLOT_F, tiles * D).rearrange("p (t n) -> p t n", t=tiles)

        HB = 2 * NTOK
        rbuf = [part(work, n * HB, HB).rearrange("p (d t) -> p d t", d=2) for n in range(2)]
        gibuf = [part(work, (2 + n) * HB, HB).rearrange("p (d t) -> p d t", d=2) for n in range(2)]
        ab = [part(work, (4 + n) * HB, HB).rearrange("p (d t) -> p d t", d=2) for n in range(2)]
        asq = part(work, 6 * HB, HB).rearrange("p (d t) -> p d t", d=2)
        hs = part(work, 7 * HB, HB).rearrange("p (d t) -> p d t", d=2)
        junk_v = junk_x = part(work, 4 * HB, D)
        junk_h = part(work, 4 * HB + D, UW)
        def modp(q):
            return part(work, 4 * HB + D + (q % 2) * UW, UW)

        tmpo = part(work, 4 * HB, 2 * UW).rearrange("p (b n) -> p b n", b=2)
        g2s = part(work, 6144, UW)
        h2T = part(work, 0, KT * NTOK).rearrange("p (k t) -> p k t", k=KT)
        lgT = part(work, 3072, NTOK)
        affT = work[0:NE, 3456:3456 + NTOK]
        posT = work[0:NE, 3840:3840 + NTOK]
        onesT = work[0:NE, 4224:4224 + NTOK]
        top8 = work[0:NE, 4608:4608 + 48].rearrange("p (r n) -> p r n", n=8)
        exl = part(work, 4672, TILES * NE).rearrange("p (t e) -> p t e", t=TILES)
        maskT = work[0:NE, 4736:4736 + NTOK]
        xg = part(work, 0, UW)
        xgT = [part(work, UW * (1 + n), UW).rearrange("p (k s) -> p k s", k=KT) for n in range(2)]
        sgact = [part(work, UW * (3 + n), UW) for n in range(2)]
        actT = [part(work, 2560 + 256 * n, 256).rearrange("p (f s) -> p f s", f=4) for n in range(2)]
        o_pair = part(work, 3072, D)
        GT = part(work, 4096, TILES * P).rearrange("p (b t) -> p b t", b=TILES)
        S = [part(work, 5120 + 96 * n, 96).rearrange("p (t s) -> p t s", t=TILES) for n in range(2)]
        G = part(work, 5312, 192).rearrange("p (b e s) -> p b e s", b=3, e=2)
        b_gate2 = work[0:1, 5120:5120 + D]
        ns_t = work[0:2 * KT, 5504:5504 + P]

        bank = [ctx.enter_context(nc.psum_tensor(f"bank{n}", [P, 512], F32)) for n in range(8)]

        rg_in, bg2_in = sem("rg_in"), sem("bg2_in")
        x_in, emb_in, col_in, wr_in = sem("x_in"), sem("emb_in"), sem("col_in"), sem("wr_in")
        sp_in, bg_in, gf_in = sem("sp_in"), sem("bg_in"), sem("gf_in")
        slot_in = [sem(f"slot_in{s}") for s in range(SLOTS)]
        raw_in = [sem(f"raw_in{s}") for s in range(RAW)]
        piece_hi, piece_lo = sem("piece_hi"), {"v": sem("piece_lo_v"), "p": sem("piece_lo_p")}
        half_mm = sem("half_mm")
        hi_ready = {k: sem(f"{k}_hi") for k in ("hT", "yaT", "ybT", "mT")}
        lo_ready = {k: sem(f"{k}_lo") for k in ("hT", "yaT", "ybT", "mT")}
        consts = sem("consts")
        c32_ready = sem("c32_ready")
        link_v, link_p, link_a = sem("link_v"), sem("link_p"), sem("link_a")
        ms_ready, rstd_ready = sem("ms_ready"), sem("rstd_ready")
        xh_ready = sem("xh_ready")
        ada_half = sem("ada_half")
        ada_mm, modp_ready, ada_out, mod_ready = sem("ada_mm"), sem("modp_ready"), sem("ada_out"), sem("mod_ready")
        wide_mm = sem("wide_mm")
        emptied = {"v": sem("emptied_v"), "a": sem("emptied_a")}
        lam_exp, lam_one, lam_ln, lam_ready = sem("lam_exp"), sem("lam_one"), sem("lam_ln"), sem("lam_ready")
        exp_done = sem("exp_done")
        conv_done, tanh_done, om_ready, sqrt_done = sem("conv_done"), sem("tanh_done"), sem("om_ready"), sem("sqrt_done")
        gx_done, scan_done, yb_done = sem("gx_done"), sem("scan_done"), sem("yb_done")
        v_ready, ya_ready, merged_ready, x1_ready = sem("v_ready"), sem("ya_ready"), sem("merged_ready"), sem("x1_ready")
        ns_mm, ns_ready, out_done = sem("ns_mm"), sem("ns_ready"), sem("out_done")
        sq_done = sem("sq_done")
        lg_mm, lg_ready, lg_tok, sub_ready, exp_ready = (sem(n) for n in ("lg_mm", "lg_ready", "lg_tok", "sub_ready", "exp_ready"))
        aff_ready, aff_mm, pos_ready, pos_mm = (sem(n) for n in ("aff_ready", "aff_mm", "pos_ready", "pos_mm"))
        s_ready, gather_mm, xg_ready, xgt_mm, xgt_ready = (sem(n) for n in ("s_ready", "gather_mm", "xg_ready", "xgt_mm", "xgt_ready"))
        xgt_scaled = sem("xgt_scaled")
        gu_mm, silu_done, act_done, actt_mm, actt_ready = (sem(n) for n in ("gu_mm", "silu_done", "act_done", "actt_mm", "actt_ready"))
        down_mm, o_ready, g_ready, gt_mm, gt_ready = (sem(n) for n in ("down_mm", "o_ready", "g_ready", "gt_mm", "gt_ready"))
        comb_mm, comb_added, y_ready = sem("comb_mm"), sem("comb_added"), sem("y_ready")

        def vcol(name, *shape):
            at, n = COLS[name]
            v = col[:, at:at + n]
            if len(shape) == 2:
                v = v.rearrange("p (a b) -> p a b", a=shape[0])
            return v

        cw, cb = vcol("conv_w", CONV_W, KT), vcol("conv_b")
        st0 = vcol("state", 2, KT)

        LO_BY_V = (15,)

        def split_done(m):
            by_v = sum(n <= m for n in LO_BY_V)
            return (piece_lo["v"], by_v) if m in LO_BY_V else (piece_lo["p"], m + 1 - by_v)

        def raw_loaded(n):
            return raw_in[n % RAW], 16 * (n // RAW + 1)

        def expert_loads(i, u):
            s = SLOT_ORDER[u % SLOTS]
            return s, 16 * (u // SLOTS + 1) + i * (16 * (UPP // SLOTS))

        CHAN_AT = {("in", 12 + g): (f"gr{g}", 0) for g in range(4)} | {("in", g): (f"u{g}", 0) for g in range(4)}
        CHAN_AT |= {("in", 8 + g): ("xr", 2 * g) for g in range(4)}
        CHAN_AT |= {("in", 16 + g): ("glA", 2 * g) for g in range(4)} | {("in", 20 + g): ("glB", 2 * g) for g in range(4)}
        CHAN_AT |= {(k, g): (k, 2 * g) for k in ("br_a", "br_b") for g in range(4)}

        def groups_of(q):
            if q[0] == "tok":
                return WIDE["v" if q[1] == "in" else "out"] + TILES * (q[2] % 2)
            name, at = CHAN_AT[q[1], q[2]]
            return WIDE[name] + at

        def piece_mm(n):
            q = PIECES[n]
            if q[0] == "ada":
                return (ada_mm if q[2] else ada_half), ADA_AT[q[1]] + 1
            if q[0] == "tok" and q[3] == 0:
                return half_mm, sum(p[0] == "tok" and p[3] == 0 for p in PIECES[:n]) + 1
            return wide_mm, groups_of(q) + (TILES if q[0] == "tok" else 2)

        def raw_used(n):
            return piece_mm(n) if PIECES[n][0] == "ada" else split_done(SPLITS.index(n))

        def pair_used(i, u):
            p, kind, j = PAIR_UNITS[u]
            return (down_mm, i * (2 * NJ) + (NJ * p + j + 3)) if kind == "down" else (gu_mm, i * (2 * NJ) + (NJ * p + j + 1))

        def outs_before(q):
            return sum(2 if u // 2 == 2 else 1 for u in ADA_ORDER[:q])

        def comb_bank(c):
            return bank[6 + c % 2]

        SETS = ((0, 0, NCTX), (1, NCTX, NTOK))

        block = ctx.enter_context(nc.Block())

        @block.sync
        def _(sp):
            sources = {
                "ada": w_ada, "in": w_in, "br_a": w_br_a, "br_b": w_br_b, "out": w_out}
            sp.dma_start(x[:, 0, :], x_prompt).then_inc(x_in, 16)
            sp.dma_start(x[:, 1:3, :], x_sample.rearrange("(t p) d -> p t d", p=P)).then_inc(x_in, 16)
            sp.dma_start(embt, emb.rearrange("(t p) d -> p t d", p=P)).then_inc(emb_in, 16)
            def load_piece(n):
                if n >= RAW:
                    sp.wait_ge(*raw_used(n - RAW))
                q = PIECES[n]
                if q[0] == "tok":
                    rows, cols_ = slice(q[3] * 4 * P, (q[3] + 1) * 4 * P), slice(q[2] * UW, (q[2] + 1) * UW)
                elif q[0] == "chan":
                    rows, cols_ = slice(0, D), slice(q[2] * PW, (q[2] + 1) * PW)
                else:
                    rows, cols_ = slice(0, D), slice((2 * q[1] + q[2]) * PW, (2 * q[1] + q[2] + 1) * PW)
                src = sources["ada" if q[0] == "ada" else q[1]][rows, cols_].rearrange("(k p) n -> p k n", p=P)
                sp.dma_start(raw_piece(n), src).then_inc(raw_in[n % RAW], 16)

            for n in range(NPIECES):
                load_piece(n)

            def load(i, u, e):
                _, kind, j = PAIR_UNITS[u]
                f, w = FCH[j]
                s, _ = expert_loads(i, u)
                if kind == "down":
                    dst = by_ff(s, w // P)
                    src = w_down[bass.ds(e, 1), f:f + w, :].rearrange("e (t p) n -> p (e t) n", p=P)
                else:
                    dst = by_rows(s, w)
                    src = (w_gate if kind == "gate" else w_up)[bass.ds(e, 1), :, f:f + w]
                    src = src.rearrange("e (k p) n -> p (e k) n", p=P)
                sp.dma_start(dst, src).then_inc(slot_in[s], 16)

            def used(*q):
                return piece_mm(PIECE_AT[q])

            out_done_mm = used("tok", "out", 1, 1)
            x1_done = (emptied["v"], emptied_by("v", WIDE["out"] + 2 * TILES))
            dead = [
                (lo_ready["mT"], KT),
                (lo_ready["mT"], KT),
                (lo_ready["mT"], KT),
                split_done(len(SPLITS) - 1),
                used("tok", "out", 1, 0),
                out_done_mm,
                out_done_mm,
                out_done_mm,
                x1_done,
            ]
            for n in range(SLOTS):
                sp.wait_ge(*dead[n])
                load(0, n, PAIR_UNITS[n][0])

            def ahead(i, u):
                sp.wait_ge(*pair_used(i, u - SLOTS))
                nxt, v = divmod(u, UPP)
                load(i, v, i * 2 + (2 * nxt + PAIR_UNITS[v][0]))

            with sp.Fori(0, PAIRS - 1) as i:
                for u in range(SLOTS, UPP + SLOTS):
                    ahead(i, u)
            for u in range(SLOTS, UPP):
                ahead(PAIRS - 1, u)

            for t in range(TILES):
                sp.wait_ge(y_ready, t + 1)
                dst = y_prompt if t == 0 else y_sample[(t - 1) * P:t * P, :]
                sp.dma_start(dst, x[:, t, :]).then_inc(out_done, 16)
            sp.wait_ge(out_done, 16 * (TILES + 1))

        @block.gpsimd
        def _(pool):
            count = [0]

            def link(ins):
                count[0] += 1
                ins.then_inc(link_p, 1)
                pool.wait_ge(link_p, count[0])

            link(pool.memset(c32[:, :, :], 0.0))
            pool.memset(half[:, :], -0.5)
            link(pool.memset(two_ones[:, :], 0.0))
            pool.memset(two_ones[:, 0:2], 1.0)
            pool.memset(posm[:, :, :], 0.0)
            pool.memset(selb[:, :, :], 0.0)
            link(pool.memset(ident[:, :], 0.0))
            for j in range(4):
                link(pool.affine_select(out=selb[:, :, :], in_=selb[:, :, :], compare_op=ALU.not_equal, fill=1.0,
                                        base=-32 * j, pattern=[[-1, 2], [0, P]], channel_multiplier=1))
            link(pool.affine_select(out=ident[:, :], in_=ident[:, :], compare_op=ALU.not_equal, fill=1.0,
                                    base=0, pattern=[[-1, P]], channel_multiplier=1))
            sg = selg[:, :].rearrange("p (h m s) -> p h m s", h=2, m=2)
            for m in range(2):
                sv = selb[:, 1 - m, 0:64].rearrange("p (h s) -> p h s", h=2)
                pool.tensor_copy(sg[:, :, m, :], sv)
            pool.memset(wr[:, :, NE:32], 0.0)
            link(pool.memset(sel4[:, :], 0.0))
            for j in range(4):
                link(pool.affine_select(out=sel4[:, :], in_=sel4[:, :], compare_op=ALU.not_equal, fill=1.0,
                                        base=-32 * j, pattern=[[-1, NE]], channel_multiplier=1))
            link(pool.iota(iota_i[:, :], pattern=[[1, SL]], base=1, channel_multiplier=0))
            pool.tensor_copy(iota[:, :], iota_i[:, :]).then_inc(consts, 1)

            def power(n):
                pool.wait_ge(ms_ready, n + 1)
                pool.tensor_tensor(rstd[:, n, :], ss[:, n, 0:TILES], half[:, 0:1].to_broadcast([P, TILES]),
                                   ALU.pow).then_inc(rstd_ready, 1)

            def low_part(m):
                hi, lo = split_piece(m)
                pool.wait_ge(piece_hi, m + 1)
                pool.tensor_tensor(lo, raw_piece(SPLITS[m]), f32(hi), ALU.subtract).then_inc(piece_lo["p"], 1)

            def gates_times_x(h):
                pool.wait_ge(emptied["a"], emptied_by("a", WIDE[f"rg{h // 2}"] + 4 * (h % 2) + 4))
                pool.wait_ge(conv_done, h + 1)
                g = gibuf[h % 2]
                pool.tensor_tensor(g, g, xc[:, h, :].unsqueeze(1).to_broadcast([P, 2, NTOK]),
                                   ALU.mult).then_inc(gx_done, 1)

            def states_times_gr(h):
                pool.wait_ge(scan_done, h + 1)
                pool.wait_ge(emptied["a"], emptied_by("a", WIDE[f"gr{h // 2}"] + h % 2 + 1))
                link(pool.tensor_copy(ns[:, 0, h:h + 1], hs[:, 0, NCTX - 1:NCTX]))
                link(pool.tensor_copy(ns[:, 1, h:h + 1], hs[:, 1, 0:1]))
                link(pool.tensor_tensor(hs[:, 0, :], hs[:, 0, :], hs[:, 1, :], ALU.add))
                pool.tensor_tensor(grT[:, h, :], grT[:, h, :], hs[:, 0, :], ALU.mult).then_inc(yb_done, 1)

            power(0)
            for m in range(6):
                low_part(m)
            for g in range(4):
                low_part(6 + 2 * g)
                if g >= 1:
                    states_times_gr(2 * g - 2)
                    states_times_gr(2 * g - 1)
                low_part(7 + 2 * g)
                gates_times_x(2 * g)
                gates_times_x(2 * g + 1)
            low_part(14)
            states_times_gr(KT - 2)
            states_times_gr(KT - 1)
            for m in range(16, 18):
                low_part(m)
            power(1)
            for m in range(18, len(SPLITS)):
                low_part(m)
            power(2)
            for t in range(TILES):
                pool.wait_ge(ms_ready, 4 + t)
                pool.tensor_tensor(rstd[:, 3, t:t + 1], ss[:, 3, t:t + 1], half[:, 0:1], ALU.pow).then_inc(rstd_ready, 1)

        @block.scalar
        def _(act):
            act.dma_start(col[:, :], cols).then_inc(col_in, 16)
            act.dma_start(wr[:, :, 0:NE], w_router.rearrange("p (k e) -> p k e", k=KT)).then_inc(wr_in, 16)
            act.wait_ge(col_in, 16)
            act.wait_ge(link_p, 1)
            act.activation(c32[:, :, 0:2], vcol("c", KT, 2), ACT.Silu).then_inc(c32_ready, 1)
            act.wait_ge(lam_one, 1)
            act.activation(lam[:, 1, :], lam[:, 0, :], ACT.Exp, scale=-1.0).then_inc(lam_exp, 1)
            act.wait_ge(lam_one, 2)
            act.activation(lam[:, 3, :], lam[:, 2, :], ACT.Ln).then_inc(lam_ln, 1)

            def take(n, out, src, func, **kw):
                act.wait_ge(wide_mm, n + 1)
                return act.activation(out, src, func, **kw).then_inc(emptied["a"], 1)

            def modulated(k, name, out, mod):
                n = WIDE[name] + k
                act.wait_ge(wide_mm, n + 1)
                for m, a, b in SETS:
                    ins = act.activation(out[:, k, a:b], bank[n % WIDE_BANKS][:, a:b], ACT.Identity,
                                         scale=mod[:, 0, k, m:m + 1], bias=mod[:, 1, k, m:m + 1])
                ins.then_inc(emptied["a"], 1)

            def high_part(m):
                act.wait_ge(*raw_loaded(SPLITS[m]))
                if m >= SPLIT:
                    act.wait_ge(*piece_mm(SPLITS[m - SPLIT]))
                act.activation(split_piece(m)[0], raw_piece(SPLITS[m]), ACT.Copy).then_inc(piece_hi, 1)

            def high(name, parts, src, k):
                act.activation(parts[0][:, k, :], src[:, k, :], ACT.Copy).then_inc(hi_ready[name], 1)

            high_part(0)
            act.wait_ge(mod_ready, 4)
            for k in range(0, KT, 2):
                modulated(k + 1, "hT", hfull, mod1)
                act.wait_ge(emptied["v"], k // 2 + 1)
                high("hT", hT, hfull, k)
                act.wait_ge(emptied["a"], k // 2 + 1)
                high("hT", hT, hfull, k + 1)
            high_part(1)
            act.wait_ge(wide_mm, WIDE["hT"] + KT)
            act.dma_start(wsp, w_spatial_t.rearrange("q (g p) -> q g p", g=KT)).then_inc(sp_in, 16)
            act.dma_start(bsp, b_spatial.to_broadcast([P, D]).rearrange("q (g p) -> q g p", g=KT)).then_inc(sp_in, 16)
            for n in range(4):
                act.dma_start(rgw[n], rg_w[:, n * D:(n + 1) * D]).then_inc(rg_in, 16)

            def take_two(q, out, at, func):
                for b in range(2):
                    n = groups_of(q) + b
                    take(n, out[:, at + b, :], bank[n % WIDE_BANKS][:, 0:NTOK], func)
                high_part(SPLIT_AT[q] + SPLIT)

            act.wait_ge(lo_ready["hT"], KT)
            for g in range(4):
                take_two(("chan", "in", 8 + g), xr, 2 * g, ACT.Copy)

            def root(h):
                act.wait_ge(om_ready, h + 1)
                t2 = rbuf[h % 2]
                act.activation(t2, t2, ACT.Sqrt, scale=-1.0, bias=tiny[:, 0:1]).then_inc(sqrt_done, 1)

            act.wait_ge(lam_ready, 1)
            for g in range(4):
                take_two(("chan", "in", 12 + g), grT, 2 * g, ACT.Gelu_apprx_tanh)
                take_two(("chan", "in", g), uT, 2 * g, ACT.Gelu_apprx_tanh)
                if g >= 1:
                    act.wait_ge(scan_done, 2 * g)
                for b in range(2 * g, 2 * g + 2):
                    for q in range(4):
                        n = WIDE[f"rg{g}"] + 4 * (b % 2) + q
                        d, buf, bias = q % 2, (rbuf, gibuf)[q // 2][b % 2], vcol(("rg_b_a", "rg_b_x")[q // 2], 2, KT)
                        take(n, buf[:, d, :], bank[n % WIDE_BANKS][:, 0:NTOK], ACT.Sigmoid, bias=bias[:, d, b:b + 1])
                act.wait_ge(emptied["a"], emptied_by("a", WIDE[f"rg{g}"] + 8))
                for b in range(2 * g, 2 * g + 2):
                    for d in range(2):
                        act.activation(ab[b % 2][:, d, :], rbuf[b % 2][:, d, :], ACT.Exp,
                                       scale=negsp[:, d, b:b + 1]).then_inc(exp_done, 1)
                act.wait_ge(exp_done, 4 * (g + 1))
                for b in range(2 * g, 2 * g + 2):
                    for d in range(2):
                        act.activation(rbuf[b % 2][:, d, :], rbuf[b % 2][:, d, :], ACT.Tanh,
                                       scale=negsp[:, d, b:b + 1]).then_inc(tanh_done, 1)
                root(2 * g)
                root(2 * g + 1)
            for hf in range(2):
                high_part(14 + 2 * hf)
                for t in range(TILES):
                    n = WIDE["v"] + TILES * hf + t
                    take(n, vtok[:, t, hf * UW:(hf + 1) * UW], bank[n % WIDE_BANKS][:, :], ACT.Gelu_apprx_tanh)
                high_part(15 + 2 * hf)
            act.wait_ge(gx_done, KT)
            for g in range(4):
                take_two(("chan", "in", 20 + g), glB, 2 * g, ACT.Sigmoid)
            for k in range(KT):
                act.wait_ge(ya_ready, k + 1)
                high("yaT", yaT, uT, k)
            act.wait_ge(yb_done, KT)
            act.dma_start(b_gate2, b_ada[:, 5 * D:6 * D]).then_inc(bg2_in, 16)
            for g in range(4):
                take_two(("chan", "in", 16 + g), glA, 2 * g, ACT.Sigmoid)
            act.dma_start(b_gate1, b_ada[:, 2 * D:3 * D]).then_inc(bg_in, 16)
            for k in range(KT):
                high("ybT", ybT, grT, k)
            first_b = SPLIT_AT["chan", "br_b", 0]
            for m in range(first_b - 2, first_b + SPLIT):
                high_part(m)
            for k in range(KT):
                act.wait_ge(merged_ready, k + 1)
                high("mT", mT, glA, k)
                if k % 2 == 1:
                    high_part(first_b + SPLIT + k // 2)
            for m in range(first_b + SPLIT + 4, len(SPLITS)):
                high_part(m)
            act.wait_ge(mod_ready, outs_before(8))
            act.wait_ge(ns_ready, 1)
            act.dma_start(new_state, ns_t).then_inc(out_done, 16)
            for k in range(1, KT, 2):
                modulated(k, "h2T", h2T, mod2)
            act.wait_ge(sub_ready, 1)
            act.activation(exl, exl, ACT.Exp).then_inc(exp_ready, 1)

            with act.Fori(0, PAIRS) as i:
                for p in range(2):
                    for j, (_, w) in enumerate(FCH):
                        act.wait_ge(gu_mm, i * (2 * NJ) + (NJ * p + j + 1))
                        act.activation(sgact[j % 2][0:64, 0:w], bank[j % 2][0:64, 0:w],
                                       ACT.Silu).then_inc(silu_done, 1)
            act.wait_ge(gather_mm, NE + 1)
            act.dma_start(gfin, final_norm_g.to_broadcast([P, D])).then_inc(gf_in, 16)
            for t in range(TILES):
                act.wait_ge(comb_added, PAIRS * 6 + 2 * t + 3)
                if t >= 1:
                    act.wait_ge(sq_done, t)
                act.activation(junk_f, x[:, t, :], ACT.Square, accum_out=ss[:, 3, t:t + 1]).then_inc(sq_done, 1)

        @block.vector
        def _(dve):
            count = [0]

            def link(ins):
                count[0] += 1
                ins.then_inc(link_v, 1)
                dve.wait_ge(link_v, count[0])

            dve.memset(tiny[:, :], 1e-30)
            dve.wait_ge(col_in, 16)
            L = vcol("rg_lambda")
            link(dve.tensor_scalar(lam[:, 1, :], L, -1.0, None, ALU.mult))
            dve.tensor_tensor(lam[:, 0, :], L, lam[:, 1, :], ALU.max).then_inc(lam_one, 1)
            dve.wait_ge(lam_exp, 1)
            dve.tensor_scalar(lam[:, 2, :], lam[:, 1, :], 1.0, None, ALU.add).then_inc(lam_one, 1)
            dve.wait_ge(lam_ln, 1)
            link(dve.tensor_scalar(lam[:, 2, :], lam[:, 2, :], -1.0, None, ALU.add))
            link(dve.tensor_scalar(lam[:, 0, :], lam[:, 2, :], 0.0, None, ALU.is_equal))
            dve.tensor_tensor(lam[:, 2, :], lam[:, 2, :], lam[:, 0, :], ALU.add)
            link(dve.tensor_tensor(lam[:, 3, :], lam[:, 3, :], lam[:, 0, :], ALU.add))
            link(dve.reciprocal(lam[:, 2, :], lam[:, 2, :]))
            link(dve.tensor_tensor(lam[:, 3, :], lam[:, 3, :], lam[:, 2, :], ALU.mult))
            link(dve.tensor_tensor(lam[:, 3, :], lam[:, 3, :], lam[:, 1, :], ALU.mult))
            link(dve.tensor_scalar(lam[:, 2, :], L, -1.0, 0.0, ALU.mult, ALU.max))
            link(dve.tensor_tensor(lam[:, 3, :], lam[:, 3, :], lam[:, 2, :], ALU.add))
            dve.tensor_scalar(negsp[:, :, :].rearrange("p d k -> p (d k)"), lam[:, 3, :], -RG_C, None,
                              ALU.mult).then_inc(lam_ready, 1)

            dve.wait_ge(emb_in, 16)
            dve.wait_ge(x_in, 32)
            link(dve.tensor_tensor(x[:, 1:3, :], x[:, 1:3, :], embt, ALU.add))

            def mean_square(n, sums=1):
                if sums == 2:
                    link(dve.tensor_tensor(ss[:, n, 0:TILES], ss[:, n, 0:TILES], ss[:, n, TILES:2 * TILES], ALU.add))
                dve.tensor_scalar(ss[:, n, 0:TILES], ss[:, n, 0:TILES], 1.0 / D, EPS, ALU.mult,
                                  ALU.add).then_inc(ms_ready, 1)
                dve.wait_ge(rstd_ready, n + 1)

            def squares(n, t, src, junk):
                link(dve.tensor_tensor_reduce(out=junk, in0=src, in1=src, scale=1.0, scalar=0.0, op0=ALU.mult,
                                              op1=ALU.add, accum_out=ss[:, n, t:t + 1]))

            def normed(n, out, src, signal):
                for t in range(TILES):
                    dve.tensor_scalar(out[:, t, :], src[:, t, :], rstd[:, n, t:t + 1], None,
                                      ALU.mult).then_inc(signal, 1)

            for t in range(TILES):
                squares(0, t, x[:, t, :], junk_x)
            mean_square(0)
            normed(0, xh, x, xh_ready)

            def ada(u):
                ada_rows(u)
                ada_result(u)

            def ada_rows(u):
                q = ADA_AT[u]
                dve.wait_ge(ada_mm, q + 1)
                if q >= 2:
                    dve.wait_ge(ada_out, outs_before(q - 1))
                dve.tensor_copy(modp(q), bank[6 + q % 2][:, :]).then_inc(modp_ready, 1)

            def ada_result(u):
                q, kind, hf = ADA_AT[u], u // 2, u % 2
                base = outs_before(q)
                if kind in (2, 5):
                    for m in range(2 if kind == 2 else 1):
                        dve.wait_ge(ada_out, base + m + 1)
                        if kind == 2:
                            dve.tensor_copy(g1b[:, m, hf * UW:(hf + 1) * UW], bank[5][:, :]).then_inc(mod_ready, 1)
                        else:
                            rows = slice(64 * hf, 64 * hf + 64)
                            dve.tensor_copy(g2s[rows, :], bank[5][rows, :]).then_inc(mod_ready, 1)
                    return
                dve.wait_ge(ada_out, base + 1)
                ks = slice(4 * hf, 4 * hf + 4)
                rows = bank[5][:, :].rearrange("p (k j c) -> p k c j", k=4, j=4)[:, :, 0:2, :]
                got = mod_sum[:, :, :]
                link(dve.tensor_reduce(got, rows, AX.X, ALU.add))
                bias = vcol("b_ada", 6, KT)[:, kind, ks].unsqueeze(2).to_broadcast([P, 4, 2])
                mod, gain = (mod1, vcol("norm1_g")) if kind < 2 else (mod2, vcol("norm2_g"))
                if kind in (0, 3):
                    dve.tensor_tensor(mod[:, 1, ks, :], got, bias, ALU.add).then_inc(mod_ready, 1)
                else:
                    link(dve.tensor_tensor(mod_raw[:, :, :], got, bias, ALU.add))
                    dve.scalar_tensor_tensor(out=mod[:, 0, ks, :], in0=mod_raw[:, :, :], scalar=1.0,
                                             in1=gain[:, ks].unsqueeze(2).to_broadcast([P, 4, 2]), op0=ALU.add,
                                             op1=ALU.mult).then_inc(mod_ready, 1)

            def modulated(k, name, out, mod):
                n = WIDE[name] + k
                dve.wait_ge(wide_mm, n + 1)
                for m, a, b in SETS:
                    ins = dve.tensor_scalar(out[:, k, a:b], bank[n % WIDE_BANKS][:, a:b],
                                            mod[:, 0, k, m:m + 1], mod[:, 1, k, m:m + 1], ALU.mult, ALU.add)
                ins.then_inc(emptied["v"], 1)

            def low(name, parts, src, k):
                dve.wait_ge(hi_ready[name], k + 1)
                dve.tensor_tensor(parts[1][:, k, :], src[:, k, :], f32(parts[0][:, k, :]),
                                  ALU.subtract).then_inc(lo_ready[name], 1)

            for u in ADA_FIRST:
                ada(u)
            dve.wait_ge(mod_ready, 4)
            for k in range(0, KT, 2):
                modulated(k, "hT", hfull, mod1)
                if k >= 2:
                    low("hT", hT, hfull, k - 2)
                    low("hT", hT, hfull, k - 1)
            low("hT", hT, hfull, KT - 2)
            low("hT", hT, hfull, KT - 1)

            for h in range(KT):
                dve.wait_ge(emptied["a"], emptied_by("a", WIDE["xr"] + h + 1))
                link(dve.tensor_scalar(xc[:, h, :], xr[:, h, :], cw[:, 2, h:h + 1], cb[:, h:h + 1], ALU.mult, ALU.add))
                for k in (0, 1, 3):
                    s = k - 2
                    for _, a, b in SETS:
                        lo, hi = max(a, a - s), min(b, b - s)
                        ins = dve.scalar_tensor_tensor(out=xc[:, h, lo:hi], in0=xr[:, h, lo + s:hi + s],
                                                       scalar=cw[:, k, h:h + 1], in1=xc[:, h, lo:hi],
                                                       op0=ALU.mult, op1=ALU.add)
                        if k == 3 and a:
                            ins.then_inc(conv_done, 1)
                        elif a:
                            link(ins)

            def decay(h):
                a_, t2 = ab[h % 2], rbuf[h % 2]
                dve.wait_ge(tanh_done, 2 * h + 2)
                if h >= 1:
                    dve.wait_ge(om_ready, h)
                link(dve.tensor_tensor(asq, a_, a_, ALU.mult))
                dve.scalar_tensor_tensor(out=t2, in0=asq, scalar=1.0, in1=t2, op0=ALU.add, op1=ALU.mult)\
                    .then_inc(om_ready, 1)

            def scans(h):
                a_, o = ab[h % 2], rbuf[h % 2]
                dve.wait_ge(sqrt_done, h + 1)
                dve.wait_ge(gx_done, h + 1)
                link(dve.tensor_tensor(o, o, gibuf[h % 2], ALU.mult))
                if h >= 1:
                    dve.wait_ge(yb_done, h)
                for m, a, b in SETS:
                    start = [0.0, 0.0] if m == 0 else [st0[:, d, h:h + 1] for d in range(2)]
                    dve.tensor_tensor_scan(hs[:, 0, a:b], a_[:, 0, a:b], o[:, 0, a:b], start[0], ALU.mult, ALU.add)
                    ins = dve.tensor_tensor_scan(hs[:, 1, a:b][:, ::-1], a_[:, 1, a:b][:, ::-1],
                                                 o[:, 1, a:b][:, ::-1], start[1], ALU.mult, ALU.add)
                ins.then_inc(scan_done, 1)

            for h in range(0, KT, 2):
                decay(h)
                decay(h + 1)
                scans(h)
                scans(h + 1)
            for m in LO_BY_V:
                hi, lo = split_piece(m)
                dve.wait_ge(piece_hi, m + 1)
                dve.tensor_tensor(lo, raw_piece(SPLITS[m]), f32(hi), ALU.subtract).then_inc(piece_lo["v"], 1)

            dve.wait_ge(emptied["a"], emptied_by("a", WIDE["v"] + 2 * TILES))
            for t in range(TILES):
                squares(1, t, vtok[:, t, :], junk_v)
            mean_square(1)
            normed(1, vtok, vtok, v_ready)
            dve.wait_ge(sp_in, 32)

            def three(ap):
                return ap.rearrange("p (t q) -> p t q", t=TILES)

            U = ADA_LATER
            ada_rows(U[0])
            ada_result(U[0])
            ada_rows(U[1])
            for g in range(KT):
                n = WIDE["spatial"] + g
                tmp = tmpc[:, g % 2, 0:NTOK]
                dve.wait_ge(wide_mm, n + 1)
                dve.scalar_tensor_tensor(out=three(tmp), in0=three(bank[n % WIDE_BANKS][:, 0:NTOK]),
                                         scalar=vcol("v_norm_g")[:, g:g + 1],
                                         in1=bsp[:, g, :].unsqueeze(1).to_broadcast([P, TILES, P]),
                                         op0=ALU.mult, op1=ALU.add).then_inc(emptied["v"], 1)
                dve.wait_ge(emptied["v"], emptied_by("v", n + 1))
                dve.wait_ge(emptied["a"], emptied_by("a", WIDE[f"u{g // 2}"] + g % 2 + 1))
                dve.tensor_tensor(uT[:, g, :], uT[:, g, :], tmp, ALU.mult).then_inc(ya_ready, 1)
            ada_result(U[1])
            for k in range(KT):
                low("yaT", yaT, uT, k)
            ada_rows(U[2])
            ada_result(U[2])
            ada_rows(U[3])

            def gated_a(b):
                n = WIDE["br_a"] + b
                dve.wait_ge(wide_mm, n + 1)
                dve.wait_ge(emptied["a"], emptied_by("a", WIDE["glA"] + b + 1))
                dve.tensor_tensor(glA[:, b, :], glA[:, b, :], bank[n % WIDE_BANKS][:, 0:NTOK],
                                  ALU.mult).then_inc(emptied["v"], 1)

            def gated_b(b):
                n = WIDE["br_b"] + b
                tmp = tmpc[:, b % 2, 0:NTOK]
                dve.wait_ge(wide_mm, n + 1)
                dve.wait_ge(emptied["a"], emptied_by("a", WIDE["glB"] + b + 1))
                dve.tensor_tensor(tmp, glB[:, b, :], bank[n % WIDE_BANKS][:, 0:NTOK],
                                  ALU.mult).then_inc(emptied["v"], 1)
                dve.wait_ge(emptied["v"], emptied_by("v", n + 1))
                dve.tensor_tensor(glA[:, b, :], glA[:, b, :], tmp, ALU.add).then_inc(merged_ready, 1)
                if b >= 1:
                    low("mT", mT, glA, b - 1)

            gated_a(0)
            gated_a(1)
            ada_result(U[3])
            gated_a(2)
            gated_a(3)
            for k in range(KT):
                low("ybT", ybT, grT, k)
            ada_rows(U[4])
            gated_a(4)
            gated_a(5)
            ada_result(U[4])
            gated_a(6)
            gated_a(7)
            ada_rows(U[5])
            gated_b(0)
            gated_b(1)
            ada_result(U[5])
            gated_b(2)
            gated_b(3)
            ada_rows(U[6])
            gated_b(4)
            gated_b(5)
            ada_result(U[6])
            gated_b(6)
            gated_b(7)
            low("mT", mT, glA, KT - 1)
            ada_rows(U[7])
            ada_result(U[7])
            dve.wait_ge(mod_ready, outs_before(len(ADA_ORDER)))

            for g in range(2 * TILES):
                n, t, hf = WIDE["out"] + g, g % TILES, g // TILES
                hs_ = slice(hf * UW, (hf + 1) * UW)
                dve.wait_ge(wide_mm, n + 1)
                dve.tensor_tensor(tmpo[:, g % 2, :], g1b[:, min(t, 1), hs_], bank[n % WIDE_BANKS][:, :],
                                  ALU.mult).then_inc(emptied["v"], 1)
                dve.wait_ge(emptied["v"], emptied_by("v", n + 1))
                dve.tensor_tensor(x[:, t, hs_], x[:, t, hs_], tmpo[:, g % 2, :], ALU.add).then_inc(x1_ready, 1)
                dve.wait_ge(x1_ready, g + 1)
                link(dve.tensor_tensor_reduce(out=junk_h, in0=x[:, t, hs_], in1=x[:, t, hs_], scale=1.0, scalar=0.0,
                                              op0=ALU.mult, op1=ALU.add, accum_out=ss[:, 2, g:g + 1]))
                if g == TILES - 1:
                    dve.wait_ge(ns_mm, 1)
                    dve.tensor_copy(ns_t, bank[5][0:2 * KT, 0:P]).then_inc(ns_ready, 1)
            mean_square(2, sums=2)
            normed(2, xh, x, xh_ready)
            for k in range(0, KT, 2):
                modulated(k, "h2T", h2T, mod2)

            dve.wait_ge(lg_mm, 1)
            dve.tensor_copy(lgT, bank[0][:, 0:NTOK]).then_inc(lg_ready, 1)
            dve.wait_ge(lg_tok, 1)
            lg = bank[1][:, 0:TILES * NE].rearrange("p (t e) -> p t e", t=TILES)
            link(dve.tensor_reduce(smax[:, 0, :], lg, AX.X, ALU.max))
            dve.tensor_tensor(exl, lg, smax[:, 0, :].unsqueeze(2).to_broadcast([P, TILES, NE]),
                              ALU.subtract).then_inc(sub_ready, 1)
            dve.wait_ge(exp_ready, 1)
            link(dve.tensor_reduce(smax[:, 1, :], exl, AX.X, ALU.add))
            link(dve.reciprocal(smax[:, 2, :], smax[:, 1, :]))
            dve.tensor_tensor(aff[:, :, :], exl, smax[:, 2, :].unsqueeze(2).to_broadcast([P, TILES, NE]),
                              ALU.mult).then_inc(aff_ready, 1)
            dve.memset(onesT, 1.0)
            dve.wait_ge(aff_mm, 1)
            link(dve.tensor_copy(affT, bank[2][0:NE, 0:NTOK]))
            r = 0
            for (_, a, b), cap in zip(SETS, (CAP_CTX, CAP_LAT)):
                for _ in range(cap // 8):
                    link(dve.max(top8[:, r, :], affT[:, a:b]))
                    link(dve.match_replace(out=affT[:, a:b], in_to_replace=top8[:, r, :], in_values=affT[:, a:b],
                                           imm_value=-1.0))
                    r += 1
            link(dve.tensor_scalar(maskT, affT, -1.0, None, ALU.is_equal))
            for _, a, b in SETS:
                last = dve.tensor_tensor_scan(posT[:, a:b], onesT[:, a:b], maskT[:, a:b], 0.0, ALU.mult, ALU.add)
            link(last)
            dve.tensor_tensor(posT, posT, maskT, ALU.mult).then_inc(pos_ready, 1)
            dve.wait_ge(pos_mm, 1)
            link(dve.tensor_copy(posm[:, :, 0:NE], bank[1][:, 0:TILES * NE].rearrange("p (t e) -> p t e", t=TILES)))

            def choose(e, par):
                dve.tensor_tensor(S[par], iota[:, :].unsqueeze(1).to_broadcast([P, TILES, SL]),
                                  posm[:, :, bass.ds(e, 1)].to_broadcast([P, TILES, SL]),
                                  ALU.is_equal).then_inc(s_ready, 1)

            def gathered():
                dve.tensor_copy(xg, bank[6][:, :]).then_inc(xg_ready, 1)

            def modulate(par, n):
                for m, rows in ((1, slice(0, SL)), (0, slice(SL, 2 * SL))):
                    got = bank[7][:, :].rearrange("p (b h s) -> p h b s", b=4, h=2)[:, :, :, rows]
                    out = xgT[par].rearrange("p (h b) s -> p h b s", h=2)[:, :, :, rows]
                    for hf in range(2):
                        ks = slice(4 * hf, 4 * hf + 4)
                        last = dve.tensor_tensor(out[:, hf], got[:, hf],
                                                 mod2[:, 0, ks, m:m + 1].to_broadcast([P, 4, SL]), ALU.mult)
                last.then_inc(xgt_scaled, 1)
                dve.wait_ge(xgt_scaled, n)
                for m, rows in ((1, slice(0, SL)), (0, slice(SL, 2 * SL))):
                    last = dve.tensor_tensor(xgT[par][:, :, rows], xgT[par][:, :, rows],
                                             mod2[:, 1, :, m:m + 1].to_broadcast([P, KT, SL]), ALU.add)
                last.then_inc(xgt_ready, 1)

            def add_combined(c, n):
                t, hf = c // 2, c % 2
                dve.wait_ge(comb_mm, n + 1)
                hs_ = slice(hf * UW, (hf + 1) * UW)
                dve.tensor_tensor(x[:, t, hs_], x[:, t, hs_], comb_bank(c)[:, :], ALU.add).then_inc(comb_added, 1)

            def copy_act_t(n, j):
                dve.wait_ge(actt_mm, n + 3)
                dve.wait_ge(down_mm, n + 1)
                tiles = FCH[j][1] // P
                got = bank[2 + j % 2][:, 0:P * tiles].rearrange("p (f h s) -> p f h s", f=tiles, h=2)
                dve.tensor_copy(actT[j % 2][:, 0:tiles, :], got[:, :, 1, :]).then_inc(actt_ready, 1)

            choose(0, 0)
            for n, (freed, uses) in enumerate(((act_done, 2), (actt_mm, 2), (actt_ready, 2), (down_mm, 2),
                                               (gt_mm, 1), (comb_added, 1))):
                dve.memset(lam[:, 0, n:n + 1], 0.0).then_inc(freed, uses)
            dve.wait_ge(gather_mm, 1)
            gathered()
            dve.wait_ge(xgt_mm, 1)
            modulate(0, 1)
            dve.memset(o_pair, 0.0).then_inc(o_ready, 2)
            dve.memset(GT, 0.0).then_inc(gt_ready, 1)

            with dve.Fori(0, PAIRS) as i:
                for p in range(2):
                    e = i * 2 + p
                    for j, (_, w) in enumerate(FCH):
                        n = i * (2 * NJ) + (NJ * p + j)
                        if j >= 1:
                            copy_act_t(n - 1, j - 1)
                        dve.wait_ge(silu_done, n + 1)
                        dve.wait_ge(actt_mm, n + 1)
                        dve.tensor_tensor(sgact[j % 2][64:128, 0:w], sgact[j % 2][0:64, 0:w],
                                          bank[j % 2][64:128, 0:w], ALU.mult).then_inc(act_done, 1)
                        if j == 0:
                            dve.wait_ge(s_ready, e + 1)
                            dve.wait_ge(gt_mm, i + 1)
                            dve.tensor_tensor(G[:, 0:3:2, p, :], S[p][:, 1:3, :],
                                              aff[:, 1:3, bass.ds(e, 1)].to_broadcast([P, 2, SL]), ALU.mult)
                            dve.tensor_tensor(G[:, 1, p, :].unsqueeze(1), S[p][:, 0:1, :],
                                              aff[:, 0:1, bass.ds(e, 1)].to_broadcast([P, 1, SL]),
                                              ALU.mult).then_inc(g_ready, 1)
                            dve.wait_ge(gather_mm, e + 1)
                            choose(e + 1, 1 - p)
                        if j == 2:
                            dve.wait_ge(gather_mm, e + 2)
                            gathered()
                        if j == 3:
                            dve.wait_ge(xgt_mm, e + 2)
                            modulate(1 - p, e + 2)
                        if p == 0 and j >= 4:
                            for c in range(2 * (j - 4), 2 * (j - 4) + 2):
                                add_combined(c, i * 6 + c)
                        if p == 1 and j == 4:
                            dve.wait_ge(gt_mm, i + 2)
                            dve.tensor_copy(GT[64:128, 0, :], bank[6][64:128, 0:P])
                            dve.tensor_copy(GT[0:64, 1, :], bank[6][0:64, 0:P])
                            dve.tensor_copy(GT[0:64, 2, :], bank[6][0:64, P:2 * P]).then_inc(gt_ready, 1)
                    if p == 0:
                        for c in (4, 5):
                            add_combined(c, i * 6 + c)
                    copy_act_t(i * (2 * NJ) + (NJ * p + NJ - 1), NJ - 1)
                    dve.wait_ge(down_mm, i * (2 * NJ) + (NJ * (p + 1) + 2))
                    for q, row in enumerate((32 * p, 64 + 32 * p, 32 * p, 64 + 32 * p)):
                        src, hf = slice(32 * q, 32 * q + 32), q // 2
                        last = dve.tensor_tensor(o_pair[row:row + 32, hf * UW:(hf + 1) * UW], bank[4 + p][src, :],
                                                 g2s[src, :], ALU.mult)
                    last.then_inc(o_ready, 1)

            def final_mean(t):
                dve.wait_ge(sq_done, t + 1)
                dve.tensor_scalar(ss[:, 3, t:t + 1], ss[:, 3, t:t + 1], 1.0 / D, EPS, ALU.mult,
                                  ALU.add).then_inc(ms_ready, 1)

            def final_scale(t):
                dve.wait_ge(rstd_ready, 4 + t)
                dve.scalar_tensor_tensor(out=x[:, t, :], in0=x[:, t, :], scalar=rstd[:, 3, t:t + 1], in1=gfin,
                                         op0=ALU.mult, op1=ALU.mult).then_inc(y_ready, 1)

            dve.wait_ge(gf_in, 16)
            for t in range(TILES):
                add_combined(2 * t, PAIRS * 6 + 2 * t)
                add_combined(2 * t + 1, PAIRS * 6 + 2 * t + 1)
                if t >= 1:
                    final_mean(t - 1)
            final_scale(0)
            final_mean(TILES - 1)
            final_scale(1)
            final_scale(2)

        @block.tensor
        def _(pe):
            def wide(n):
                if n >= WIDE_BANKS:
                    e = _EVAC[n - WIDE_BANKS]
                    pe.wait_ge(emptied[e], emptied_by(e, n - WIDE_BANKS + 1))
                return bank[n % WIDE_BANKS]

            def all_emptied(n):
                for e in "va":
                    pe.wait_ge(emptied[e], emptied_by(e, n))

            def transposed(name):
                for k in range(KT):
                    to = wide(WIDE[name] + k)
                    for t in range(TILES):
                        ins = pe.transpose(to[:, t * P:(t + 1) * P], xh[:, t, k * P:(k + 1) * P], ident[:, :])
                    ins.then_inc(wide_mm, 1)

            PASSES = ((0, 0), (0, 1), (1, 0))

            def channel_major(kind, g, src, ready=None):
                q = ("chan", kind, g)
                w = split_piece(SPLIT_AT[q])
                pe.wait_ge(*split_done(SPLIT_AT[q]))
                for b in range(2):
                    n = groups_of(q) + b
                    to = wide(n)
                    for k in range(KT):
                        if ready is not None and b == 0:
                            pe.wait_ge(ready, k + 1)
                        for x_, y_ in PASSES:
                            ins = pe.matmul(to[:, 0:NTOK], w[x_][:, k, b * P:(b + 1) * P], src[y_][:, k, :],
                                            start=(k == 0 and (x_, y_) == (0, 0)),
                                            stop=(k == KT - 1 and (x_, y_) == (1, 0)))
                    ins.then_inc(wide_mm, 1)

            def token_major(kind, u, kh, src):
                q = ("tok", kind, u, kh)
                w = split_piece(SPLIT_AT[q])
                pe.wait_ge(*split_done(SPLIT_AT[q]))
                for t in range(TILES):
                    n = groups_of(q) + t
                    to = wide(n) if kh == 0 else bank[n % WIDE_BANKS]
                    for k in range(4):
                        for x_, y_ in PASSES:
                            ins = pe.matmul(to[:, :], src[y_][:, 4 * kh + k, t * P:(t + 1) * P], w[x_][:, k, :],
                                            start=(kh == 0 and k == 0 and (x_, y_) == (0, 0)),
                                            stop=(kh == 1 and k == 3 and (x_, y_) == (1, 0)))
                    if kh:
                        ins.then_inc(wide_mm, 1)
                if not kh:
                    ins.then_inc(half_mm, 1)

            def ada_rows(u):
                q, gate = ADA_AT[u], u // 2 in (2, 5)
                if q >= 2:
                    pe.wait_ge(modp_ready, q - 1)
                to = bank[6 + q % 2]
                for h in range(2):
                    n = PIECE_AT["ada", u, h]
                    w = raw_piece(n)
                    pe.wait_ge(*raw_loaded(n))
                    cols_ = slice(h * PW, (h + 1) * PW)
                    for k in range(KT):
                        j = k % 4
                        ins = pe.matmul(to[32 * j:32 * j + 32, cols_], c32[:, k, :], w[:, k, :], start=(k < 4),
                                        stop=(k >= 4 and not (gate and j == 0)))
                    if gate:
                        at = (u % 2) * UW + h * PW
                        bias = (b_gate1 if u // 2 == 2 else b_gate2)[:, at:at + PW]
                        ins = pe.matmul(to[0:32, cols_], two_ones[:, :], bias, start=False, stop=True)
                    ins.then_inc(ada_mm if h else ada_half, 1)

            def ada_sums(u):
                q, kind = ADA_AT[u], u // 2
                pe.wait_ge(modp_ready, q + 1)
                rows = modp(q)
                if kind in (2, 5):
                    for m in range(2 if kind == 2 else 1):
                        pe.wait_ge(mod_ready, outs_before(q) + m)
                        pe.matmul(bank[5][:, :], selb[:, m, :] if kind == 2 else selg[:, :], rows, start=True,
                                  stop=True).then_inc(ada_out, 1)
                    return
                pe.wait_ge(mod_ready, outs_before(q))
                for b in range(4):
                    ins = pe.transpose(bank[5][:, b * P:(b + 1) * P], rows[:, b * P:(b + 1) * P], ident[:, :])
                ins.then_inc(ada_out, 1)

            def ada(units):
                for a, b in zip(units, units[1:] + [None]):
                    if a == units[0]:
                        ada_rows(a)
                    if b is not None:
                        ada_rows(b)
                    ada_sums(a)

            pe.wait_ge(consts, 1)
            pe.wait_ge(c32_ready, 1)
            ada(ADA_FIRST)
            pe.wait_ge(xh_ready, TILES)
            transposed("hT")
            for g in range(4):
                channel_major("in", 8 + g, hT, lo_ready["hT"] if g == 0 else None)
            pe.wait_ge(rg_in, 64)
            for g in range(4):
                channel_major("in", 12 + g, hT)
                channel_major("in", g, hT)
                for b in range(2 * g, 2 * g + 2):
                    pe.wait_ge(conv_done, b + 1)
                    for q in range(4):
                        n = WIDE[f"rg{g}"] + 4 * (b % 2) + q
                        to = wide(n)
                        pe.matmul(to[:, 0:NTOK], rgw[q][:, b * P:(b + 1) * P], xc[:, b, :], start=True,
                                  stop=True).then_inc(wide_mm, 1)
            for hf in range(2):
                for kh in range(2):
                    token_major("in", 2 + hf, kh, hT)
            U = ADA_LATER
            channel_major("in", 20, hT)
            channel_major("in", 21, hT)
            ada_rows(U[0])
            channel_major("in", 22, hT)
            ada_sums(U[0])
            channel_major("in", 23, hT)
            ada_rows(U[1])
            pe.wait_ge(v_ready, TILES)
            pe.wait_ge(sp_in, 32)
            for g in range(KT):
                n = WIDE["spatial"] + g
                to = wide(n)
                for t in range(TILES):
                    ins = pe.matmul(to[:, t * P:(t + 1) * P], vtok[:, t, g * P:(g + 1) * P], wsp[:, g, :],
                                    start=True, stop=True)
                ins.then_inc(wide_mm, 1)
            ada_sums(U[1])
            channel_major("in", 16, hT)
            channel_major("in", 17, hT)
            ada_rows(U[2])
            channel_major("in", 18, hT)
            ada_sums(U[2])
            channel_major("in", 19, hT)
            ada_rows(U[3])
            pe.wait_ge(lo_ready["yaT"], KT)
            channel_major("br_a", 0, yaT)
            ada_sums(U[3])
            channel_major("br_a", 1, yaT)
            pe.wait_ge(bg2_in, 16)
            ada_rows(U[4])
            channel_major("br_a", 2, yaT)
            ada_sums(U[4])
            channel_major("br_a", 3, yaT)
            ada_rows(U[5])
            pe.wait_ge(lo_ready["ybT"], KT)
            channel_major("br_b", 0, ybT)
            ada_sums(U[5])
            channel_major("br_b", 1, ybT)
            pe.wait_ge(bg_in, 16)
            ada_rows(U[6])
            channel_major("br_b", 2, ybT)
            ada_sums(U[6])
            channel_major("br_b", 3, ybT)
            ada_rows(U[7])
            pe.wait_ge(lo_ready["mT"], 4)
            token_major("out", 0, 0, mT)
            ada_sums(U[7])
            pe.wait_ge(lo_ready["mT"], KT)
            token_major("out", 0, 1, mT)
            pe.wait_ge(mod_ready, outs_before(len(ADA_ORDER)))
            pe.transpose(bank[5][0:2 * KT, 0:P], ns[:, :, :].rearrange("p d k -> p (d k)"), ident[:, :])\
                .then_inc(ns_mm, 1)
            token_major("out", 1, 0, mT)
            token_major("out", 1, 1, mT)
            pe.wait_ge(xh_ready, 2 * TILES)
            transposed("h2T")
            pe.wait_ge(wr_in, 16)
            all_emptied(WIDE["h2T"] + KT)
            for k in range(KT):
                j = k % 4
                ins = pe.matmul(bank[0][32 * j:32 * j + 32, 0:NTOK], wr[:, k, :], h2T[:, k, :], start=(k < 4),
                                stop=(k >= 4))
            ins.then_inc(lg_mm, 1)
            pe.wait_ge(lg_ready, 1)
            for t in range(TILES):
                ins = pe.matmul(bank[1][:, t * NE:(t + 1) * NE], lgT[:, t * P:(t + 1) * P], sel4[:, :], start=True,
                                stop=True)
            ins.then_inc(lg_tok, 1)
            pe.wait_ge(aff_ready, 1)
            for t in range(TILES):
                ins = pe.transpose(bank[2][0:NE, t * P:(t + 1) * P], aff[:, t, :], ident[:, :])
            ins.then_inc(aff_mm, 1)
            pe.wait_ge(pos_ready, 1)
            for t in range(TILES):
                ins = pe.transpose(bank[1][:, t * NE:(t + 1) * NE], posT[:, t * P:(t + 1) * P], ident[0:NE, 0:NE])
            ins.then_inc(pos_mm, 1)

            def gather(par):
                for t in (1, 0, 2):
                    for hf in range(2):
                        at = 64 * hf + (SL if t == 0 else 0)
                        ins = pe.matmul(bank[6][at:at + SL, :], S[par][:, t, :], xh[:, t, hf * UW:(hf + 1) * UW],
                                        start=(t != 2), stop=(t != 1))
                ins.then_inc(gather_mm, 1)

            def gathered_t():
                for b in range(4):
                    ins = pe.transpose(bank[7][:, b * P:(b + 1) * P], xg[:, b * P:(b + 1) * P], ident[:, :])
                ins.then_inc(xgt_mm, 1)

            def combine(c):
                t, hf = c // 2, c % 2
                pe.matmul(comb_bank(c)[:, :], GT[:, t, :], o_pair[:, hf * UW:(hf + 1) * UW], start=True,
                          stop=True).then_inc(comb_mm, 1)

            def gate_up(i, p, j):
                n = i * (2 * NJ) + (NJ * p + j)
                w = FCH[j][1]
                slots = []
                for kind in ("gate", "up"):
                    s, loads = expert_loads(i, PAIR_AT[p, kind, j])
                    pe.wait_ge(slot_in[s], loads)
                    slots.append(by_rows(s, w))
                if j == 0:
                    pe.wait_ge(xgt_ready, i * 2 + (p + 1))
                pe.wait_ge(act_done, n + 1)
                for k in range(KT):
                    for q in range(2):
                        ins = pe.matmul(bank[j % 2][64 * q:64 * q + 64, 0:w], xgT[p][:, k, :], slots[q][:, k, :],
                                        start=(k == 0), stop=(k == KT - 1))
                ins.then_inc(gu_mm, 1)

            def act_t(i, p, j):
                n = i * (2 * NJ) + (NJ * p + j)
                pe.wait_ge(act_done, n + 3)
                pe.wait_ge(actt_ready, n + 1)
                for f in range(FCH[j][1] // P):
                    ins = pe.transpose(bank[2 + j % 2][:, f * P:(f + 1) * P],
                                       sgact[j % 2][:, f * P:(f + 1) * P], ident[:, :])
                ins.then_inc(actt_mm, 1)

            def down(i, p, j):
                n = i * (2 * NJ) + (NJ * p + j)
                s, loads = expert_loads(i, PAIR_AT[p, "down", j])
                tiles = FCH[j][1] // P
                w = by_ff(s, tiles)
                pe.wait_ge(slot_in[s], loads)
                pe.wait_ge(actt_ready, n + 3)
                if j == 0:
                    pe.wait_ge(o_ready, i * 2 + (p + 1))
                for f in range(tiles):
                    for q in range(2):
                        ins = pe.matmul(bank[4 + p][64 * q:64 * q + 64, :], actT[j % 2][:, f, :],
                                        w[:, f, q * UW:(q + 1) * UW], start=(j == 0 and f == 0),
                                        stop=(j == NJ - 1 and f == tiles - 1))
                ins.then_inc(down_mm, 1)

            pe.wait_ge(s_ready, 1)
            pe.wait_ge(modp_ready, len(ADA_ORDER))
            gather(0)
            pe.wait_ge(xg_ready, 1)
            gathered_t()
            with pe.Fori(0, PAIRS) as i:
                for p in range(2):
                    e = i * 2 + p
                    for j in range(NJ):
                        gate_up(i, p, j)
                        if j >= 1:
                            act_t(i, p, j - 1)
                        if j == 1:
                            pe.wait_ge(s_ready, e + 2)
                            pe.wait_ge(xg_ready, e + 1)
                            pe.wait_ge(comb_added, i * 6 + (6 * p + 1))
                            pe.wait_ge(gt_ready, i + 1)
                            gather(1 - p)
                        if j == 2:
                            pe.wait_ge(xg_ready, e + 2)
                            pe.wait_ge(xgt_ready, e + 1)
                            gathered_t()
                        if p == 0 and j >= 3:
                            for c in range(2 * (j - 3), 2 * (j - 3) + 2):
                                if c == 0:
                                    pe.wait_ge(gt_ready, i + 1)
                                    pe.wait_ge(o_ready, e + 2)
                                    pe.wait_ge(xgt_ready, e + 2)
                                if c >= 2:
                                    pe.wait_ge(comb_added, i * 6 + c)
                                combine(c)
                        if p == 1 and j == 3:
                            pe.wait_ge(g_ready, i * 2 + 2)
                            pe.transpose(bank[6][:, 0:P], G[:, 0:2, :, :].rearrange("p b e s -> p (b e s)"), ident[:, :])
                            pe.transpose(bank[6][0:64, P:2 * P], G[:, 2, :, :].rearrange("p e s -> p (e s)"),
                                         ident[:, :]).then_inc(gt_mm, 1)
                        if j >= 1:
                            down(i, p, j - 1)
                    act_t(i, p, NJ - 1)
                    down(i, p, NJ - 1)
            pe.wait_ge(gt_ready, PAIRS + 1)
            pe.wait_ge(o_ready, NE + 2)
            pe.wait_ge(xgt_ready, NE + 1)
            for c in range(6):
                if c >= 2:
                    pe.wait_ge(comb_added, PAIRS * 6 + c)
                combine(c)


def position_table():
    import numpy as np

    rr, cc = np.meshgrid(np.arange(NLAT // GRID_W, dtype=np.float32), np.arange(GRID_W, dtype=np.float32), indexing="ij")
    quarter = D // 4
    omega = (1.0 / (10000.0 ** (np.arange(quarter, dtype=np.float32) / np.float32(quarter)))).astype(np.float32)
    r, c = rr.reshape(-1)[:, None] * omega, cc.reshape(-1)[:, None] * omega
    return np.ascontiguousarray(np.concatenate([np.sin(r), np.cos(r), np.sin(c), np.cos(c)], axis=-1), np.float32)


def kernel(x_prompt, x_sample, state_rglru, c, c_ctx, w_ada, b_ada, norm1_g, norm2_g, w_in, v_norm_g,
           w_spatial, b_spatial, conv_w, conv_b, rg_w_a, rg_b_a, rg_w_x, rg_b_x, rg_lambda,
           w_br_a, w_br_b, w_out, w_router, w_gate_e, w_up_e, w_down_e, final_norm_g):
    import concourse.bacc as bacc
    import numpy as np
    from concourse.bass_utils import run_bass_kernel_spmd

    def columns(a):
        return np.asarray(a).reshape(-1, P).T

    conditions = np.stack([np.asarray(c_ctx).reshape(KT, P), np.asarray(c).reshape(KT, P)], axis=1)
    cols = np.concatenate([columns(conditions)] + [columns(a) for a in (
        norm1_g, norm2_g, b_ada, v_norm_g, conv_w, conv_b, rg_b_a, rg_b_x, rg_lambda, state_rglru)], axis=1)
    arrays = {
        "x_prompt": np.asarray(x_prompt)[0], "x_sample": np.asarray(x_sample)[0], "emb": position_table(),
        "cols": cols, "w_ada": np.asarray(w_ada)[0], "b_ada": np.asarray(b_ada), "w_in": np.asarray(w_in)[0],
        "w_spatial_t": np.asarray(w_spatial)[0].transpose(2, 0, 1).reshape(P, D),
        "b_spatial": np.asarray(b_spatial).reshape(1, D),
        "rg_w": np.stack([np.asarray(rg_w_a)[0], np.asarray(rg_w_x)[0]]).transpose(3, 0, 1, 2, 4).reshape(P, -1),
        "w_br_a": np.asarray(w_br_a)[0], "w_br_b": np.asarray(w_br_b)[0], "w_out": np.asarray(w_out)[0],
        "w_router": np.asarray(w_router)[0].reshape(KT, P, NE).transpose(1, 0, 2).reshape(P, KT * NE),
        "w_gate": np.asarray(w_gate_e)[0], "w_up": np.asarray(w_up_e)[0], "w_down": np.asarray(w_down_e)[0],
        "final_norm_g": np.asarray(final_norm_g).reshape(1, D),
    }
    arrays = {k: np.ascontiguousarray(v) for k, v in arrays.items()}
    outs = {"y_prompt": (NCTX, D), "y_sample": (NLAT, D), "new_state": (2 * KT, P)}

    nc = bacc.Bacc("TRN2", target_bir_lowering=False, num_devices=1)
    args = {k: nc.dram_tensor(f"in_{k}", v.shape, mybir.dt.from_np(v.dtype), kind="ExternalInput").ap()
            for k, v in arrays.items()}
    args |= {k: nc.dram_tensor(f"out_{k}", shape, mybir.dt.float32, kind="ExternalOutput").ap()
             for k, shape in outs.items()}
    build(nc, **args)
    r = run_bass_kernel_spmd(nc, [{f"in_{k}": v for k, v in arrays.items()}], core_ids=[0]).results[0]
    return (r["out_y_prompt"].reshape(x_prompt.shape), r["out_y_sample"].reshape(x_sample.shape),
            r["out_new_state"].reshape(x_prompt.shape[0], 1, 2, D))
```

```python
from contextlib import ExitStack

import concourse.bass as bass
from concourse import mybir

D = 1024
P = 128
KT = D // P
TILES = 3
NCTX, NLAT = 128, 256
NTOK = NCTX + NLAT
GRID_W = 64
NE = 16
PAIRS = NE // 2
D_FF = 2816
UW = 512
FCH = [(f, min(UW, D_FF - f)) for f in range(0, D_FF, UW)]
NJ = len(FCH)
CAP_CTX, CAP_LAT = 2 * NCTX // NE, 2 * NLAT // NE
SL = 32
RG_C = 8.0
EPS = 1e-6
CONV_W = 4
SLOTS = 9
SLOT_F = KT * UW
PW = 256
PIECE_F = KT * PW
RAW, SPLIT = 4, 2

COLS, _at = {}, 0
for _name, _n in (("c", 2 * KT), ("norm1_g", KT), ("norm2_g", KT), ("b_ada", 6 * KT), ("v_norm_g", KT),
                  ("conv_w", CONV_W * KT), ("conv_b", KT), ("rg_b_a", 2 * KT), ("rg_b_x", 2 * KT),
                  ("rg_lambda", 2 * KT), ("state", 2 * KT)):
    COLS[_name] = (_at, _n)
    _at += _n
NCOLS = _at

ADA_FIRST = [2, 0, 3, 1]
ADA_GATE1, ADA_SCALE2, ADA_SHIFT2, ADA_GATE2 = [4, 5], [8, 9], [6, 7], [10, 11]
ADA_LATER = ADA_SCALE2 + ADA_SHIFT2 + ADA_GATE1
ADA_ORDER = ADA_FIRST + ADA_LATER + ADA_GATE2
N_MOD = len(ADA_FIRST + ADA_LATER)
def _chan(kind, first, n=4):
    return [("chan", kind, first + g) for g in range(n)]


def _tok(kind, first):
    return [("tok", kind, first + hf, kh) for hf in range(2) for kh in range(2)]


def _ada(*us):
    return [("ada", u, h) for u in us for h in range(2)]


PIECES = _ada(*ADA_FIRST) + _chan("in", 8)
for _g in range(4):
    PIECES += _chan("in", 12 + _g, 1) + _chan("in", _g, 1)
PIECES += _tok("in", 2)
for _kind, _first, _units in (("in", 20, ADA_LATER[0:2]), ("in", 16, ADA_LATER[2:4]),
                              ("br_a", 0, [None, ADA_LATER[4]]), ("br_b", 0, [ADA_LATER[5], None])):
    for _g, _u in zip((0, 2), _units):
        PIECES += _chan(_kind, _first + _g, 2) + ([] if _u is None else _ada(_u))
PIECES += _tok("out", 0) + _ada(*ADA_GATE2)
NPIECES = len(PIECES)
PIECE_AT = {q: n for n, q in enumerate(PIECES)}
SPLITS = [n for n, q in enumerate(PIECES) if q[0] != "ada"]
SPLIT_AT = {PIECES[n]: m for m, n in enumerate(SPLITS)}
ADA_AT = {u: n for n, u in enumerate(ADA_ORDER)}

WIDE_BANKS = 5
WIDE, _EVAC = {}, []


def _groups(name, n, engines):
    WIDE[name] = len(_EVAC)
    _EVAC.extend(engines[i % len(engines)] for i in range(n))


_groups("hT", KT, "va")
_groups("xr", KT, "a")
for _g in range(4):
    _groups(f"gr{_g}", 2, "a")
    _groups(f"u{_g}", 2, "a")
    _groups(f"rg{_g}", 8, "a")
_groups("v", 2 * TILES, "a")
_groups("glB", KT, "a")
_groups("spatial", KT, "v")
_groups("glA", KT, "a")
_groups("br_a", KT, "v")
_groups("br_b", KT, "v")
_groups("out", 2 * TILES, "v")
_groups("h2T", KT, "va")


def emptied_by(engine, n):
    return sum(e == engine for e in _EVAC[:n])


PAIR_UNITS = []
for _p in range(2):
    for _j in range(NJ):
        PAIR_UNITS += [(_p, "gate", _j), (_p, "up", _j)]
        if _j >= 1:
            PAIR_UNITS.append((_p, "down", _j - 1))
    PAIR_UNITS.append((_p, "down", NJ - 1))
UPP = len(PAIR_UNITS)
assert UPP % SLOTS == 0
PAIR_AT = {u: n for n, u in enumerate(PAIR_UNITS)}
SLOT_ORDER = [0, 1, 2, 8, 4, 3, 5, 6, 7]


def build(nc, x_prompt, x_sample, emb, cols, w_ada, b_ada, w_in, w_spatial_t, b_spatial, rg_w, w_br_a,
          w_br_b, w_out, w_router, w_gate, w_up, w_down, final_norm_g, y_prompt, y_sample, new_state):
    F32, F32R, I32 = mybir.dt.float32, mybir.dt.float32r, mybir.dt.int32
    ALU, ACT, AX = mybir.AluOpType, mybir.ActivationFunctionType, mybir.AxisListType

    ctx = ExitStack()
    with ctx:
        def sb(name, shape, dt=F32):
            return ctx.enter_context(nc.sbuf_tensor(name, shape, dt))

        def sem(name):
            return ctx.enter_context(nc.semaphore(name))

        ring_at = -(-nc.sbuf_base // 32) * 32
        W1 = KT * NTOK
        raw0 = 7 * W1
        split0 = raw0 + RAW * PIECE_F
        ring = sb("ring", [P, max(SLOTS * SLOT_F, split0 + SPLIT * 2 * PIECE_F)])
        x = sb("x", [P, TILES, D])
        xh = sb("xh", [P, TILES, D])
        work = sb("work", [P, 6656])
        col = sb("col", [P, NCOLS])
        ident = sb("ident", [P, P])
        c32 = sb("c32", [P, KT, 32])
        selb = sb("selb", [P, 2, P])
        selg = sb("selg", [P, P])
        two_ones = sb("two_ones", [1, 32])
        mod1 = sb("mod1", [P, 2, KT, 2])
        mod2 = sb("mod2", [P, 2, KT, 2])
        mod_raw = sb("mod_raw", [P, 4, 2])
        mod_sum = sb("mod_sum", [P, 4, 2])
        negsp = sb("negsp", [P, 2, KT])
        lam = sb("lam", [P, 4, 2 * KT])
        ss = sb("ss", [P, 4, 2 * TILES])
        rstd = sb("rstd", [P, 4, TILES])
        half = sb("half", [P, 1])
        tiny = sb("tiny", [P, 1])
        ns = sb("ns", [P, 2, KT])
        wr = sb("wr", [P, KT, 32])
        sel4 = sb("sel4", [P, NE])
        ns_t = sb("ns_t", [2 * KT, P])
        iota_i = sb("iota_i", [P, SL], I32)
        iota = sb("iota", [P, SL])
        modp_g2 = sb("modp_g2", [P, UW])
        posm = sb("posm", [P, TILES, NE + 1])
        aff = sb("aff", [P, TILES, NE])
        smax = sb("smax", [P, 3, TILES])

        def part(tensor, at, n):
            return tensor[:, at:at + n]

        def chan(at):
            return part(ring, at, KT * NTOK).rearrange("p (k t) -> p k t", k=KT)

        def rounded(name, at, n):
            return nc.alloc_sbuf_tensor_at(name, [P, n], F32R, offset=ring_at + 4 * at)

        area_r = {a: rounded(f"area_r{a}", a * W1, W1) for a in (0, 3, 4, 5, 6)}

        def chan_r(area):
            return area_r[area][:, :].rearrange("p (k t) -> p k t", k=KT)

        def f32(ap):
            return ap.bitcast(F32)

        hT = [chan_r(0), chan_r(4)]
        ybT = [chan_r(0), chan_r(3)]
        yaT, mT = ([chan_r(5), chan_r(6)] for _ in range(2))
        vtok = part(ring, W1, TILES * D).rearrange("p (t d) -> p t d", t=TILES)
        embt = part(ring, W1, 2 * D).rearrange("p (t d) -> p t d", t=2)
        glA = chan(W1)
        xc = glB = chan(2 * W1)
        grT = chan(3 * W1)
        g1b = part(ring, 4 * W1, 2 * D).rearrange("p (m d) -> p m d", m=2)
        b_gate1 = ring[0:1, 4 * W1 + 2 * D:4 * W1 + 3 * D]
        xr = hfull = chan(5 * W1)
        uT = chan(6 * W1)
        tmpc = xh[:, 2, :].rearrange("p (b n) -> p b n", b=2)
        rgw = [part(ring, W1 + n * D, D) for n in range(3)] + [xh[:, 2, :]]
        wsp = part(xh[:, :, :].rearrange("p t d -> p (t d)"), 0, D).rearrange("p (g q) -> p g q", g=KT)
        bsp = part(xh[:, :, :].rearrange("p t d -> p (t d)"), D, D).rearrange("p (g q) -> p g q", g=KT)
        gfin = xh[:, 0, :]
        squared_last = xh[:, 1, :]

        split_r = [[rounded(f"split{n}_{h}", split0 + (2 * n + h) * PIECE_F, PIECE_F) for h in range(2)]
                   for n in range(SPLIT)]

        def piece(tensor, at, q):
            width = UW if q[0] == "tok" else PW
            return part(tensor, at, PIECE_F).rearrange("p (k n) -> p k n", n=width)

        def raw_piece(n):
            return piece(ring, raw0 + n % RAW * PIECE_F, PIECES[n])

        def split_piece(m):
            return [piece(tensor, 0, PIECES[SPLITS[m]]) for tensor in split_r[m % SPLIT]]

        def by_rows(s, width):
            return part(ring, s * SLOT_F, KT * width).rearrange("p (k n) -> p k n", k=KT)

        def by_ff(s, tiles):
            return part(ring, s * SLOT_F, tiles * D).rearrange("p (t n) -> p t n", t=tiles)

        HB = 2 * NTOK
        rbuf = [part(work, n * HB, HB).rearrange("p (d t) -> p d t", d=2) for n in range(2)]
        gibuf = [part(work, (2 + n) * HB, HB).rearrange("p (d t) -> p d t", d=2) for n in range(2)]
        ab = [part(work, (4 + n) * HB, HB).rearrange("p (d t) -> p d t", d=2) for n in range(2)]
        asq = part(work, 6 * HB, HB).rearrange("p (d t) -> p d t", d=2)
        hs = part(work, 7 * HB, HB).rearrange("p (d t) -> p d t", d=2)
        squared = part(work, 4 * HB, D)
        squared_half = part(work, 4 * HB + D, UW)

        def modp(q):
            if q >= N_MOD:
                return (part(work, 6 * HB, UW), modp_g2[:, :])[q - N_MOD]
            return part(work, 4 * HB + D + (q % 2) * UW, UW)

        tmpo = part(work, 4 * HB, 2 * UW).rearrange("p (b n) -> p b n", b=2)
        g2s = part(work, 6144, UW)
        h2T = part(work, 0, KT * NTOK).rearrange("p (k t) -> p k t", k=KT)
        lgT = part(work, 3072, NTOK)
        affT = work[0:NE, 3456:3456 + NTOK]
        posT = work[0:NE, 3840:3840 + NTOK]
        onesT = work[0:NE, 4224:4224 + NTOK]
        top8 = work[0:NE, 5504:5504 + 48].rearrange("p (r n) -> p r n", n=8)
        exl = part(work, 5568, TILES * NE).rearrange("p (t e) -> p t e", t=TILES)
        maskT = work[0:NE, 5632:5632 + NTOK]
        xg = part(work, 0, UW)
        xgT = [part(work, UW * (1 + n), UW).rearrange("p (k s) -> p k s", k=KT) for n in range(2)]
        sgact = [part(work, UW * (3 + n), UW) for n in range(2)]
        actT = [part(work, 2560 + 256 * n, 256).rearrange("p (f s) -> p f s", f=4) for n in range(2)]
        o_pair = part(work, 3072, D)
        GT = part(work, 4096, TILES * P).rearrange("p (b t) -> p b t", b=TILES)
        S = [part(work, 5120 + 96 * n, 96).rearrange("p (t s) -> p t s", t=TILES) for n in range(2)]
        G = part(work, 5312, 192).rearrange("p (b e s) -> p b e s", b=3, e=2)
        b_gate2 = work[0:1, 5120:5120 + D]

        bank = [ctx.enter_context(nc.psum_tensor(f"bank{n}", [P, 512], F32)) for n in range(8)]

        rg_in, bg2_in = sem("rg_in"), sem("bg2_in")
        x_in, emb_in, col_in, wr_in = sem("x_in"), sem("emb_in"), sem("col_in"), sem("wr_in")
        sp_in, bg_in, gf_in = sem("sp_in"), sem("bg_in"), sem("gf_in")
        slot_in = [sem(f"slot_in{s}") for s in range(SLOTS)]
        raw_in = [sem(f"raw_in{s}") for s in range(RAW)]
        piece_hi, piece_lo = sem("piece_hi"), {"v": sem("piece_lo_v"), "p": sem("piece_lo_p")}
        half_mm = sem("half_mm")
        hi_ready = {k: sem(f"{k}_hi") for k in ("hT", "yaT", "ybT", "mT")}
        lo_ready = {k: sem(f"{k}_lo") for k in ("hT", "yaT", "ybT", "mT")}
        consts = sem("consts")
        c32_ready = sem("c32_ready")
        link_v, link_p = sem("link_v"), sem("link_p")
        ms_ready, rstd_ready = sem("ms_ready"), sem("rstd_ready")
        xh_ready = sem("xh_ready")
        ada_half = sem("ada_half")
        ada_mm, modp_ready, ada_out, mod_ready = sem("ada_mm"), sem("modp_ready"), sem("ada_out"), sem("mod_ready")
        modp2_ready, g2_mm, g2_ready = sem("modp2_ready"), sem("g2_mm"), sem("g2_ready")
        wide_mm = sem("wide_mm")
        emptied = {"v": sem("emptied_v"), "a": sem("emptied_a")}
        lam_exp, lam_one, lam_ln, lam_ready = sem("lam_exp"), sem("lam_one"), sem("lam_ln"), sem("lam_ready")
        exp_done = sem("exp_done")
        conv_done, tanh_done, om_ready, sqrt_done = sem("conv_done"), sem("tanh_done"), sem("om_ready"), sem("sqrt_done")
        gx_done, scan_done, yb_done = sem("gx_done"), sem("scan_done"), sem("yb_done")
        v_ready, ya_ready, merged_ready, x1_ready = sem("v_ready"), sem("ya_ready"), sem("merged_ready"), sem("x1_ready")
        ns_mm, ns_ready, out_done = sem("ns_mm"), sem("ns_ready"), sem("out_done")
        sq_done = sem("sq_done")
        lg_mm, lg_ready, lg_tok, sub_ready, exp_ready = (sem(n) for n in ("lg_mm", "lg_ready", "lg_tok", "sub_ready", "exp_ready"))
        aff_ready, aff_mm, pos_ready, pos_mm = (sem(n) for n in ("aff_ready", "aff_mm", "pos_ready", "pos_mm"))
        s_ready, gather_mm, xg_ready, xgt_mm, xgt_ready = (sem(n) for n in ("s_ready", "gather_mm", "xg_ready", "xgt_mm", "xgt_ready"))
        xgt_scaled = sem("xgt_scaled")
        gu_mm, silu_done, act_done, actt_mm, actt_ready = (sem(n) for n in ("gu_mm", "silu_done", "act_done", "actt_mm", "actt_ready"))
        down_mm, o_ready, g_ready, gt_mm, gt_ready = (sem(n) for n in ("down_mm", "o_ready", "g_ready", "gt_mm", "gt_ready"))
        o_half = sem("o_half")
        comb_mm, comb_added, y_ready = sem("comb_mm"), sem("comb_added"), sem("y_ready")

        def vcol(name, *shape):
            at, n = COLS[name]
            v = col[:, at:at + n]
            if len(shape) == 2:
                v = v.rearrange("p (a b) -> p a b", a=shape[0])
            return v

        cw, cb = vcol("conv_w", CONV_W, KT), vcol("conv_b")
        st0 = vcol("state", 2, KT)

        LO_BY_V = (8, 10, 12, 14, 15)

        def split_done(m):
            by_v = sum(n <= m for n in LO_BY_V)
            return (piece_lo["v"], by_v) if m in LO_BY_V else (piece_lo["p"], m + 1 - by_v)

        def raw_loaded(n):
            return raw_in[n % RAW], 16 * (n // RAW + 1)

        def expert_loads(i, u):
            s = SLOT_ORDER[u % SLOTS]
            return s, 16 * (u // SLOTS + 1) + i * (16 * (UPP // SLOTS))

        CHAN_AT = {("in", 12 + g): (f"gr{g}", 0) for g in range(4)} | {("in", g): (f"u{g}", 0) for g in range(4)}
        CHAN_AT |= {("in", 8 + g): ("xr", 2 * g) for g in range(4)}
        CHAN_AT |= {("in", 16 + g): ("glA", 2 * g) for g in range(4)} | {("in", 20 + g): ("glB", 2 * g) for g in range(4)}
        CHAN_AT |= {(k, g): (k, 2 * g) for k in ("br_a", "br_b") for g in range(4)}

        def groups_of(q):
            if q[0] == "tok":
                return WIDE["v" if q[1] == "in" else "out"] + TILES * (q[2] % 2)
            name, at = CHAN_AT[q[1], q[2]]
            return WIDE[name] + at

        def piece_mm(n):
            q = PIECES[n]
            if q[0] == "ada":
                return (ada_mm if q[2] else ada_half), ADA_AT[q[1]] + 1
            if q[0] == "tok" and q[3] == 0:
                return half_mm, sum(p[0] == "tok" and p[3] == 0 for p in PIECES[:n]) + 1
            return wide_mm, groups_of(q) + (TILES if q[0] == "tok" else 2)

        def raw_used(n):
            return piece_mm(n) if PIECES[n][0] == "ada" else split_done(SPLITS.index(n))

        def pair_used(i, u):
            p, kind, j = PAIR_UNITS[u]
            return (down_mm, i * (2 * NJ) + (NJ * p + j + 3)) if kind == "down" else (gu_mm, i * (2 * NJ) + (NJ * p + j + 1))

        def outs_before(q):
            return sum(2 if u // 2 == 2 else 1 for u in ADA_ORDER[:q])

        def stats(n, t):
            return 2 + (n - 2) * TILES + t + 1

        def comb_bank(c):
            return bank[6 + c % 2]

        LAST = ((0, 0), (1, 0), (0, 1), (1, 1), (2, 0), (2, 1))
        LAST_BANKS = (6, 7, 0, 1, 2, 3)

        SETS = ((0, 0, NCTX), (1, NCTX, NTOK))

        block = ctx.enter_context(nc.Block())

        @block.sync
        def _(sp):
            sources = {"ada": w_ada, "in": w_in, "br_a": w_br_a, "br_b": w_br_b, "out": w_out}
            sp.dma_start(x[:, 0, :], x_prompt).then_inc(x_in, 16)
            sp.dma_start(x[:, 1:3, :], x_sample.rearrange("(t p) d -> p t d", p=P)).then_inc(x_in, 16)
            sp.dma_start(embt, emb.rearrange("(t p) d -> p t d", p=P)).then_inc(emb_in, 16)

            def load_piece(n):
                if n >= RAW:
                    sp.wait_ge(*raw_used(n - RAW))
                q = PIECES[n]
                if q[0] == "tok":
                    rows, cols_ = slice(q[3] * 4 * P, (q[3] + 1) * 4 * P), slice(q[2] * UW, (q[2] + 1) * UW)
                elif q[0] == "chan":
                    rows, cols_ = slice(0, D), slice(q[2] * PW, (q[2] + 1) * PW)
                else:
                    rows, cols_ = slice(0, D), slice((2 * q[1] + q[2]) * PW, (2 * q[1] + q[2] + 1) * PW)
                src = sources["ada" if q[0] == "ada" else q[1]][rows, cols_].rearrange("(k p) n -> p k n", p=P)
                sp.dma_start(raw_piece(n), src).then_inc(raw_in[n % RAW], 16)

            for n in range(NPIECES - 4):
                load_piece(n)

            def load(i, u, e):
                _, kind, j = PAIR_UNITS[u]
                f, w = FCH[j]
                s, _ = expert_loads(i, u)
                if kind == "down":
                    dst = by_ff(s, w // P)
                    src = w_down[bass.ds(e, 1), f:f + w, :].rearrange("e (t p) n -> p (e t) n", p=P)
                else:
                    dst = by_rows(s, w)
                    src = (w_gate if kind == "gate" else w_up)[bass.ds(e, 1), :, f:f + w]
                    src = src.rearrange("e (k p) n -> p (e k) n", p=P)
                sp.dma_start(dst, src).then_inc(slot_in[s], 16)

            def used(*q):
                return piece_mm(PIECE_AT[q])

            out_done_mm = used("tok", "out", 1, 1)
            x1_done = (emptied["v"], emptied_by("v", WIDE["out"] + 2 * TILES))
            dead = [
                (lo_ready["mT"], KT),
                (lo_ready["mT"], KT),
                (lo_ready["mT"], KT),
                out_done_mm,
                out_done_mm,
                x1_done,
                piece_mm(NPIECES - 1),
                piece_mm(NPIECES - 1),
                piece_mm(NPIECES - 1),
            ]
            for n in range(SLOTS):
                if n == 3:
                    for q in range(NPIECES - 4, NPIECES):
                        load_piece(q)
                sp.wait_ge(*dead[n])
                load(0, n, PAIR_UNITS[n][0])

            def ahead(i, u):
                sp.wait_ge(*pair_used(i, u - SLOTS))
                nxt, v = divmod(u, UPP)
                load(i, v, i * 2 + (2 * nxt + PAIR_UNITS[v][0]))

            with sp.Fori(0, PAIRS - 1) as i:
                for u in range(SLOTS, UPP + SLOTS):
                    ahead(i, u)
            for u in range(SLOTS, UPP):
                ahead(PAIRS - 1, u)

            for t in range(TILES):
                sp.wait_ge(y_ready, t + 1)
                dst = y_prompt if t == 0 else y_sample[(t - 1) * P:t * P, :]
                sp.dma_start(dst, x[:, t, :]).then_inc(out_done, 16)
            sp.wait_ge(out_done, 16 * (TILES + 1))

        @block.gpsimd
        def _(pool):
            count = [0]

            def link(ins):
                count[0] += 1
                ins.then_inc(link_p, 1)
                pool.wait_ge(link_p, count[0])

            link(pool.memset(c32[:, :, :], 0.0))
            pool.memset(half[:, :], -0.5)
            link(pool.memset(two_ones[:, :], 0.0))
            pool.memset(two_ones[:, 0:2], 1.0)
            pool.memset(posm[:, :, :], 0.0)
            pool.memset(selb[:, :, :], 0.0)
            link(pool.memset(ident[:, :], 0.0))
            for j in range(4):
                link(pool.affine_select(out=selb[:, :, :], in_=selb[:, :, :], compare_op=ALU.not_equal, fill=1.0,
                                        base=-32 * j, pattern=[[-1, 2], [0, P]], channel_multiplier=1))
            link(pool.affine_select(out=ident[:, :], in_=ident[:, :], compare_op=ALU.not_equal, fill=1.0,
                                    base=0, pattern=[[-1, P]], channel_multiplier=1))
            sg = selg[:, :].rearrange("p (h m s) -> p h m s", h=2, m=2)
            for m in range(2):
                sv = selb[:, 1 - m, 0:64].rearrange("p (h s) -> p h s", h=2)
                pool.tensor_copy(sg[:, :, m, :], sv)
            pool.memset(wr[:, :, NE:32], 0.0)
            link(pool.memset(sel4[:, :], 0.0))
            for j in range(4):
                link(pool.affine_select(out=sel4[:, :], in_=sel4[:, :], compare_op=ALU.not_equal, fill=1.0,
                                        base=-32 * j, pattern=[[-1, NE]], channel_multiplier=1))
            link(pool.iota(iota_i[:, :], pattern=[[1, SL]], base=1, channel_multiplier=0))
            pool.tensor_copy(iota[:, :], iota_i[:, :]).then_inc(consts, 1)

            def power(n):
                pool.wait_ge(ms_ready, n + 1)
                pool.tensor_tensor(rstd[:, n, :], ss[:, n, 0:TILES], half[:, 0:1].to_broadcast([P, TILES]),
                                   ALU.pow).then_inc(rstd_ready, 1)

            def low_part(m):
                hi, lo = split_piece(m)
                pool.wait_ge(piece_hi, m + 1)
                pool.tensor_tensor(lo, raw_piece(SPLITS[m]), f32(hi), ALU.subtract).then_inc(piece_lo["p"], 1)

            def gates_times_x(h):
                pool.wait_ge(emptied["a"], emptied_by("a", WIDE[f"rg{h // 2}"] + 4 * (h % 2) + 4))
                pool.wait_ge(conv_done, h + 1)
                g = gibuf[h % 2]
                pool.tensor_tensor(g, g, xc[:, h, :].unsqueeze(1).to_broadcast([P, 2, NTOK]),
                                   ALU.mult).then_inc(gx_done, 1)

            def states_times_gr(h):
                pool.wait_ge(scan_done, h + 1)
                pool.wait_ge(emptied["a"], emptied_by("a", WIDE[f"gr{h // 2}"] + h % 2 + 1))
                link(pool.tensor_copy(ns[:, 0, h:h + 1], hs[:, 0, NCTX - 1:NCTX]))
                link(pool.tensor_copy(ns[:, 1, h:h + 1], hs[:, 1, 0:1]))
                link(pool.tensor_tensor(hs[:, 0, :], hs[:, 0, :], hs[:, 1, :], ALU.add))
                pool.tensor_tensor(grT[:, h, :], grT[:, h, :], hs[:, 0, :], ALU.mult).then_inc(yb_done, 1)

            power(0)
            for m in range(7):
                low_part(m)
            for g in range(4):
                if g >= 1:
                    states_times_gr(2 * g - 2)
                    states_times_gr(2 * g - 1)
                low_part(7 + 2 * g)
                gates_times_x(2 * g)
                gates_times_x(2 * g + 1)
            states_times_gr(KT - 2)
            states_times_gr(KT - 1)
            for m in range(16, 18):
                low_part(m)
            power(1)
            for m in range(18, len(SPLITS)):
                low_part(m)
            for n in (2, 3):
                for t in range(TILES):
                    pool.wait_ge(ms_ready, stats(n, t))
                    pool.tensor_tensor(rstd[:, n, t:t + 1], ss[:, n, t:t + 1], half[:, 0:1],
                                       ALU.pow).then_inc(rstd_ready, 1)

        @block.scalar
        def _(act):
            act.dma_start(col[:, :], cols).then_inc(col_in, 16)
            act.dma_start(wr[:, :, 0:NE], w_router.rearrange("p (k e) -> p k e", k=KT)).then_inc(wr_in, 16)
            act.wait_ge(col_in, 16)
            act.wait_ge(link_p, 1)
            act.activation(c32[:, :, 0:2], vcol("c", KT, 2), ACT.Silu).then_inc(c32_ready, 1)
            act.wait_ge(lam_one, 1)
            act.activation(lam[:, 1, :], lam[:, 0, :], ACT.Exp, scale=-1.0).then_inc(lam_exp, 1)
            act.wait_ge(lam_one, 2)
            act.activation(lam[:, 3, :], lam[:, 2, :], ACT.Ln).then_inc(lam_ln, 1)

            def take(n, out, src, func, **kw):
                act.wait_ge(wide_mm, n + 1)
                return act.activation(out, src, func, **kw).then_inc(emptied["a"], 1)

            def modulated(k, name, out, mod):
                n = WIDE[name] + k
                act.wait_ge(wide_mm, n + 1)
                for m, a, b in SETS:
                    ins = act.activation(out[:, k, a:b], bank[n % WIDE_BANKS][:, a:b], ACT.Identity,
                                         scale=mod[:, 0, k, m:m + 1], bias=mod[:, 1, k, m:m + 1])
                ins.then_inc(emptied["a"], 1)

            def high_part(m):
                act.wait_ge(*raw_loaded(SPLITS[m]))
                if m >= SPLIT:
                    act.wait_ge(*piece_mm(SPLITS[m - SPLIT]))
                act.activation(split_piece(m)[0], raw_piece(SPLITS[m]), ACT.Copy).then_inc(piece_hi, 1)

            def high(name, parts, src, k):
                act.activation(parts[0][:, k, :], src[:, k, :], ACT.Copy).then_inc(hi_ready[name], 1)

            for k in range(0, KT, 2):
                if k % 4 == 0:
                    act.wait_ge(mod_ready, 2 + k // 2)
                modulated(k + 1, "hT", hfull, mod1)
                act.wait_ge(emptied["v"], k // 2 + 1)
                high("hT", hT, hfull, k)
                act.wait_ge(emptied["a"], k // 2 + 1)
                high("hT", hT, hfull, k + 1)
                if k == 2:
                    high_part(0)
            high_part(1)
            act.wait_ge(wide_mm, WIDE["hT"] + KT)
            act.dma_start(wsp, w_spatial_t.rearrange("q (g p) -> q g p", g=KT)).then_inc(sp_in, 16)
            act.dma_start(bsp, b_spatial.to_broadcast([P, D]).rearrange("q (g p) -> q g p", g=KT)).then_inc(sp_in, 16)
            for n in range(4):
                act.dma_start(rgw[n], rg_w[:, n * D:(n + 1) * D]).then_inc(rg_in, 16)

            def take_two(q, out, at, func):
                for b in range(2):
                    n = groups_of(q) + b
                    take(n, out[:, at + b, :], bank[n % WIDE_BANKS][:, 0:NTOK], func)
                high_part(SPLIT_AT[q] + SPLIT)

            act.wait_ge(lo_ready["hT"], KT)
            for g in range(4):
                take_two(("chan", "in", 8 + g), xr, 2 * g, ACT.Copy)

            def root(h):
                act.wait_ge(om_ready, h + 1)
                t2 = rbuf[h % 2]
                act.activation(t2, t2, ACT.Sqrt, scale=-1.0, bias=tiny[:, 0:1]).then_inc(sqrt_done, 1)

            act.wait_ge(lam_ready, 1)
            for g in range(4):
                take_two(("chan", "in", 12 + g), grT, 2 * g, ACT.Gelu_apprx_tanh)
                take_two(("chan", "in", g), uT, 2 * g, ACT.Gelu_apprx_tanh)
                if g >= 1:
                    act.wait_ge(scan_done, 2 * g)
                for b in range(2 * g, 2 * g + 2):
                    for q in range(4):
                        n = WIDE[f"rg{g}"] + 4 * (b % 2) + q
                        d, buf, bias = q % 2, (rbuf, gibuf)[q // 2][b % 2], vcol(("rg_b_a", "rg_b_x")[q // 2], 2, KT)
                        take(n, buf[:, d, :], bank[n % WIDE_BANKS][:, 0:NTOK], ACT.Sigmoid, bias=bias[:, d, b:b + 1])
                act.wait_ge(emptied["a"], emptied_by("a", WIDE[f"rg{g}"] + 8))
                for b in range(2 * g, 2 * g + 2):
                    for d in range(2):
                        act.activation(ab[b % 2][:, d, :], rbuf[b % 2][:, d, :], ACT.Exp,
                                       scale=negsp[:, d, b:b + 1]).then_inc(exp_done, 1)
                act.wait_ge(exp_done, 4 * (g + 1))
                for b in range(2 * g, 2 * g + 2):
                    for d in range(2):
                        act.activation(rbuf[b % 2][:, d, :], rbuf[b % 2][:, d, :], ACT.Tanh,
                                       scale=negsp[:, d, b:b + 1]).then_inc(tanh_done, 1)
                root(2 * g)
                root(2 * g + 1)
            for hf in range(2):
                high_part(14 + 2 * hf)
                for t in range(TILES):
                    n = WIDE["v"] + TILES * hf + t
                    take(n, vtok[:, t, hf * UW:(hf + 1) * UW], bank[n % WIDE_BANKS][:, :], ACT.Gelu_apprx_tanh)
                high_part(15 + 2 * hf)
            act.wait_ge(gx_done, KT)
            for g in range(4):
                take_two(("chan", "in", 20 + g), glB, 2 * g, ACT.Sigmoid)
            for k in range(KT):
                act.wait_ge(ya_ready, k + 1)
                high("yaT", yaT, uT, k)
            act.wait_ge(yb_done, KT)
            act.dma_start(b_gate2, b_ada[:, 5 * D:6 * D]).then_inc(bg2_in, 16)
            for g in range(4):
                take_two(("chan", "in", 16 + g), glA, 2 * g, ACT.Sigmoid)
            act.dma_start(b_gate1, b_ada[:, 2 * D:3 * D]).then_inc(bg_in, 16)
            for k in range(KT):
                high("ybT", ybT, grT, k)
            first_b = SPLIT_AT["chan", "br_b", 0]
            for m in range(first_b - 2, first_b + SPLIT):
                high_part(m)
            for k in range(KT):
                act.wait_ge(merged_ready, k + 1)
                high("mT", mT, glA, k)
                if k % 2 == 1:
                    high_part(first_b + SPLIT + k // 2)
            for m in range(first_b + SPLIT + 4, len(SPLITS)):
                high_part(m)
            for q in range(N_MOD, len(ADA_ORDER)):
                act.wait_ge(ada_mm, q + 1)
                act.activation(modp(q), bank[6 + q % 2][:, :], ACT.Copy).then_inc(modp2_ready, 1)
            act.wait_ge(mod_ready, outs_before(8))
            act.wait_ge(ns_ready, 1)
            act.dma_start(new_state, ns_t[:, :]).then_inc(out_done, 16)
            for k in range(1, KT, 2):
                modulated(k, "h2T", h2T, mod2)
            act.wait_ge(sub_ready, 1)
            act.activation(exl, exl, ACT.Exp).then_inc(exp_ready, 1)
            for n in range(2):
                act.wait_ge(g2_mm, n + 1)
                rows = slice(64 * n, 64 * n + 64)
                act.activation(g2s[rows, :], bank[4 + n][rows, :], ACT.Copy).then_inc(g2_ready, 1)

            with act.Fori(0, PAIRS) as i:
                for p in range(2):
                    for j, (_, w) in enumerate(FCH):
                        act.wait_ge(gu_mm, i * (2 * NJ) + (NJ * p + j + 1))
                        act.activation(sgact[j % 2][0:64, 0:w], bank[j % 2][0:64, 0:w],
                                       ACT.Silu).then_inc(silu_done, 1)
            act.wait_ge(gather_mm, NE + 1)
            act.dma_start(gfin, final_norm_g.to_broadcast([P, D])).then_inc(gf_in, 16)
            for t in range(TILES):
                act.wait_ge(comb_added, PAIRS * 6 + LAST.index((t, 1)) + 2)
                if t >= 1:
                    act.wait_ge(sq_done, t)
                act.activation(squared_last, x[:, t, :], ACT.Square, accum_out=ss[:, 3, t:t + 1]).then_inc(sq_done, 1)

        @block.vector
        def _(dve):
            count = [0]

            def link(ins):
                count[0] += 1
                ins.then_inc(link_v, 1)
                dve.wait_ge(link_v, count[0])

            dve.memset(tiny[:, :], 1e-30)
            dve.wait_ge(col_in, 16)
            L = vcol("rg_lambda")
            link(dve.tensor_scalar(lam[:, 1, :], L, -1.0, None, ALU.mult))
            dve.tensor_tensor(lam[:, 0, :], L, lam[:, 1, :], ALU.max).then_inc(lam_one, 1)
            dve.wait_ge(lam_exp, 1)
            dve.tensor_scalar(lam[:, 2, :], lam[:, 1, :], 1.0, None, ALU.add).then_inc(lam_one, 1)
            dve.wait_ge(lam_ln, 1)
            link(dve.tensor_scalar(lam[:, 2, :], lam[:, 2, :], -1.0, None, ALU.add))
            link(dve.tensor_scalar(lam[:, 0, :], lam[:, 2, :], 0.0, None, ALU.is_equal))
            dve.tensor_tensor(lam[:, 2, :], lam[:, 2, :], lam[:, 0, :], ALU.add)
            link(dve.tensor_tensor(lam[:, 3, :], lam[:, 3, :], lam[:, 0, :], ALU.add))
            link(dve.reciprocal(lam[:, 2, :], lam[:, 2, :]))
            link(dve.tensor_tensor(lam[:, 3, :], lam[:, 3, :], lam[:, 2, :], ALU.mult))
            link(dve.tensor_tensor(lam[:, 3, :], lam[:, 3, :], lam[:, 1, :], ALU.mult))
            link(dve.tensor_scalar(lam[:, 2, :], L, -1.0, 0.0, ALU.mult, ALU.max))
            link(dve.tensor_tensor(lam[:, 3, :], lam[:, 3, :], lam[:, 2, :], ALU.add))
            dve.tensor_scalar(negsp[:, :, :].rearrange("p d k -> p (d k)"), lam[:, 3, :], -RG_C, None,
                              ALU.mult).then_inc(lam_ready, 1)

            dve.wait_ge(emb_in, 16)
            dve.wait_ge(x_in, 32)
            link(dve.tensor_tensor(x[:, 1:3, :], x[:, 1:3, :], embt, ALU.add))

            def mean_square(n):
                dve.tensor_scalar(ss[:, n, 0:TILES], ss[:, n, 0:TILES], 1.0 / D, EPS, ALU.mult,
                                  ALU.add).then_inc(ms_ready, 1)
                dve.wait_ge(rstd_ready, n + 1)

            def squares(n, t, src, squares_out):
                link(dve.tensor_tensor_reduce(out=squares_out, in0=src, in1=src, scale=1.0, scalar=0.0, op0=ALU.mult,
                                              op1=ALU.add, accum_out=ss[:, n, t:t + 1]))

            def normed(n, out, src, signal):
                for t in range(TILES):
                    dve.tensor_scalar(out[:, t, :], src[:, t, :], rstd[:, n, t:t + 1], None,
                                      ALU.mult).then_inc(signal, 1)

            def mean_tile(n, t):
                dve.tensor_scalar(ss[:, n, t:t + 1], ss[:, n, t:t + 1], 1.0 / D, EPS, ALU.mult,
                                  ALU.add).then_inc(ms_ready, 1)

            def normed_tile(n, t):
                dve.wait_ge(rstd_ready, stats(n, t))
                dve.tensor_scalar(xh[:, t, :], x[:, t, :], rstd[:, n, t:t + 1], None, ALU.mult).then_inc(xh_ready, 1)

            for t in range(TILES):
                squares(0, t, x[:, t, :], squared)
            mean_square(0)
            normed(0, xh, x, xh_ready)

            def ada(u):
                ada_rows(u)
                ada_result(u)

            def ada_rows(u):
                q = ADA_AT[u]
                dve.wait_ge(ada_mm, q + 1)
                if q >= 2:
                    dve.wait_ge(ada_out, outs_before(q - 1))
                dve.tensor_copy(modp(q), bank[6 + q % 2][:, :]).then_inc(modp_ready, 1)

            def ada_result(u):
                q, kind, hf = ADA_AT[u], u // 2, u % 2
                base = outs_before(q)
                if kind == 2:
                    for m in range(2):
                        dve.wait_ge(ada_out, base + m + 1)
                        dve.tensor_copy(g1b[:, m, hf * UW:(hf + 1) * UW], bank[5][:, :]).then_inc(mod_ready, 1)
                    return
                dve.wait_ge(ada_out, base + 1)
                ks = slice(4 * hf, 4 * hf + 4)
                rows = bank[5][:, :].rearrange("p (k j c) -> p k c j", k=4, j=4)[:, :, 0:2, :]
                got = mod_sum[:, :, :]
                link(dve.tensor_reduce(got, rows, AX.X, ALU.add))
                bias = vcol("b_ada", 6, KT)[:, kind, ks].unsqueeze(2).to_broadcast([P, 4, 2])
                mod, gain = (mod1, vcol("norm1_g")) if kind < 2 else (mod2, vcol("norm2_g"))
                if kind in (0, 3):
                    dve.tensor_tensor(mod[:, 1, ks, :], got, bias, ALU.add).then_inc(mod_ready, 1)
                else:
                    link(dve.tensor_tensor(mod_raw[:, :, :], got, bias, ALU.add))
                    dve.scalar_tensor_tensor(out=mod[:, 0, ks, :], in0=mod_raw[:, :, :], scalar=1.0,
                                             in1=gain[:, ks].unsqueeze(2).to_broadcast([P, 4, 2]), op0=ALU.add,
                                             op1=ALU.mult).then_inc(mod_ready, 1)

            def modulated(k, name, out, mod):
                n = WIDE[name] + k
                dve.wait_ge(wide_mm, n + 1)
                for m, a, b in SETS:
                    ins = dve.tensor_scalar(out[:, k, a:b], bank[n % WIDE_BANKS][:, a:b],
                                            mod[:, 0, k, m:m + 1], mod[:, 1, k, m:m + 1], ALU.mult, ALU.add)
                ins.then_inc(emptied["v"], 1)

            def low(name, parts, src, k):
                dve.wait_ge(hi_ready[name], k + 1)
                dve.tensor_tensor(parts[1][:, k, :], src[:, k, :], f32(parts[0][:, k, :]),
                                  ALU.subtract).then_inc(lo_ready[name], 1)

            for k in range(0, KT, 2):
                if k % 4 == 0:
                    ada(ADA_FIRST[k // 2])
                    ada(ADA_FIRST[k // 2 + 1])
                    dve.wait_ge(mod_ready, 2 + k // 2)
                modulated(k, "hT", hfull, mod1)
                if k >= 2:
                    low("hT", hT, hfull, k - 2)
                    low("hT", hT, hfull, k - 1)
            low("hT", hT, hfull, KT - 2)
            low("hT", hT, hfull, KT - 1)

            for h in range(KT):
                dve.wait_ge(emptied["a"], emptied_by("a", WIDE["xr"] + h + 1))
                link(dve.tensor_scalar(xc[:, h, :], xr[:, h, :], cw[:, 2, h:h + 1], cb[:, h:h + 1], ALU.mult, ALU.add))
                for k in (0, 1, 3):
                    s = k - 2
                    for _, a, b in SETS:
                        lo, hi = max(a, a - s), min(b, b - s)
                        ins = dve.scalar_tensor_tensor(out=xc[:, h, lo:hi], in0=xr[:, h, lo + s:hi + s],
                                                       scalar=cw[:, k, h:h + 1], in1=xc[:, h, lo:hi],
                                                       op0=ALU.mult, op1=ALU.add)
                        if k == 3 and a:
                            ins.then_inc(conv_done, 1)
                        elif a:
                            link(ins)

            def decay(h):
                a_, t2 = ab[h % 2], rbuf[h % 2]
                dve.wait_ge(tanh_done, 2 * h + 2)
                if h >= 1:
                    dve.wait_ge(om_ready, h)
                link(dve.tensor_tensor(asq, a_, a_, ALU.mult))
                dve.scalar_tensor_tensor(out=t2, in0=asq, scalar=1.0, in1=t2, op0=ALU.add, op1=ALU.mult)\
                    .then_inc(om_ready, 1)

            def scans(h):
                a_, o = ab[h % 2], rbuf[h % 2]
                dve.wait_ge(sqrt_done, h + 1)
                dve.wait_ge(gx_done, h + 1)
                link(dve.tensor_tensor(o, o, gibuf[h % 2], ALU.mult))
                if h >= 1:
                    dve.wait_ge(yb_done, h)
                for m, a, b in SETS:
                    start = [0.0, 0.0] if m == 0 else [st0[:, d, h:h + 1] for d in range(2)]
                    dve.tensor_tensor_scan(hs[:, 0, a:b], a_[:, 0, a:b], o[:, 0, a:b], start[0], ALU.mult, ALU.add)
                    ins = dve.tensor_tensor_scan(hs[:, 1, a:b][:, ::-1], a_[:, 1, a:b][:, ::-1],
                                                 o[:, 1, a:b][:, ::-1], start[1], ALU.mult, ALU.add)
                ins.then_inc(scan_done, 1)

            def low_part(m):
                hi, lo = split_piece(m)
                dve.wait_ge(piece_hi, m + 1)
                dve.tensor_tensor(lo, raw_piece(SPLITS[m]), f32(hi), ALU.subtract).then_inc(piece_lo["v"], 1)

            for h in range(0, KT, 2):
                decay(h)
                decay(h + 1)
                scans(h)
                low_part(8 + h)
                scans(h + 1)
            low_part(15)

            dve.wait_ge(emptied["a"], emptied_by("a", WIDE["v"] + 2 * TILES))
            for t in range(TILES):
                squares(1, t, vtok[:, t, :], squared)
            mean_square(1)
            normed(1, vtok, vtok, v_ready)
            dve.wait_ge(sp_in, 32)

            def three(ap):
                return ap.rearrange("p (t q) -> p t q", t=TILES)

            U = ADA_LATER
            ada_rows(U[0])
            ada_result(U[0])
            ada_rows(U[1])
            for g in range(KT):
                n = WIDE["spatial"] + g
                tmp = tmpc[:, g % 2, 0:NTOK]
                dve.wait_ge(wide_mm, n + 1)
                dve.scalar_tensor_tensor(out=three(tmp), in0=three(bank[n % WIDE_BANKS][:, 0:NTOK]),
                                         scalar=vcol("v_norm_g")[:, g:g + 1],
                                         in1=bsp[:, g, :].unsqueeze(1).to_broadcast([P, TILES, P]),
                                         op0=ALU.mult, op1=ALU.add).then_inc(emptied["v"], 1)
                dve.wait_ge(emptied["v"], emptied_by("v", n + 1))
                dve.wait_ge(emptied["a"], emptied_by("a", WIDE[f"u{g // 2}"] + g % 2 + 1))
                dve.tensor_tensor(uT[:, g, :], uT[:, g, :], tmp, ALU.mult).then_inc(ya_ready, 1)
            ada_result(U[1])
            for k in range(KT):
                low("yaT", yaT, uT, k)
            ada_rows(U[2])
            ada_result(U[2])
            ada_rows(U[3])

            def gated_a(b):
                n = WIDE["br_a"] + b
                dve.wait_ge(wide_mm, n + 1)
                dve.wait_ge(emptied["a"], emptied_by("a", WIDE["glA"] + b + 1))
                dve.tensor_tensor(glA[:, b, :], glA[:, b, :], bank[n % WIDE_BANKS][:, 0:NTOK],
                                  ALU.mult).then_inc(emptied["v"], 1)

            def gated_b(b):
                n = WIDE["br_b"] + b
                tmp = tmpc[:, b % 2, 0:NTOK]
                dve.wait_ge(wide_mm, n + 1)
                dve.wait_ge(emptied["a"], emptied_by("a", WIDE["glB"] + b + 1))
                dve.tensor_tensor(tmp, glB[:, b, :], bank[n % WIDE_BANKS][:, 0:NTOK],
                                  ALU.mult).then_inc(emptied["v"], 1)
                dve.wait_ge(emptied["v"], emptied_by("v", n + 1))
                dve.tensor_tensor(glA[:, b, :], glA[:, b, :], tmp, ALU.add).then_inc(merged_ready, 1)
                if b >= 1:
                    low("mT", mT, glA, b - 1)

            gated_a(0)
            gated_a(1)
            ada_result(U[3])
            gated_a(2)
            gated_a(3)
            for k in range(KT):
                low("ybT", ybT, grT, k)
            for b in range(4, KT):
                gated_a(b)
            ada_rows(U[4])
            gated_b(0)
            gated_b(1)
            ada_result(U[4])
            gated_b(2)
            gated_b(3)
            ada_rows(U[5])
            gated_b(4)
            gated_b(5)
            ada_result(U[5])
            gated_b(6)
            gated_b(7)
            low("mT", mT, glA, KT - 1)
            dve.wait_ge(mod_ready, outs_before(N_MOD))

            for g in range(2 * TILES):
                n, t, hf = WIDE["out"] + g, g % TILES, g // TILES
                hs_ = slice(hf * UW, (hf + 1) * UW)
                dve.wait_ge(wide_mm, n + 1)
                dve.tensor_tensor(tmpo[:, g % 2, :], g1b[:, min(t, 1), hs_], bank[n % WIDE_BANKS][:, :],
                                  ALU.mult).then_inc(emptied["v"], 1)
                dve.wait_ge(emptied["v"], emptied_by("v", n + 1))
                dve.tensor_tensor(x[:, t, hs_], x[:, t, hs_], tmpo[:, g % 2, :], ALU.add).then_inc(x1_ready, 1)
                dve.wait_ge(x1_ready, g + 1)
                link(dve.tensor_tensor_reduce(out=squared_half, in0=x[:, t, hs_], in1=x[:, t, hs_], scale=1.0, scalar=0.0,
                                              op0=ALU.mult, op1=ALU.add, accum_out=ss[:, 2, g:g + 1]))
                if g == TILES - 1:
                    dve.wait_ge(ns_mm, 1)
                    dve.tensor_copy(ns_t[:, :], bank[5][0:2 * KT, 0:P]).then_inc(ns_ready, 1)
                if hf == 1:
                    if t >= 1:
                        normed_tile(2, t - 1)
                    link(dve.tensor_tensor(ss[:, 2, t:t + 1], ss[:, 2, t:t + 1], ss[:, 2, TILES + t:TILES + t + 1],
                                           ALU.add))
                    mean_tile(2, t)
            normed_tile(2, TILES - 1)
            for k in range(0, KT, 2):
                modulated(k, "h2T", h2T, mod2)

            dve.wait_ge(lg_mm, 1)
            dve.tensor_copy(lgT, bank[0][:, 0:NTOK]).then_inc(lg_ready, 1)
            dve.wait_ge(lg_tok, 1)
            lg = bank[1][:, 0:TILES * NE].rearrange("p (t e) -> p t e", t=TILES)
            link(dve.tensor_reduce(smax[:, 0, :], lg, AX.X, ALU.max))
            dve.tensor_tensor(exl, lg, smax[:, 0, :].unsqueeze(2).to_broadcast([P, TILES, NE]),
                              ALU.subtract).then_inc(sub_ready, 1)
            dve.wait_ge(exp_ready, 1)
            link(dve.tensor_reduce(smax[:, 1, :], exl, AX.X, ALU.add))
            link(dve.reciprocal(smax[:, 2, :], smax[:, 1, :]))
            dve.tensor_tensor(aff[:, :, :], exl, smax[:, 2, :].unsqueeze(2).to_broadcast([P, TILES, NE]),
                              ALU.mult).then_inc(aff_ready, 1)
            dve.memset(onesT, 1.0)
            dve.wait_ge(aff_mm, 1)
            link(dve.tensor_copy(affT, bank[2][0:NE, 0:NTOK]))
            r = 0
            for (_, a, b), cap in zip(SETS, (CAP_CTX, CAP_LAT)):
                for _ in range(cap // 8):
                    link(dve.max(top8[:, r, :], affT[:, a:b]))
                    link(dve.match_replace(out=affT[:, a:b], in_to_replace=top8[:, r, :], in_values=affT[:, a:b],
                                           imm_value=-1.0))
                    r += 1
            link(dve.tensor_scalar(maskT, affT, -1.0, None, ALU.is_equal))
            for _, a, b in SETS:
                last = dve.tensor_tensor_scan(posT[:, a:b], onesT[:, a:b], maskT[:, a:b], 0.0, ALU.mult, ALU.add)
            link(last)
            dve.tensor_tensor(posT, posT, maskT, ALU.mult).then_inc(pos_ready, 1)
            dve.wait_ge(pos_mm, 1)
            link(dve.tensor_copy(posm[:, :, 0:NE], bank[1][:, 0:TILES * NE].rearrange("p (t e) -> p t e", t=TILES)))

            def choose(e, par):
                dve.tensor_tensor(S[par], iota[:, :].unsqueeze(1).to_broadcast([P, TILES, SL]),
                                  posm[:, :, bass.ds(e, 1)].to_broadcast([P, TILES, SL]),
                                  ALU.is_equal).then_inc(s_ready, 1)

            def gathered():
                dve.tensor_copy(xg, bank[6][:, :]).then_inc(xg_ready, 1)

            def modulate(par, n):
                for m, rows in ((1, slice(0, SL)), (0, slice(SL, 2 * SL))):
                    got = bank[7][:, :].rearrange("p (b h s) -> p h b s", b=4, h=2)[:, :, :, rows]
                    out = xgT[par].rearrange("p (h b) s -> p h b s", h=2)[:, :, :, rows]
                    for hf in range(2):
                        ks = slice(4 * hf, 4 * hf + 4)
                        last = dve.tensor_tensor(out[:, hf], got[:, hf],
                                                 mod2[:, 0, ks, m:m + 1].to_broadcast([P, 4, SL]), ALU.mult)
                last.then_inc(xgt_scaled, 1)
                dve.wait_ge(xgt_scaled, n)
                for m, rows in ((1, slice(0, SL)), (0, slice(SL, 2 * SL))):
                    last = dve.tensor_tensor(xgT[par][:, :, rows], xgT[par][:, :, rows],
                                             mod2[:, 1, :, m:m + 1].to_broadcast([P, KT, SL]), ALU.add)
                last.then_inc(xgt_ready, 1)

            def add_combined(t, hf, from_, n):
                dve.wait_ge(comb_mm, n + 1)
                hs_ = slice(hf * UW, (hf + 1) * UW)
                dve.tensor_tensor(x[:, t, hs_], x[:, t, hs_], from_[:, :], ALU.add).then_inc(comb_added, 1)

            def copy_act_t(n, j):
                dve.wait_ge(actt_mm, n + 3)
                dve.wait_ge(down_mm, n + 1)
                tiles = FCH[j][1] // P
                got = bank[2 + j % 2][:, 0:P * tiles].rearrange("p (f h s) -> p f h s", f=tiles, h=2)
                dve.tensor_copy(actT[j % 2][:, 0:tiles, :], got[:, :, 1, :]).then_inc(actt_ready, 1)

            choose(0, 0)
            for n, (freed, uses) in enumerate(((act_done, 2), (actt_mm, 2), (actt_ready, 2), (down_mm, 2),
                                               (gt_mm, 1), (comb_added, 1))):
                dve.memset(lam[:, 0, n:n + 1], 0.0).then_inc(freed, uses)
            dve.wait_ge(gather_mm, 1)
            gathered()
            dve.wait_ge(xgt_mm, 1)
            modulate(0, 1)
            dve.memset(o_pair, 0.0).then_inc(o_ready, 2)
            dve.memset(GT, 0.0).then_inc(gt_ready, 1)
            dve.wait_ge(g2_ready, 2)

            with dve.Fori(0, PAIRS) as i:
                for p in range(2):
                    e = i * 2 + p
                    for j, (_, w) in enumerate(FCH):
                        n = i * (2 * NJ) + (NJ * p + j)
                        if j >= 1:
                            copy_act_t(n - 1, j - 1)
                        dve.wait_ge(silu_done, n + 1)
                        dve.wait_ge(actt_mm, n + 1)
                        dve.tensor_tensor(sgact[j % 2][64:128, 0:w], sgact[j % 2][0:64, 0:w],
                                          bank[j % 2][64:128, 0:w], ALU.mult).then_inc(act_done, 1)
                        if j == 0:
                            dve.wait_ge(s_ready, e + 1)
                            dve.wait_ge(gt_mm, i + 1)
                            dve.tensor_tensor(G[:, 0:3:2, p, :], S[p][:, 1:3, :],
                                              aff[:, 1:3, bass.ds(e, 1)].to_broadcast([P, 2, SL]), ALU.mult)
                            dve.tensor_tensor(G[:, 1, p, :].unsqueeze(1), S[p][:, 0:1, :],
                                              aff[:, 0:1, bass.ds(e, 1)].to_broadcast([P, 1, SL]),
                                              ALU.mult).then_inc(g_ready, 1)
                            dve.wait_ge(gather_mm, e + 1)
                            choose(e + 1, 1 - p)
                        if j == 2:
                            dve.wait_ge(gather_mm, e + 2)
                            gathered()
                        if j == 3:
                            dve.wait_ge(xgt_mm, e + 2)
                            modulate(1 - p, e + 2)
                        if p == 0 and j >= 4:
                            for c in range(2 * (j - 4), 2 * (j - 4) + 2):
                                add_combined(c // 2, c % 2, comb_bank(c), i * 6 + c)
                        if p == 1 and j == 4:
                            dve.wait_ge(gt_mm, i + 2)
                            dve.tensor_copy(GT[64:128, 0, :], bank[6][64:128, 0:P])
                            dve.tensor_copy(GT[0:64, 1, :], bank[6][0:64, 0:P])
                            dve.tensor_copy(GT[0:64, 2, :], bank[6][0:64, P:2 * P]).then_inc(gt_ready, 1)
                    if p == 0:
                        for c in (4, 5):
                            add_combined(c // 2, c % 2, comb_bank(c), i * 6 + c)
                    copy_act_t(i * (2 * NJ) + (NJ * p + NJ - 1), NJ - 1)
                    dve.wait_ge(down_mm, i * (2 * NJ) + (NJ * (p + 1) + 2))
                    for q, row in enumerate((32 * p, 64 + 32 * p, 32 * p, 64 + 32 * p)):
                        src, hf = slice(32 * q, 32 * q + 32), q // 2
                        last = dve.tensor_tensor(o_pair[row:row + 32, hf * UW:(hf + 1) * UW], bank[4 + p][src, :],
                                                 g2s[src, :], ALU.mult)
                        if q == 1:
                            last.then_inc(o_half, 1)
                    last.then_inc(o_ready, 1)

            def final_mean(t):
                dve.wait_ge(sq_done, t + 1)
                mean_tile(3, t)

            def final_scale(t):
                dve.wait_ge(rstd_ready, stats(3, t))
                dve.scalar_tensor_tensor(out=x[:, t, :], in0=x[:, t, :], scalar=rstd[:, 3, t:t + 1], in1=gfin,
                                         op0=ALU.mult, op1=ALU.mult).then_inc(y_ready, 1)

            dve.wait_ge(gf_in, 16)
            for c, (t, hf) in enumerate(LAST):
                add_combined(t, hf, bank[LAST_BANKS[c]], PAIRS * 6 + c)
                if c in (3, 4):
                    final_mean(c - 3)
            final_scale(0)
            final_mean(TILES - 1)
            final_scale(1)
            final_scale(2)

        @block.tensor
        def _(pe):
            def wide(n):
                if n >= WIDE_BANKS:
                    e = _EVAC[n - WIDE_BANKS]
                    pe.wait_ge(emptied[e], emptied_by(e, n - WIDE_BANKS + 1))
                return bank[n % WIDE_BANKS]

            def all_emptied(n):
                for e in "va":
                    pe.wait_ge(emptied[e], emptied_by(e, n))

            def keep_clock(products):
                for _ in range(products):
                    pe.matmul(bank[3][:, 0:2 * P], ident[:, :], selb[:, :, :].rearrange("p m c -> p (m c)"),
                              start=True, stop=True)

            def transposed(name, first=0, end=KT):
                for k in range(first, end):
                    to = wide(WIDE[name] + k)
                    for t in range(TILES):
                        ins = pe.transpose(to[:, t * P:(t + 1) * P], xh[:, t, k * P:(k + 1) * P], ident[:, :])
                    ins.then_inc(wide_mm, 1)

            PASSES = ((0, 0), (0, 1), (1, 0))

            def first_piece():
                m = SPLIT_AT["chan", "in", 8]
                w = split_piece(m)
                pe.wait_ge(piece_hi, m + 1)
                for x_, y_ in PASSES:
                    if x_:
                        pe.wait_ge(*split_done(m))
                    for b in range(2):
                        to = wide(WIDE["xr"] + b) if (x_, y_) == PASSES[0] else bank[(WIDE["xr"] + b) % WIDE_BANKS]
                        for k in range(KT):
                            if not x_ and not b:
                                pe.wait_ge((lo_ready if y_ else hi_ready)["hT"], k + 1)
                            ins = pe.matmul(to[:, 0:NTOK], w[x_][:, k, b * P:(b + 1) * P], hT[y_][:, k, :],
                                            start=(k == 0 and (x_, y_) == PASSES[0]),
                                            stop=(k == KT - 1 and (x_, y_) == PASSES[-1]))
                        if x_:
                            ins.then_inc(wide_mm, 1)

            def channel_major(kind, g, src):
                q = ("chan", kind, g)
                w = split_piece(SPLIT_AT[q])
                pe.wait_ge(*split_done(SPLIT_AT[q]))
                for b in range(2):
                    n = groups_of(q) + b
                    to = wide(n)
                    for k in range(KT):
                        for x_, y_ in PASSES:
                            ins = pe.matmul(to[:, 0:NTOK], w[x_][:, k, b * P:(b + 1) * P], src[y_][:, k, :],
                                            start=(k == 0 and (x_, y_) == (0, 0)),
                                            stop=(k == KT - 1 and (x_, y_) == (1, 0)))
                    ins.then_inc(wide_mm, 1)

            def token_major(kind, u, kh, src):
                q = ("tok", kind, u, kh)
                w = split_piece(SPLIT_AT[q])
                pe.wait_ge(*split_done(SPLIT_AT[q]))
                for t in range(TILES):
                    n = groups_of(q) + t
                    to = wide(n) if kh == 0 else bank[n % WIDE_BANKS]
                    for k in range(4):
                        for x_, y_ in PASSES:
                            ins = pe.matmul(to[:, :], src[y_][:, 4 * kh + k, t * P:(t + 1) * P], w[x_][:, k, :],
                                            start=(kh == 0 and k == 0 and (x_, y_) == (0, 0)),
                                            stop=(kh == 1 and k == 3 and (x_, y_) == (1, 0)))
                    if kh:
                        ins.then_inc(wide_mm, 1)
                if not kh:
                    ins.then_inc(half_mm, 1)

            def ada_rows(u):
                q, gate = ADA_AT[u], u // 2 in (2, 5)
                if q >= 2:
                    pe.wait_ge(modp_ready, q - 1)
                to = bank[6 + q % 2]
                for h in range(2):
                    n = PIECE_AT["ada", u, h]
                    w = raw_piece(n)
                    pe.wait_ge(*raw_loaded(n))
                    cols_ = slice(h * PW, (h + 1) * PW)
                    for k in range(KT):
                        j = k % 4
                        ins = pe.matmul(to[32 * j:32 * j + 32, cols_], c32[:, k, :], w[:, k, :], start=(k < 4),
                                        stop=(k >= 4 and not (gate and j == 0)))
                    if gate:
                        at = (u % 2) * UW + h * PW
                        bias = (b_gate1 if u // 2 == 2 else b_gate2)[:, at:at + PW]
                        ins = pe.matmul(to[0:32, cols_], two_ones[:, :], bias, start=False, stop=True)
                    ins.then_inc(ada_mm if h else ada_half, 1)

            def ada_sums(u):
                q, kind = ADA_AT[u], u // 2
                pe.wait_ge(modp_ready, q + 1)
                rows = modp(q)
                if kind == 2:
                    for m in range(2):
                        pe.wait_ge(mod_ready, outs_before(q) + m)
                        pe.matmul(bank[5][:, :], selb[:, m, :], rows, start=True, stop=True).then_inc(ada_out, 1)
                    return
                pe.wait_ge(mod_ready, outs_before(q))
                for b in range(4):
                    ins = pe.transpose(bank[5][:, b * P:(b + 1) * P], rows[:, b * P:(b + 1) * P], ident[:, :])
                ins.then_inc(ada_out, 1)

            pe.wait_ge(consts, 1)
            pe.wait_ge(c32_ready, 1)
            A = ADA_FIRST
            ada_rows(A[0])
            ada_rows(A[1])
            ada_sums(A[0])
            pe.wait_ge(xh_ready, TILES)
            transposed("hT", 0, WIDE_BANKS)
            ada_sums(A[1])
            ada_rows(A[2])
            transposed("hT", WIDE_BANKS)
            ada_sums(A[2])
            ada_rows(A[3])
            ada_sums(A[3])
            first_piece()
            for g in range(1, 4):
                channel_major("in", 8 + g, hT)
            pe.wait_ge(rg_in, 64)
            for g in range(4):
                channel_major("in", 12 + g, hT)
                channel_major("in", g, hT)
                for b in range(2 * g, 2 * g + 2):
                    pe.wait_ge(conv_done, b + 1)
                    for q in range(4):
                        n = WIDE[f"rg{g}"] + 4 * (b % 2) + q
                        to = wide(n)
                        pe.matmul(to[:, 0:NTOK], rgw[q][:, b * P:(b + 1) * P], xc[:, b, :], start=True,
                                  stop=True).then_inc(wide_mm, 1)
            for hf in range(2):
                for kh in range(2):
                    token_major("in", 2 + hf, kh, hT)
            U = ADA_LATER
            channel_major("in", 20, hT)
            channel_major("in", 21, hT)
            ada_rows(U[0])
            channel_major("in", 22, hT)
            ada_sums(U[0])
            channel_major("in", 23, hT)
            ada_rows(U[1])
            pe.wait_ge(v_ready, TILES)
            pe.wait_ge(sp_in, 32)
            for g in range(KT):
                n = WIDE["spatial"] + g
                to = wide(n)
                for t in range(TILES):
                    ins = pe.matmul(to[:, t * P:(t + 1) * P], vtok[:, t, g * P:(g + 1) * P], wsp[:, g, :],
                                    start=True, stop=True)
                ins.then_inc(wide_mm, 1)
            ada_sums(U[1])
            channel_major("in", 16, hT)
            channel_major("in", 17, hT)
            ada_rows(U[2])
            channel_major("in", 18, hT)
            ada_sums(U[2])
            channel_major("in", 19, hT)
            ada_rows(U[3])
            pe.wait_ge(lo_ready["yaT"], KT)
            channel_major("br_a", 0, yaT)
            ada_sums(U[3])
            channel_major("br_a", 1, yaT)
            channel_major("br_a", 2, yaT)
            channel_major("br_a", 3, yaT)
            pe.wait_ge(bg_in, 16)
            ada_rows(U[4])
            pe.wait_ge(lo_ready["ybT"], KT)
            channel_major("br_b", 0, ybT)
            ada_sums(U[4])
            channel_major("br_b", 1, ybT)
            ada_rows(U[5])
            channel_major("br_b", 2, ybT)
            ada_sums(U[5])
            channel_major("br_b", 3, ybT)
            pe.wait_ge(lo_ready["mT"], 4)
            token_major("out", 0, 0, mT)
            pe.wait_ge(lo_ready["mT"], KT)
            token_major("out", 0, 1, mT)
            pe.wait_ge(mod_ready, outs_before(N_MOD))
            pe.transpose(bank[5][0:2 * KT, 0:P], ns[:, :, :].rearrange("p d k -> p (d k)"), ident[:, :])\
                .then_inc(ns_mm, 1)
            token_major("out", 1, 0, mT)
            token_major("out", 1, 1, mT)
            pe.wait_ge(bg2_in, 16)
            for u in ADA_GATE2:
                ada_rows(u)
            pe.wait_ge(xh_ready, 2 * TILES)
            transposed("h2T")
            pe.wait_ge(wr_in, 16)
            all_emptied(WIDE["h2T"] + KT)
            for k in range(KT):
                j = k % 4
                ins = pe.matmul(bank[0][32 * j:32 * j + 32, 0:NTOK], wr[:, k, :], h2T[:, k, :], start=(k < 4),
                                stop=(k >= 4))
            ins.then_inc(lg_mm, 1)
            pe.wait_ge(lg_ready, 1)
            for t in range(TILES):
                ins = pe.matmul(bank[1][:, t * NE:(t + 1) * NE], lgT[:, t * P:(t + 1) * P], sel4[:, :], start=True,
                                stop=True)
            ins.then_inc(lg_tok, 1)
            pe.wait_ge(aff_ready, 1)
            for t in range(TILES):
                ins = pe.transpose(bank[2][0:NE, t * P:(t + 1) * P], aff[:, t, :], ident[:, :])
            ins.then_inc(aff_mm, 1)
            pe.wait_ge(ns_ready, 1)
            for n in range(2):
                pe.wait_ge(modp2_ready, n + 1)
                pe.matmul(bank[4 + n][:, :], selg[:, :], modp(N_MOD + n), start=True, stop=True).then_inc(g2_mm, 1)
            keep_clock(9)
            pe.wait_ge(pos_ready, 1)
            for t in range(TILES):
                ins = pe.transpose(bank[1][:, t * NE:(t + 1) * NE], posT[:, t * P:(t + 1) * P], ident[0:NE, 0:NE])
            ins.then_inc(pos_mm, 1)

            def gather(par):
                for t in (1, 0, 2):
                    for hf in range(2):
                        at = 64 * hf + (SL if t == 0 else 0)
                        ins = pe.matmul(bank[6][at:at + SL, :], S[par][:, t, :], xh[:, t, hf * UW:(hf + 1) * UW],
                                        start=(t != 2), stop=(t != 1))
                ins.then_inc(gather_mm, 1)

            def gathered_t():
                for b in range(4):
                    ins = pe.transpose(bank[7][:, b * P:(b + 1) * P], xg[:, b * P:(b + 1) * P], ident[:, :])
                ins.then_inc(xgt_mm, 1)

            def combine(c):
                combine_half(c // 2, c % 2, comb_bank(c))

            def combine_half(t, hf, to):
                pe.matmul(to[:, :], GT[:, t, :], o_pair[:, hf * UW:(hf + 1) * UW], start=True,
                          stop=True).then_inc(comb_mm, 1)

            def gate_up(i, p, j):
                n = i * (2 * NJ) + (NJ * p + j)
                w = FCH[j][1]
                slots = []
                for kind in ("gate", "up"):
                    s, loads = expert_loads(i, PAIR_AT[p, kind, j])
                    pe.wait_ge(slot_in[s], loads)
                    slots.append(by_rows(s, w))
                if j == 0:
                    pe.wait_ge(xgt_ready, i * 2 + (p + 1))
                pe.wait_ge(act_done, n + 1)
                for k in range(KT):
                    for q in range(2):
                        ins = pe.matmul(bank[j % 2][64 * q:64 * q + 64, 0:w], xgT[p][:, k, :], slots[q][:, k, :],
                                        start=(k == 0), stop=(k == KT - 1))
                ins.then_inc(gu_mm, 1)

            def act_t(i, p, j):
                n = i * (2 * NJ) + (NJ * p + j)
                pe.wait_ge(act_done, n + 3)
                pe.wait_ge(actt_ready, n + 1)
                for f in range(FCH[j][1] // P):
                    ins = pe.transpose(bank[2 + j % 2][:, f * P:(f + 1) * P],
                                       sgact[j % 2][:, f * P:(f + 1) * P], ident[:, :])
                ins.then_inc(actt_mm, 1)

            def down(i, p, j):
                n = i * (2 * NJ) + (NJ * p + j)
                s, loads = expert_loads(i, PAIR_AT[p, "down", j])
                tiles = FCH[j][1] // P
                w = by_ff(s, tiles)
                pe.wait_ge(slot_in[s], loads)
                pe.wait_ge(actt_ready, n + 3)
                if j == 0:
                    pe.wait_ge(o_ready, i * 2 + (p + 1))
                for f in range(tiles):
                    for q in range(2):
                        ins = pe.matmul(bank[4 + p][64 * q:64 * q + 64, :], actT[j % 2][:, f, :],
                                        w[:, f, q * UW:(q + 1) * UW], start=(j == 0 and f == 0),
                                        stop=(j == NJ - 1 and f == tiles - 1))
                ins.then_inc(down_mm, 1)

            pe.wait_ge(s_ready, 1)
            pe.wait_ge(modp2_ready, 2)
            pe.wait_ge(g2_ready, 2)
            gather(0)
            pe.wait_ge(xg_ready, 1)
            gathered_t()
            keep_clock(4)
            with pe.Fori(0, PAIRS) as i:
                for p in range(2):
                    e = i * 2 + p
                    for j in range(NJ):
                        gate_up(i, p, j)
                        if j >= 1:
                            act_t(i, p, j - 1)
                        if j == 1:
                            pe.wait_ge(s_ready, e + 2)
                            pe.wait_ge(xg_ready, e + 1)
                            pe.wait_ge(comb_added, i * 6 + (6 * p + 1))
                            pe.wait_ge(gt_ready, i + 1)
                            gather(1 - p)
                        if j == 2:
                            pe.wait_ge(xg_ready, e + 2)
                            pe.wait_ge(xgt_ready, e + 1)
                            gathered_t()
                        if p == 0 and j >= 3:
                            for c in range(2 * (j - 3), 2 * (j - 3) + 2):
                                if c == 0:
                                    pe.wait_ge(gt_ready, i + 1)
                                    pe.wait_ge(o_ready, e + 2)
                                    pe.wait_ge(xgt_ready, e + 2)
                                if c >= 2:
                                    pe.wait_ge(comb_added, i * 6 + c)
                                combine(c)
                        if p == 1 and j == 3:
                            pe.wait_ge(g_ready, i * 2 + 2)
                            pe.transpose(bank[6][:, 0:P], G[:, 0:2, :, :].rearrange("p b e s -> p (b e s)"), ident[:, :])
                            pe.transpose(bank[6][0:64, P:2 * P], G[:, 2, :, :].rearrange("p e s -> p (e s)"),
                                         ident[:, :]).then_inc(gt_mm, 1)
                        if j >= 1:
                            down(i, p, j - 1)
                    act_t(i, p, NJ - 1)
                    down(i, p, NJ - 1)
            pe.wait_ge(gt_ready, PAIRS + 1)
            pe.wait_ge(xgt_ready, NE + 1)
            for c, (t, hf) in enumerate(LAST):
                pe.wait_ge(*((o_ready, NE + 2) if hf else (o_half, NE)))
                combine_half(t, hf, bank[LAST_BANKS[c]])


def position_table():
    import numpy as np

    rr, cc = np.meshgrid(np.arange(NLAT // GRID_W, dtype=np.float32), np.arange(GRID_W, dtype=np.float32), indexing="ij")
    quarter = D // 4
    omega = (1.0 / (10000.0 ** (np.arange(quarter, dtype=np.float32) / np.float32(quarter)))).astype(np.float32)
    r, c = rr.reshape(-1)[:, None] * omega, cc.reshape(-1)[:, None] * omega
    return np.ascontiguousarray(np.concatenate([np.sin(r), np.cos(r), np.sin(c), np.cos(c)], axis=-1), np.float32)


def kernel(x_prompt, x_sample, state_rglru, c, c_ctx, w_ada, b_ada, norm1_g, norm2_g, w_in, v_norm_g,
           w_spatial, b_spatial, conv_w, conv_b, rg_w_a, rg_b_a, rg_w_x, rg_b_x, rg_lambda,
           w_br_a, w_br_b, w_out, w_router, w_gate_e, w_up_e, w_down_e, final_norm_g):
    import concourse.bacc as bacc
    import numpy as np
    from concourse.bass_utils import run_bass_kernel_spmd

    def columns(a):
        return np.asarray(a).reshape(-1, P).T

    conditions = np.stack([np.asarray(c_ctx).reshape(KT, P), np.asarray(c).reshape(KT, P)], axis=1)
    cols = np.concatenate([columns(conditions)] + [columns(a) for a in (
        norm1_g, norm2_g, b_ada, v_norm_g, conv_w, conv_b, rg_b_a, rg_b_x, rg_lambda, state_rglru)], axis=1)
    arrays = {
        "x_prompt": np.asarray(x_prompt)[0], "x_sample": np.asarray(x_sample)[0], "emb": position_table(),
        "cols": cols, "w_ada": np.asarray(w_ada)[0], "b_ada": np.asarray(b_ada), "w_in": np.asarray(w_in)[0],
        "w_spatial_t": np.asarray(w_spatial)[0].transpose(2, 0, 1).reshape(P, D),
        "b_spatial": np.asarray(b_spatial).reshape(1, D),
        "rg_w": np.stack([np.asarray(rg_w_a)[0], np.asarray(rg_w_x)[0]]).transpose(3, 0, 1, 2, 4).reshape(P, -1),
        "w_br_a": np.asarray(w_br_a)[0], "w_br_b": np.asarray(w_br_b)[0], "w_out": np.asarray(w_out)[0],
        "w_router": np.asarray(w_router)[0].reshape(KT, P, NE).transpose(1, 0, 2).reshape(P, KT * NE),
        "w_gate": np.asarray(w_gate_e)[0], "w_up": np.asarray(w_up_e)[0], "w_down": np.asarray(w_down_e)[0],
        "final_norm_g": np.asarray(final_norm_g).reshape(1, D),
    }
    arrays = {k: np.ascontiguousarray(v) for k, v in arrays.items()}
    outs = {"y_prompt": (NCTX, D), "y_sample": (NLAT, D), "new_state": (2 * KT, P)}

    nc = bacc.Bacc("TRN2", target_bir_lowering=False, num_devices=1)
    args = {k: nc.dram_tensor(f"in_{k}", v.shape, mybir.dt.from_np(v.dtype), kind="ExternalInput").ap()
            for k, v in arrays.items()}
    args |= {k: nc.dram_tensor(f"out_{k}", shape, mybir.dt.float32, kind="ExternalOutput").ap()
             for k, shape in outs.items()}
    build(nc, **args)
    r = run_bass_kernel_spmd(nc, [{f"in_{k}": v for k, v in arrays.items()}], core_ids=[0]).results[0]
    return (r["out_y_prompt"].reshape(x_prompt.shape), r["out_y_sample"].reshape(x_sample.shape),
            r["out_new_state"].reshape(x_prompt.shape[0], 1, 2, D))
```
